# Optimizing a Trainium2 kernel written in Bass

```python
import jax, jax.numpy as jnp
from jax import lax
import numpy as np

D_MODEL = 1024
BATCH = 1
SEQ = 512
DEPTH = 2

GRID_W = 64
CTX_LEN = 256

NA_HEADS = 6
NA_DIM = 64
NA_WIN_ROWS = 8
NA_WIN_COLS = 16
MLA_HEADS = 4
MLA_Q_RANK = 256
MLA_KV_RANK = 128
MLA_NOPE = 128
MLA_ROPE = 64
MLA_V = 128
MLA_BLOCK = 128
SWA_HEADS = 6
SWA_KV_HEADS = 2
SWA_DIM = 64
SWA_WINDOW = 128
SWA_BLOCK = 128
N_EXPERTS = 16
EXPERT_FF = 1024
CAPACITY_FACTOR = 2

N_BRANCH = 3
ROPE_BASE = 10000.0
EPS = 1e-6

NA_W = NA_HEADS * NA_DIM
MLA_QK = MLA_NOPE + MLA_ROPE
MLA_W = MLA_HEADS * MLA_V
SWA_W = SWA_HEADS * SWA_DIM
SWA_KV_W = SWA_KV_HEADS * SWA_DIM
IN_SPLITS = (NA_W, NA_W, NA_W, MLA_Q_RANK, MLA_KV_RANK, MLA_ROPE, SWA_W, SWA_KV_W, SWA_KV_W, N_BRANCH * D_MODEL)
D_IN = sum(IN_SPLITS)

kernel_name = 'hybrid_na_mla_swa_ecmoe_dit'

def _rmsnorm(x, g):
    xf = x.astype(jnp.float32)
    y = xf * lax.rsqrt(jnp.mean(xf * xf, axis=-1, keepdims=True) + EPS)
    return (y * g.astype(jnp.float32)).astype(x.dtype)

def _heads(t, n):
    B, T, _ = t.shape
    return t.reshape(B, T, n, -1).transpose(0, 2, 1, 3)

def _merge_heads(t):
    B, n, T, d = t.shape
    return t.transpose(0, 2, 1, 3).reshape(B, T, n * d)

def _softmax32(s):
    return jax.nn.softmax(s.astype(jnp.float32), axis=-1)

def _rotate(x, ang):
    f = ang.shape[-1]
    x1, x2 = x[..., :f], x[..., f:]
    cos, sin = jnp.cos(ang), jnp.sin(ang)
    return jnp.concatenate([x1 * cos - x2 * sin, x2 * cos + x1 * sin], axis=-1)

def _axial_rope(x, row, col):
    half = x.shape[-1] // 2
    f = half // 2
    inv = ROPE_BASE ** (-jnp.arange(f, dtype=jnp.float32) / f)
    ar = row.astype(jnp.float32)[:, None] * inv
    ac = col.astype(jnp.float32)[:, None] * inv
    out = jnp.concatenate([_rotate(x[..., :half], ar), _rotate(x[..., half:], ac)], axis=-1)
    return out.astype(x.dtype)

def _rope_tail(t, n_rope, row, col):
    return jnp.concatenate([t[..., :-n_rope], _axial_rope(t[..., -n_rope:], row, col)], axis=-1)

def _ctx_attention(qc, kc, vc, scale, sink=None):
    B, Hq, L, _ = qc.shape
    Hk = kc.shape[1]
    G = Hq // Hk
    qg = qc.reshape(B, Hk, G, L, -1)
    s = jnp.einsum('bkgqd,bkcd->bkgqc', qg, kc).astype(jnp.float32) * scale
    if sink is not None:
        sk = jnp.broadcast_to(sink.reshape(1, Hk, G, 1, 1).astype(jnp.float32), s.shape[:-1] + (1,))
        p = _softmax32(jnp.concatenate([s, sk], axis=-1))[..., :L]
    else:
        p = _softmax32(s)
    o = jnp.einsum('bkgqc,bkcd->bkgqd', p.astype(vc.dtype), vc)
    return o.reshape(B, Hq, L, -1)

def _na_latent(q, k, v, kc, vc, rpb):
    B, H, S, d = q.shape
    rows = S // GRID_W
    wr = min(NA_WIN_ROWS, rows)
    scale = d ** -0.5
    r = jnp.arange(rows)
    ridx = jnp.clip(r - wr // 2, 0, rows - wr)[:, None] + jnp.arange(wr)[None, :]
    col = jnp.arange(GRID_W)
    c0 = jnp.clip(col - NA_WIN_COLS // 2, 0, GRID_W - NA_WIN_COLS)
    col_ok = (col[None, :] >= c0[:, None]) & (col[None, :] < c0[:, None] + NA_WIN_COLS)
    dr = ridx - r[:, None] + (NA_WIN_ROWS - 1)
    dc = jnp.clip(col[None, :] - col[:, None] + NA_WIN_COLS - 1, 0, 2 * NA_WIN_COLS - 2)
    bias = rpb[:, dr[:, None, :, None], dc[None, :, None, :]]
    qg = q.reshape(B, H, rows, GRID_W, d)
    kb = k.reshape(B, H, rows, GRID_W, d)[:, :, ridx]
    vb = v.reshape(B, H, rows, GRID_W, d)[:, :, ridx].reshape(B, H, rows, wr * GRID_W, d)
    s_loc = jnp.einsum('bhrqd,bhrwkd->bhrqwk', qg, kb).astype(jnp.float32) * scale + bias.astype(jnp.float32)
    s_loc = jnp.where(col_ok[:, None, :], s_loc, -jnp.inf).reshape(B, H, rows, GRID_W, wr * GRID_W)
    s_ctx = jnp.einsum('bhrqd,bhcd->bhrqc', qg, kc).astype(jnp.float32) * scale
    p = _softmax32(jnp.concatenate([s_loc, s_ctx], axis=-1)).astype(v.dtype)
    nl = wr * GRID_W
    o = jnp.einsum('bhrqj,bhrjd->bhrqd', p[..., :nl], vb) + jnp.einsum('bhrqc,bhcd->bhrqd', p[..., nl:], vc)
    return o.reshape(B, H, S, d)

def _mla_q(cq, q_norm, w_uq, q_g):
    B, T, _ = cq.shape
    q = (_rmsnorm(cq, q_norm) @ w_uq).reshape(B, T, MLA_HEADS, MLA_QK)
    return _rmsnorm(q, q_g).transpose(0, 2, 1, 3)

def _mla_kv(ckv, kr, kv_norm, w_ukv, k_g):
    B, T, _ = ckv.shape
    kv = (_rmsnorm(ckv, kv_norm) @ w_ukv).reshape(B, T, MLA_HEADS, MLA_NOPE + MLA_V)
    k_nope, v = kv[..., :MLA_NOPE], kv[..., MLA_NOPE:]
    k = jnp.concatenate([k_nope, jnp.broadcast_to(kr[:, :, None, :], (B, T, MLA_HEADS, MLA_ROPE))], axis=-1)
    return _rmsnorm(k, k_g).transpose(0, 2, 1, 3), v.transpose(0, 2, 1, 3)

def _mla_latent(q, k, v, kc, vc):
    B, H, S, dq = q.shape
    scale = dq ** -0.5
    k_all = jnp.concatenate([k, kc], axis=2)
    v_all = jnp.concatenate([v, vc], axis=2)
    nb = S // MLA_BLOCK
    qb = q.reshape(B, H, nb, MLA_BLOCK, dq).transpose(2, 0, 1, 3, 4)

    def block(qi):
        s = jnp.einsum('bhqd,bhkd->bhqk', qi, k_all).astype(jnp.float32) * scale
        return jnp.einsum('bhqk,bhkd->bhqd', _softmax32(s).astype(v_all.dtype), v_all)

    o = lax.map(block, qb)
    return o.transpose(1, 2, 0, 3, 4).reshape(B, H, S, -1)

def _swa_latent(q, k, v, kc, vc, sink):
    B, Hq, S, d = q.shape
    Hk = k.shape[1]
    G = Hq // Hk
    scale = d ** -0.5
    blk = SWA_BLOCK
    nb = S // blk
    qb = q.reshape(B, Hk, G, nb, blk, d)
    pad = jnp.zeros((B, Hk, blk, d), k.dtype)

    def band(t):
        tp = jnp.concatenate([pad, t, pad], axis=2).reshape(B, Hk, nb + 2, blk, d)
        return jnp.concatenate([tp[:, :, :-2], tp[:, :, 1:-1], tp[:, :, 2:]], axis=3)

    kb, vb = band(k), band(v)
    qpos = jnp.arange(nb)[:, None] * blk + jnp.arange(blk)[None, :]
    kpos = (jnp.arange(nb)[:, None] - 1) * blk + jnp.arange(3 * blk)[None, :]
    ok = (jnp.abs(qpos[:, :, None] - kpos[:, None, :]) <= SWA_WINDOW) & (kpos[:, None, :] >= 0) & (kpos[:, None, :] < S)
    s_loc = jnp.where(ok, jnp.einsum('bkgnqd,bknjd->bkgnqj', qb, kb).astype(jnp.float32) * scale, -jnp.inf)
    s_ctx = jnp.einsum('bkgnqd,bkcd->bkgnqc', qb, kc).astype(jnp.float32) * scale
    sk = jnp.broadcast_to(sink.reshape(1, Hk, G, 1, 1, 1).astype(jnp.float32), s_ctx.shape[:-1] + (1,))
    p = _softmax32(jnp.concatenate([s_loc, s_ctx, sk], axis=-1)).astype(v.dtype)
    nl = 3 * blk
    L = kc.shape[2]
    o = jnp.einsum('bkgnqj,bknjd->bkgnqd', p[..., :nl], vb) + jnp.einsum('bkgnqc,bkcd->bkgnqd', p[..., nl:nl + L], vc)
    return o.reshape(B, Hq, S, d)

def _ec_moe(h, router, w_gate, w_up, w_down):
    B, T, _ = h.shape
    cap = CAPACITY_FACTOR * T // N_EXPERTS
    aff = jax.nn.softmax((h @ router).astype(jnp.float32), axis=-1)
    gate, idx = lax.top_k(jnp.swapaxes(aff, 1, 2), cap)
    bidx = jnp.arange(B)[:, None, None]
    xg = h[bidx, idx]
    a = jnp.einsum('becd,edf->becf', xg, w_gate)
    u = jnp.einsum('becd,edf->becf', xg, w_up)
    y = jnp.einsum('becf,efd->becd', jax.nn.silu(a) * u, w_down) * gate[..., None].astype(h.dtype)
    return jnp.zeros_like(h).at[bidx, idx].add(y)

def _gated_merge(gl, y_na, y_mla, y_swa, w_o):
    g = jax.nn.sigmoid(gl.astype(jnp.float32)).astype(y_na.dtype)
    g = g.reshape(gl.shape[:-1] + (N_BRANCH, D_MODEL))
    return (g[..., 0, :] * y_na + g[..., 1, :] * y_mla + g[..., 2, :] * y_swa) @ w_o

def _layer(x, ctx, c_act, cctx_act, row, col, last,
           norm1_g, norm2_g, w_ada, b_ada, w_in,
           na_q_g, na_k_g, na_rpb,
           mla_q_norm, mla_w_uq, mla_kv_norm, mla_w_ukv, mla_q_g, mla_k_g,
           swa_q_g, swa_k_g, swa_sink,
           w_na_o, w_mla_o, w_swa_o, w_o,
           router, w_gate, w_up, w_down):
    mod = jnp.split((c_act @ w_ada + b_ada)[:, None, :], 6, axis=-1)
    mod_c = jnp.split(cctx_act @ w_ada + b_ada, 6, axis=-1)
    splits = [int(i) for i in np.cumsum(IN_SPLITS)[:-1]]

    h = _rmsnorm(x, norm1_g) * (1 + mod[1]) + mod[0]
    hc = _rmsnorm(ctx, norm1_g) * (1 + mod_c[1]) + mod_c[0]
    (na_q, na_k, na_v, mla_cq, mla_ckv, mla_kr, sw_q, sw_k, sw_v, gl) = jnp.split(h @ w_in, splits, axis=-1)
    (na_qc, na_kc, na_vc, mla_cqc, mla_ckvc, mla_krc, sw_qc, sw_kc, sw_vc, glc) = jnp.split(hc @ w_in, splits, axis=-1)

    na_kc_h = _rmsnorm(_heads(na_kc, NA_HEADS), na_k_g)
    na_vc_h = _heads(na_vc, NA_HEADS)
    o_na = _na_latent(_rmsnorm(_heads(na_q, NA_HEADS), na_q_g), _rmsnorm(_heads(na_k, NA_HEADS), na_k_g),
                      _heads(na_v, NA_HEADS), na_kc_h, na_vc_h, na_rpb)
    y_na = _merge_heads(o_na) @ w_na_o

    mla_kc_h, mla_vc_h = _mla_kv(mla_ckvc, mla_krc, mla_kv_norm, mla_w_ukv, mla_k_g)
    q_m = _rope_tail(_mla_q(mla_cq, mla_q_norm, mla_w_uq, mla_q_g), MLA_ROPE, row, col)
    k_m, v_m = _mla_kv(mla_ckv, mla_kr, mla_kv_norm, mla_w_ukv, mla_k_g)
    y_mla = _merge_heads(_mla_latent(q_m, _rope_tail(k_m, MLA_ROPE, row, col), v_m, mla_kc_h, mla_vc_h)) @ w_mla_o

    sw_kc_h = _rmsnorm(_heads(sw_kc, SWA_KV_HEADS), swa_k_g)
    sw_vc_h = _heads(sw_vc, SWA_KV_HEADS)
    q_s = _axial_rope(_rmsnorm(_heads(sw_q, SWA_HEADS), swa_q_g), row, col)
    k_s = _axial_rope(_rmsnorm(_heads(sw_k, SWA_KV_HEADS), swa_k_g), row, col)
    y_swa = _merge_heads(_swa_latent(q_s, k_s, _heads(sw_v, SWA_KV_HEADS), sw_kc_h, sw_vc_h, swa_sink)) @ w_swa_o

    x_new = x + mod[2] * _gated_merge(gl, y_na, y_mla, y_swa, w_o)
    h2 = _rmsnorm(x_new, norm2_g) * (1 + mod[4]) + mod[3]
    x_new = x_new + mod[5] * _ec_moe(h2, router, w_gate, w_up, w_down)
    if last:
        return x_new, ctx

    yc_na = _merge_heads(_ctx_attention(_rmsnorm(_heads(na_qc, NA_HEADS), na_q_g), na_kc_h, na_vc_h, NA_DIM ** -0.5)) @ w_na_o
    yc_mla = _merge_heads(_ctx_attention(_mla_q(mla_cqc, mla_q_norm, mla_w_uq, mla_q_g), mla_kc_h, mla_vc_h, MLA_QK ** -0.5)) @ w_mla_o
    yc_swa = _merge_heads(_ctx_attention(_rmsnorm(_heads(sw_qc, SWA_HEADS), swa_q_g), sw_kc_h, sw_vc_h, SWA_DIM ** -0.5, swa_sink)) @ w_swa_o
    ctx_new = ctx + mod_c[2] * _gated_merge(glc, yc_na, yc_mla, yc_swa, w_o)
    hc2 = _rmsnorm(ctx_new, norm2_g) * (1 + mod_c[4]) + mod_c[3]
    ctx_new = ctx_new + mod_c[5] * _ec_moe(hc2, router, w_gate, w_up, w_down)
    return x_new, ctx_new

def setup_inputs(seed: int = 0) -> dict:
    key = jax.random.key(seed)
    ks = jax.random.split(key, 32)
    L, D = DEPTH, D_MODEL

    def nrm(k, shape, scale):
        return jax.random.normal(k, shape, jnp.float32) * scale

    def gain(k, shape):
        return 1.0 + 0.1 * jax.random.normal(k, shape, jnp.float32)

    return {
        'x': nrm(ks[0], (BATCH, SEQ, D), 1.0),
        'c': nrm(ks[1], (BATCH, D), 1.0),
        'ctx': nrm(ks[2], (BATCH, CTX_LEN, D), 1.0),
        'c_ctx': nrm(ks[3], (D,), 1.0),
        'norm1_g': gain(ks[4], (L, D)),
        'norm2_g': gain(ks[5], (L, D)),
        'w_ada': nrm(ks[6], (L, D, 6 * D), 0.5 * D ** -0.5),
        'b_ada': nrm(ks[7], (L, 6 * D), 0.01),
        'w_in': nrm(ks[8], (L, D, D_IN), D ** -0.5),
        'na_q_g': gain(ks[9], (L, NA_DIM)),
        'na_k_g': gain(ks[10], (L, NA_DIM)),
        'na_rpb': nrm(ks[11], (L, NA_HEADS, 2 * NA_WIN_ROWS - 1, 2 * NA_WIN_COLS - 1), 0.5),
        'mla_q_norm': gain(ks[12], (L, MLA_Q_RANK)),
        'mla_w_uq': nrm(ks[13], (L, MLA_Q_RANK, MLA_HEADS * MLA_QK), MLA_Q_RANK ** -0.5),
        'mla_kv_norm': gain(ks[14], (L, MLA_KV_RANK)),
        'mla_w_ukv': nrm(ks[15], (L, MLA_KV_RANK, MLA_HEADS * (MLA_NOPE + MLA_V)), MLA_KV_RANK ** -0.5),
        'mla_q_g': gain(ks[16], (L, MLA_QK)),
        'mla_k_g': gain(ks[17], (L, MLA_QK)),
        'swa_q_g': gain(ks[18], (L, SWA_DIM)),
        'swa_k_g': gain(ks[19], (L, SWA_DIM)),
        'swa_sink': nrm(ks[20], (L, SWA_HEADS), 0.5),
        'w_na_o': nrm(ks[21], (L, NA_W, D), NA_W ** -0.5),
        'w_mla_o': nrm(ks[22], (L, MLA_W, D), MLA_W ** -0.5),
        'w_swa_o': nrm(ks[23], (L, SWA_W, D), SWA_W ** -0.5),
        'w_o': nrm(ks[24], (L, D, D), D ** -0.5),
        'router': nrm(ks[25], (L, D, N_EXPERTS), D ** -0.5),
        'w_gate': nrm(ks[26], (L, N_EXPERTS, D, EXPERT_FF), D ** -0.5),
        'w_up': nrm(ks[27], (L, N_EXPERTS, D, EXPERT_FF), D ** -0.5),
        'w_down': nrm(ks[28], (L, N_EXPERTS, EXPERT_FF, D), EXPERT_FF ** -0.5),
    }

def reference(x, c, ctx, c_ctx, norm1_g, norm2_g, w_ada, b_ada, w_in,
              na_q_g, na_k_g, na_rpb,
              mla_q_norm, mla_w_uq, mla_kv_norm, mla_w_ukv, mla_q_g, mla_k_g,
              swa_q_g, swa_k_g, swa_sink,
              w_na_o, w_mla_o, w_swa_o, w_o,
              router, w_gate, w_up, w_down):
    S = x.shape[1]
    t = jnp.arange(S)
    row = t // GRID_W
    col = t % GRID_W
    c_act = jax.nn.silu(c)
    cctx_act = jax.nn.silu(c_ctx)
    for l in range(DEPTH):
        x, ctx = _layer(x, ctx, c_act, cctx_act, row, col, l == DEPTH - 1,
                        norm1_g[l], norm2_g[l], w_ada[l], b_ada[l], w_in[l],
                        na_q_g[l], na_k_g[l], na_rpb[l],
                        mla_q_norm[l], mla_w_uq[l], mla_kv_norm[l], mla_w_ukv[l], mla_q_g[l], mla_k_g[l],
                        swa_q_g[l], swa_k_g[l], swa_sink[l],
                        w_na_o[l], w_mla_o[l], w_swa_o[l], w_o[l],
                        router[l], w_gate[l], w_up[l], w_down[l])
    return x


_drawn_inputs = setup_inputs


def setup_inputs(seed=0):
    import zlib

    import numpy as np

    out = dict(_drawn_inputs(seed))
    spreads = {}
    factors = {'norm1_g': 6.546,
     'b_ada': 6.248,
     'na_q_g': 8.0,
     'na_k_g': 8.0,
     'na_rpb': 6.832,
     'mla_q_norm': 8.0,
     'mla_kv_norm': 8.0,
     'mla_q_g': 8.0,
     'mla_k_g': 8.0,
     'swa_q_g': 8.0,
     'swa_k_g': 8.0,
     'swa_sink': 8.0}
    for name, (base, spread) in spreads.items():
        noise = np.random.default_rng([zlib.crc32(name.encode()), seed]).standard_normal(out[name].shape)
        drawn = base * np.exp(spread * noise) if base else spread * noise
        out[name] = __import__('jax').numpy.asarray(drawn.astype(out[name].dtype))
    for name, factor in factors.items():
        out[name] = (out[name] * factor).astype(out[name].dtype)
    return out
```

```python
from contextlib import ExitStack

import numpy as np

import concourse.bass as bass
from concourse import mybir

F32 = mybir.dt.float32
ALU = mybir.AluOpType
ACT = mybir.ActivationFunctionType
AX = mybir.AxisListType
ds = bass.ds

P = 128
GRID_W = 64
NA_HEADS, NA_DIM, NA_WIN_COLS = 6, 64, 16
MLA_HEADS, MLA_Q_RANK, MLA_KV_RANK, MLA_NOPE, MLA_ROPE, MLA_V = 4, 256, 128, 128, 64, 128
MLA_QK = MLA_NOPE + MLA_ROPE
SWA_HEADS, SWA_KV_HEADS, SWA_DIM, SWA_WINDOW = 6, 2, 64, 128
N_EXPERTS, EXPERT_FF, CAPACITY_FACTOR = 16, 1024, 2
ROPE_BASE = 10000.0
EPS = 1e-6
MASKED = -1e30

NA_W = NA_HEADS * NA_DIM
C_NAQ, C_NAK, C_NAV = 0, NA_W, 2 * NA_W
C_CQ = 3 * NA_W
C_CKV = C_CQ + MLA_Q_RANK
C_KR = C_CKV + MLA_KV_RANK
C_SQ = C_KR + MLA_ROPE
C_SK = C_SQ + SWA_HEADS * SWA_DIM
C_SV = C_SK + SWA_KV_HEADS * SWA_DIM
C_GL = C_SV + SWA_KV_HEADS * SWA_DIM
GROUPS = [(C_NAQ, NA_W, False), (C_NAK, NA_W, True), (C_NAV, NA_W, True),
          (C_CQ, C_SQ - C_CQ, True), (C_SQ, C_SK - C_SQ, False), (C_SK, C_GL - C_SK, True)]

R_NA, R_SW, R_CQ, R_CKV, R_KR, N_STATS = 0, 12, 20, 21, 22, 23


class Chain:

    def __init__(self, eng, sem, base=0):
        self.eng, self.sem, self.base, self.n = eng, sem, base, 0

    def link(self, instruction):
        self.n += 1
        instruction.then_inc(self.sem, 1)
        self.eng.wait_ge(self.sem, self.base + self.n)


def constants(S, L):
    nt, nl = (S + L) // P, S // P
    t = np.arange(S)
    f = SWA_DIM // 4
    inv = (np.float32(ROPE_BASE) ** (-np.arange(f, dtype=np.float32) / np.float32(f))).astype(np.float32)
    ar = ((t // GRID_W).astype(np.float32)[:, None] * inv).astype(np.float32)
    ac = ((t % GRID_W).astype(np.float32)[:, None] * inv).astype(np.float32)
    cos = np.concatenate([np.cos(ar), np.cos(ar), np.cos(ac), np.cos(ac)], 1)
    sin = np.concatenate([-np.sin(ar), np.sin(ar), -np.sin(ac), np.sin(ac)], 1)
    cos = np.concatenate([cos, np.ones((L, 64))]).reshape(nt, P, 64).transpose(1, 0, 2)
    sin = np.concatenate([sin, np.zeros((L, 64))]).reshape(nt, P, 64).transpose(1, 0, 2)
    i, j = np.arange(P)[:, None], np.arange(P)[None, :]
    band = np.concatenate([np.where(j >= i, 0, MASKED), np.zeros((P, P)), np.where(j <= i, 0, MASKED)], 1)
    col = np.arange(GRID_W)
    c0 = np.clip(col - NA_WIN_COLS // 2, 0, GRID_W - NA_WIN_COLS)
    ok = (col[None] >= c0[:, None]) & (col[None] < c0[:, None] + NA_WIN_COLS)
    colmask = np.tile(np.where(ok, 0, MASKED), (2, 1))
    kl, kc = CAPACITY_FACTOR * S // N_EXPERTS, CAPACITY_FACTOR * L // N_EXPERTS
    slots = np.tile(np.arange(1, kl + 1), (P, 1))
    p = np.arange(P)
    slot_of = np.stack([p % kl + 1, p % kc + 1], 1)
    e = np.arange(N_EXPERTS)[:, None, None]
    pair = np.arange(N_EXPERTS // 2)[None, :, None]
    pick = np.concatenate([e == 2 * pair + np.arange(2 * kl)[None, None] // kl,
                           e == 2 * pair + np.arange(2 * kc)[None, None] // kc], 2).reshape(N_EXPERTS, -1)
    return {n: np.ascontiguousarray(a, np.float32) for n, a in dict(
        ident=np.eye(P), cos=cos.reshape(P, -1), sin=sin.reshape(P, -1), band=band, colmask=colmask,
        slots=slots, slot_of=slot_of, pick=pick).items()}


def build(nc, x, c, ctx, c_ctx, norm1_g, norm2_g, w_ada, b_ada, w_in, na_q_g, na_k_g, na_rpb,
          mla_q_norm, mla_w_uq, mla_kv_norm, mla_w_ukv, mla_q_g, mla_k_g, swa_q_g, swa_k_g, swa_sink,
          w_na_o, w_mla_o, w_swa_o, w_o, router, w_gate, w_up, w_down, out, dbg=None, stop=None):
    _, S, D = x.shape
    L = ctx.shape[1]
    DEPTH = w_in.shape[0]
    T = S + L
    NT, NL = T // P, S // P
    KD = D // P
    NM = 6 * KD
    KL, KC = CAPACITY_FACTOR * S // N_EXPERTS, CAPACITY_FACTOR * L // N_EXPERTS
    MS = KL + KC
    FF = EXPERT_FF
    nsem = [0]

    class Scope(ExitStack):

        def __init__(self):
            super().__init__()
            self.sems = []
            self.callback(self.clear)

        def clear(self):
            if self.sems:
                nc.clear_and_free_semaphores(self.sems)
                nc.all_engine_barrier()

    def sem(stack, name):
        nsem[0] += 1
        stack.sems.append(nc.alloc_semaphore(f"{name}_{nsem[0]}"))
        return stack.sems[-1]

    def sb(stack, name, shape):
        nsem[0] += 1
        return stack.enter_context(nc.sbuf_tensor(f"{name}_{nsem[0]}", shape, F32))

    top = Scope()
    const = {n: nc.inline_tensor(a, name=f"const_{n}") for n, a in constants(S, L).items()}
    const = {n: (a.ap() if hasattr(a, "ap") else a) for n, a in const.items()}
    RPBW = 2 * GRID_W - 1
    rpb_pad = nc.dram_tensor("rpb_padded", [GRID_W, NA_HEADS * 15, RPBW], F32, kind="Internal").ap()

    with top:
        xT = sb(top, "xT", [P, KD, T])
        ident = sb(top, "ident", [P, P])
        ones = sb(top, "ones", [P, P])
        cos = sb(top, "cos", [P, NT, 64])
        sin = sb(top, "sin", [P, NT, 64])
        cT = sb(top, "cT", [P, 2, KD])
        modT = sb(top, "modT", [P, NM, 2])
        vecT = sb(top, "vecT", [P, NM + 2 * KD])
        coef = sb(top, "coef", [P, 2, KD, 2])
        ps = top.enter_context(nc.psum_tensor("ps", [P, 8, 512], F32))

        def streams(ctx_too):
            return [(0, 0, S), (1, S, L)][:1 + ctx_too]

        def finish(name):
            return stop == name

        def setup():
            with Scope() as st:
                rows = sb(st, "rows", [P, NT, D])
                crow = sb(st, "crow", [2 * KD, P])
                loaded, cl, ready = sem(st, "loaded"), sem(st, "c_loaded"), sem(st, "ones_ready")
                turned, kept_v, kept_a = sem(st, "turned"), sem(st, "kept_by_dve"), sem(st, "kept_by_act")
                block = st.enter_context(nc.Block())

                @block.sync
                def _(sp):
                    sp.dma_start(ident[:], const["ident"]).then_inc(cl, 16)
                    sp.dma_start(crow[0:KD, :], c.rearrange("b (k p) -> (b k) p", p=P)).then_inc(cl, 16)
                    sp.dma_start(crow[KD:2 * KD, :], c_ctx.rearrange("(k p) -> k p", p=P)).then_inc(cl, 16)
                    sp.dma_start(rows[:, 0:NL, :], x[0].rearrange("(t p) d -> p t d", p=P)).then_inc(loaded, 16)
                    sp.dma_start(rows[:, NL:NT, :], ctx[0].rearrange("(t p) d -> p t d", p=P)).then_inc(loaded, 16)
                    sp.dma_start(cos[:].rearrange("p a b -> p (a b)"), const["cos"]).then_inc(cl, 16)
                    sp.dma_start(sin[:].rearrange("p a b -> p (a b)"), const["sin"]).then_inc(cl, 16)
                    sp.wait_ge(cl, 80)

                @block.gpsimd
                def _(pool):
                    nc.gpsimd.memset(ones[:], 1.0).then_inc(ready, 1)

                @block.tensor
                def _(pe):
                    pe.wait_ge(cl, 80)
                    nc.tensor.transpose(ps[:, 7, 0:2 * KD], crow[:], ident[0:2 * KD, 0:2 * KD]).then_inc(turned, 1)
                    pe.wait_ge(loaded, 32)
                    for k in range(KD):
                        for s, t0, n in streams(True):
                            b = 2 * (k % 2) + s
                            if k >= 2:
                                pe.wait_ge((kept_v, kept_a)[s], k - 1)
                            for t in range(n // P):
                                mm = nc.tensor.transpose(ps[:, b, t * P:(t + 1) * P],
                                                         rows[:, t0 // P + t, k * P:(k + 1) * P], ident[:])
                            mm.then_inc(turned, 1)

                @block.vector
                def _(dve):
                    for k in range(KD):
                        dve.wait_ge(turned, 2 * k + 2)
                        nc.vector.tensor_copy(xT[:, k, 0:S], ps[:, 2 * (k % 2), 0:S]).then_inc(kept_v, 1)

                @block.scalar
                def _(act):
                    act.wait_ge(turned, 1)
                    nc.scalar.activation(cT[:].rearrange("p s k -> p (s k)"), ps[:, 7, 0:2 * KD], ACT.Silu)
                    for k in range(KD):
                        act.wait_ge(turned, 2 * k + 3)
                        nc.scalar.copy(xT[:, k, S:T], ps[:, 2 * (k % 2) + 1, 0:L]).then_inc(kept_a, 1)

        def modulation(l):
            NB = 6 * D // 512
            with Scope() as st:
                wbuf = [sb(st, f"w_ada{s}", [P, KD, 512]) for s in range(2)]
                row = [sb(st, f"mod_row{s}", [P, 512]) for s in range(2)]
                vrow = sb(st, "vec_rows", [NM + 2 * KD, P])
                wl = [sem(st, f"w_ada_loaded{s}") for s in range(2)]
                vl, mm_done, row_done = sem(st, "vec_loaded"), sem(st, "mod_mm"), sem(st, "mod_row")
                turned, kept, vt, ch = sem(st, "mod_turned"), sem(st, "mod_kept"), sem(st, "vec_turned"), sem(st, "mod_chain")
                block = st.enter_context(nc.Block())
                wv = w_ada[l].rearrange("(k p) n -> p k n", p=P)

                @block.sync
                def _(sp):
                    sp.dma_start(vrow[0:NM, :], b_ada[l].rearrange("(k p) -> k p", p=P)).then_inc(vl, 16)
                    sp.dma_start(vrow[NM:NM + KD, :], norm1_g[l].rearrange("(k p) -> k p", p=P)).then_inc(vl, 16)
                    sp.dma_start(vrow[NM + KD:, :], norm2_g[l].rearrange("(k p) -> k p", p=P)).then_inc(vl, 16)
                    for s in range(2):
                        sp.dma_start(wbuf[s][:], wv[:, :, s * 512:(s + 1) * 512]).then_inc(wl[s], 16)
                    with sp.Fori(0, NB // 2 - 1) as i:
                        for s in range(2):
                            sp.wait_ge(mm_done, 2 * i + s + 1)
                            sp.dma_start(wbuf[s][:], wv[:, :, ds((2 * i + s + 2) * 512, 512)]).then_inc(wl[s], 16)

                @block.tensor
                def _(pe):
                    pe.wait_ge(vl, 48)
                    nc.tensor.transpose(ps[:, 4, 0:NM + 2 * KD], vrow[:], ident[0:NM + 2 * KD, 0:NM + 2 * KD]).then_inc(vt, 1)
                    with pe.Fori(0, NB // 2) as i:
                        for s in range(2):
                            pe.wait_ge(wl[s], 16 * i + 16)
                            pe.wait_ge(row_done, 2 * i)
                            for k in range(KD):
                                mm = nc.tensor.matmul(ps[0:2, s, :], cT[:, :, k], wbuf[s][:, k, :],
                                                      start=(k == 0), stop=(k == KD - 1))
                            mm.then_inc(mm_done, 1)
                        for s in range(2):
                            pe.wait_ge(row_done, 2 * i + s + 1)
                            pe.wait_ge(kept, 2 * i)
                            for j in range(4):
                                mm = nc.tensor.transpose(ps[:, 2 + s, j * P:(j + 1) * P], row[s][:, j * P:(j + 1) * P], ident[:])
                            mm.then_inc(turned, 1)

                @block.vector
                def _(dve):
                    for s in range(2):
                        nc.vector.memset(row[s][:], 0.0).then_inc(ch, 1)
                    dve.wait_ge(ch, 2)
                    dve.wait_ge(vt, 1)
                    nc.vector.tensor_copy(vecT[:], ps[:, 4, 0:NM + 2 * KD]).then_inc(ch, 1)
                    with dve.Fori(0, NB // 2) as i:
                        for s in range(2):
                            dve.wait_ge(mm_done, 2 * i + s + 1)
                            dve.wait_ge(turned, 2 * i)
                            nc.vector.tensor_copy(row[s][0:2, :], ps[0:2, s, :]).then_inc(row_done, 1)
                        for s in range(2):
                            dve.wait_ge(turned, 2 * i + s + 1)
                            nc.vector.tensor_copy(modT[:, ds((2 * i + s) * 4, 4), :],
                                                  ps[:, 2 + s, :].rearrange("p (a b) -> p a b", b=P)[:, :, 0:2]).then_inc(kept, 1)
                    dve.wait_ge(kept, NB)
                    dve.wait_ge(ch, 3)
                    chain = Chain(dve, ch, 3)
                    chain.link(nc.vector.tensor_tensor(modT[:], modT[:],
                                                       vecT[:, 0:NM].unsqueeze(2).to_broadcast([P, NM, 2]), ALU.add))
                    for n in range(2):
                        m = (1 + 3 * n) * KD
                        chain.link(nc.vector.tensor_scalar(coef[:, n], modT[:, m:m + KD, :], 1.0, None, ALU.add))
                        g = vecT[:, NM + n * KD:NM + (n + 1) * KD]
                        chain.link(nc.vector.tensor_tensor(coef[:, n], coef[:, n],
                                                           g.unsqueeze(2).to_broadcast([P, KD, 2]), ALU.mult))

        def norm(n, hT, ctx_too, ahead=None):
            W = T if ctx_too else S
            with Scope() as st:
                sq = [sb(st, f"sq{s}", [P, W]) for s in range(2)]
                rs = sb(st, "rs", [P, W])
                tmp = [sb(st, f"scaled{s}", [P, W]) for s in range(2)]
                squared, summed, root, scaled, done = (sem(st, q) for q in ("squared", "summed", "root", "scaled", "normed"))
                ch = sem(st, "norm_chain")
                block = st.enter_context(nc.Block())

                @block.sync
                def _(sp):
                    if ahead:
                        ahead(sp)

                @block.scalar
                def _(act):
                    for k in range(KD):
                        if k >= 2:
                            act.wait_ge(summed, k - 1)
                        nc.scalar.activation(sq[k % 2][:], xT[:, k, 0:W], ACT.Square).then_inc(squared, 1)
                    act.wait_ge(ch, 1)
                    nc.scalar.activation(rs[:], rs[:], ACT.Sqrt).then_inc(root, 1)
                    for k in range(KD):
                        act.wait_ge(scaled, k + 1)
                        for s, t0, m in streams(ctx_too):
                            last = nc.scalar.activation(hT[:, k, t0:t0 + m], tmp[k % 2][:, t0:t0 + m], ACT.Identity,
                                                        bias=modT[:, 3 * n * KD + k, s:s + 1], scale=coef[:, n, k, s:s + 1])
                        last.then_inc(done, 1)

                @block.tensor
                def _(pe):
                    for k in range(KD):
                        pe.wait_ge(squared, k + 1)
                        for s, t0, m in streams(ctx_too):
                            mm = nc.tensor.matmul(ps[:, s, 0:m], ones[:], sq[k % 2][:, t0:t0 + m],
                                                  start=(k == 0), stop=(k == KD - 1))
                        mm.then_inc(summed, 1)

                @block.vector
                def _(dve):
                    dve.wait_ge(summed, KD)
                    for s, t0, m in streams(ctx_too):
                        last = nc.vector.tensor_scalar(rs[:, t0:t0 + m], ps[:, s, 0:m], 1.0 / D, EPS, ALU.mult, ALU.add)
                    last.then_inc(ch, 1)
                    dve.wait_ge(root, 1)
                    nc.vector.reciprocal(rs[:], rs[:]).then_inc(ch, 1)
                    dve.wait_ge(ch, 2)
                    for k in range(KD):
                        if k >= 2:
                            dve.wait_ge(done, k - 1)
                        nc.vector.tensor_tensor(tmp[k % 2][:], xT[:, k, 0:W], rs[:], ALU.mult).then_inc(scaled, 1)

        def projection(l, hT, proj, last_layer):
            with Scope() as st:
                wbuf = [sb(st, f"w_in{s}", [P, KD, 448]) for s in range(2)]
                wl = [sem(st, f"w_in_loaded{s}") for s in range(2)]
                mm_done = sem(st, "proj_mm")
                kept = [sem(st, "proj_kept_dve"), sem(st, "proj_kept_act")]
                block = st.enter_context(nc.Block())
                wv = w_in[l].rearrange("(k p) n -> p k n", p=P)
                work = [(g, t) for g in range(len(GROUPS)) for t in range(NT if not last_layer or GROUPS[g][2] else NL)]

                @block.sync
                def _(sp):
                    for g, (c0, n, _) in enumerate(GROUPS):
                        if g >= 2:
                            sp.wait_ge(mm_done, sum(w[0] <= g - 2 for w in work))
                        sp.dma_start(wbuf[g % 2][:, :, 0:n], wv[:, :, c0:c0 + n]).then_inc(wl[g % 2], 16)

                @block.tensor
                def _(pe):
                    for j, (g, t) in enumerate(work):
                        if t == 0:
                            pe.wait_ge(wl[g % 2], 16 * (g // 2 + 1))
                        if j >= 4:
                            pe.wait_ge(kept[j % 2], (j - 4) // 2 + 1)
                        n = GROUPS[g][1]
                        for k in range(KD):
                            mm = nc.tensor.matmul(ps[:, j % 4, 0:n], hT[:, k, t * P:(t + 1) * P], wbuf[g % 2][:, k, 0:n],
                                                  start=(k == 0), stop=(k == KD - 1))
                        mm.then_inc(mm_done, 1)

                def keep(eng, copy, parity):
                    for j, (g, t) in enumerate(work):
                        if j % 2 == parity:
                            c0, n, _ = GROUPS[g]
                            eng.wait_ge(mm_done, j + 1)
                            copy(proj[:, t, c0:c0 + n], ps[:, j % 4, 0:n]).then_inc(kept[parity], 1)

                @block.vector
                def _(dve):
                    keep(dve, nc.vector.tensor_copy, 0)

                @block.scalar
                def _(act):
                    keep(act, nc.scalar.copy, 1)

        def statistics(proj, stat, last_layer):
            full = [(C_NAQ, 64, 12, R_NA), (C_CQ, 256, 1, R_CQ), (C_CKV, 128, 1, R_CKV), (C_KR, 64, 1, R_KR), (C_SQ, 64, 8, R_SW)]
            keys = [(C_NAK, 64, 6, R_NA + 6), (C_CKV, 128, 1, R_CKV), (C_KR, 64, 1, R_KR), (C_SK, 64, 2, R_SW + 6)]
            with Scope() as st:
                sq = [sb(st, f"stat_sq{s}", [P, C_SV]) for s in range(2)]
                squared, summed, root, ch = (sem(st, q) for q in ("stat_squared", "stat_summed", "stat_root", "stat_chain"))
                block = st.enter_context(nc.Block())
                segs = [keys if last_layer and t >= NL else full for t in range(NT)]

                @block.scalar
                def _(act):
                    for t in range(NT):
                        if t >= 2:
                            act.wait_ge(summed, t - 1)
                        for c0, w, n, _ in segs[t]:
                            last = nc.scalar.activation(sq[t % 2][:, c0:c0 + n * w], proj[:, t, c0:c0 + n * w], ACT.Square)
                        last.then_inc(squared, 1)
                    act.wait_ge(ch, 4)
                    nc.scalar.activation(stat[:, :, 0:R_KR], stat[:, :, 0:R_KR], ACT.Sqrt).then_inc(root, 1)

                @block.vector
                def _(dve):
                    chain = Chain(dve, ch)
                    chain.link(nc.vector.memset(stat[:], 0.0))
                    for t in range(NT):
                        dve.wait_ge(squared, t + 1)
                        for c0, w, n, r in segs[t]:
                            last = nc.vector.tensor_reduce(stat[:, t, r:r + n],
                                                           sq[t % 2][:, c0:c0 + n * w].rearrange("p (h d) -> p h d", d=w),
                                                           AX.X, ALU.add)
                        last.then_inc(summed, 1)
                    dve.wait_ge(summed, NT)
                    for r0, r1, w in ((R_NA, R_CQ, 64), (R_CQ, R_CKV, 256), (R_CKV, R_KR, 128)):
                        nc.vector.tensor_scalar(stat[:, :, r0:r1], stat[:, :, r0:r1], 1.0 / w, EPS,
                                                ALU.mult, ALU.add).then_inc(ch, 1)
                    dve.wait_ge(root, 1)
                    nc.vector.reciprocal(stat[:, :, 0:R_KR], stat[:, :, 0:R_KR])

        SWAP = [(a * 32 + b * 16, a * 32 + (1 - b) * 16) for a in range(2) for b in range(2)]

        def rope_tables(chain, cg, sg, g, scale):
            chain.link(nc.vector.tensor_scalar(g[:], g[:], scale, None, ALU.mult))
            nc.vector.tensor_tensor(cg[:], cos[:], g[:].unsqueeze(1).to_broadcast([P, NT, 64]), ALU.mult)
            for d, o in SWAP:
                last = nc.vector.tensor_tensor(sg[:, :, d:d + 16], sin[:, :, d:d + 16],
                                               g[:, o:o + 16].unsqueeze(1).to_broadcast([P, NT, 16]), ALU.mult)
            chain.link(last)

        def rope(chain, res, x, part, cg, sg, nt, heads):
            nc.vector.tensor_tensor(res, x, cg[:, 0:nt].unsqueeze(2).to_broadcast([P, nt, heads, 64]), ALU.mult)
            for d, o in SWAP:
                last = nc.vector.tensor_tensor(part[:, :, :, d:d + 16], x[:, :, :, o:o + 16],
                                               sg[:, 0:nt, d:d + 16].unsqueeze(2).to_broadcast([P, nt, heads, 16]), ALU.mult)
            chain.link(last)
            return nc.vector.tensor_tensor(res, res, part, ALU.add)

        class Attention:

            def __init__(self, st, name, heads, dv, tiles, key_tiles):
                self.units = [(hh, t) for hh in range(heads) for t in tiles]
                self.U, self.dv, self.key_tiles, self.tiles = len(self.units), dv, key_tiles, tiles
                assert self.U % 2 == 0
                self.pexp = [sb(st, f"{name}_exp{s}", [P, T]) for s in range(2)]
                self.pT = [sb(st, f"{name}_expT{s}", [P, NT, P]) for s in range(2)]
                self.rowmax = sb(st, f"{name}_max", [P, 2, 4])
                self.rowsum = sb(st, f"{name}_sum", [P, 2, 3])
                self.osb = sb(st, f"{name}_o", [P, len(tiles), P])
                self.scored = sem(st, f"{name}_scored")
                self.maxed = sem(st, f"{name}_maxed")
                self.exped = sem(st, f"{name}_exped")
                self.turned = sem(st, f"{name}_turned")
                self.kept_lo = sem(st, f"{name}_kept_lo")
                self.kept_hi = sem(st, f"{name}_kept_hi")
                self.valued = sem(st, f"{name}_valued")
                self.divided = sem(st, f"{name}_divided")
                self.o_turned = sem(st, f"{name}_o_turned")
                self.o_kept = sem(st, f"{name}_o_kept")
                self.staged = sem(st, f"{name}_staged")
                self.q_turned = sem(st, f"{name}_q_turned")
                self.qk_kept = sem(st, f"{name}_qk_kept")
                self.chain = sem(st, f"{name}_chain")

            def pe_units(self, pe, i, score, value):
                def transposes(u):
                    t = self.units[u][1]
                    n = i * self.U + u
                    pe.wait_ge(self.exped, n + 1)
                    pe.wait_ge(self.kept_lo, n)
                    pe.wait_ge(self.kept_hi, n)
                    kt = self.key_tiles(t)
                    for q in range(len(kt)):
                        h = (len(kt) + 1) // 2
                        mm = nc.tensor.transpose(ps[:, 4 + q // h, (q % h) * P:(q % h + 1) * P],
                                                 self.pexp[u % 2][:, q * P:(q + 1) * P], ident[:])
                    mm.then_inc(self.turned, 1)

                def values(u):
                    hh, t = self.units[u]
                    n = i * self.U + u
                    pe.wait_ge(self.kept_lo, n + 1)
                    pe.wait_ge(self.kept_hi, n + 1)
                    pe.wait_ge(self.divided, n - 1 if u >= 1 else n)
                    kt = self.key_tiles(t)
                    o = ps[:, 6 + u % 2, 0:self.dv]
                    for q, k in enumerate(kt):
                        mm = nc.tensor.matmul(o, self.pT[u % 2][:, q, :], value(hh, k), start=(q == 0), stop=(q == len(kt) - 1))
                    mm.then_inc(self.valued, 1)

                def scores(u):
                    hh, t = self.units[u]
                    n = i * self.U + u
                    pe.wait_ge(self.exped, n - 1 if u >= 1 else n)
                    score(hh, t, 2 * (u % 2)).then_inc(self.scored, 1)

                scores(0)
                for u in range(self.U):
                    if u + 1 < self.U:
                        scores(u + 1)
                    transposes(u)
                    values(u)
                pe.wait_ge(self.divided, (i + 1) * self.U)
                pe.wait_ge(self.kept_lo, (i + 1) * self.U)
                pe.wait_ge(self.kept_hi, (i + 1) * self.U)
                for q in range(len(self.tiles)):
                    mm = nc.tensor.transpose(ps[:, 4 if q < NL else 5, (q % NL) * P:(q % NL + 1) * P],
                                             self.osb[:, q, :], ident[:])
                mm.then_inc(self.o_turned, 1)

            def dve_units(self, dve, i, chain, maximum, more_sum=None):
                def keep_hi(u):
                    t = self.units[u][1]
                    n = i * self.U + u
                    kt = len(self.key_tiles(t))
                    dve.wait_ge(self.turned, n + 1)
                    dve.wait_ge(self.valued, n - 1 if u >= 1 else n)
                    h = (kt + 1) // 2
                    nc.vector.tensor_copy(self.pT[u % 2][:, h:kt, :].rearrange("p a b -> p (a b)"),
                                          ps[:, 5, 0:(kt - h) * P]).then_inc(self.kept_hi, 1)

                def divide(u):
                    t = self.units[u][1]
                    n = i * self.U + u
                    dve.wait_ge(self.valued, n + 1)
                    s = self.rowsum[:, u % 2]
                    if more_sum:
                        chain.link(nc.vector.tensor_tensor(s[:, 0:1], s[:, 0:1], s[:, 2:3], ALU.add))
                    chain.link(nc.vector.reciprocal(s[:, 1:2], s[:, 0:1]))
                    hh = self.units[u][0]
                    if u == 0:
                        dve.wait_ge(self.o_turned, i)
                    nc.vector.tensor_scalar(self.osb[:, self.tiles.index(t), hh * self.dv:(hh + 1) * self.dv],
                                            ps[:, 6 + u % 2, 0:self.dv], s[:, 1:2], None,
                                            ALU.mult).then_inc(self.divided, 1)

                def maxima(u):
                    hh, t = self.units[u]
                    n = i * self.U + u
                    dve.wait_ge(self.scored, n + 1)
                    dve.wait_ge(self.exped, n - 1 if u >= 1 else n)
                    maximum(hh, t, 2 * (u % 2), u % 2).then_inc(self.maxed, 1)

                maxima(0)
                for u in range(self.U):
                    if u + 1 < self.U:
                        maxima(u + 1)
                    keep_hi(u)
                    divide(u)

            def act_units(self, act, i, source, oT, more_exp=None):
                def exponentials(u):
                    hh, t = self.units[u]
                    n = i * self.U + u
                    act.wait_ge(self.maxed, n + 1)
                    act.wait_ge(self.divided, n - 1 if u >= 1 else n)
                    if more_exp:
                        more_exp(hh, u % 2)
                    src = source(t, 2 * (u % 2), u % 2)
                    nc.scalar.activation(self.pexp[u % 2][:, 0:src.shape[1]], src, ACT.Exp, bias=self.rowmax[:, u % 2, 3:4],
                                         accum_out=self.rowsum[:, u % 2, 0:1]).then_inc(self.exped, 1)

                def keep_lo(u):
                    t = self.units[u][1]
                    n = i * self.U + u
                    kt = len(self.key_tiles(t))
                    act.wait_ge(self.turned, n + 1)
                    act.wait_ge(self.valued, n - 1 if u >= 1 else n)
                    h = (kt + 1) // 2
                    nc.scalar.copy(self.pT[u % 2][:, 0:h, :].rearrange("p a b -> p (a b)"),
                                   ps[:, 4, 0:h * P]).then_inc(self.kept_lo, 1)

                exponentials(0)
                for u in range(self.U):
                    if u + 1 < self.U:
                        exponentials(u + 1)
                    keep_lo(u)
                act.wait_ge(self.o_turned, i + 1)
                w = min(len(self.tiles), NL) * P
                last = nc.scalar.copy(oT[:, ds(i, 1), 0:w], ps[:, 4:5, 0:w])
                if len(self.tiles) > NL:
                    last = nc.scalar.copy(oT[:, ds(i, 1), w:T], ps[:, 5:6, 0:T - w])
                last.then_inc(self.o_kept, 1)

        def neighbourhood(l, proj, stat, oT, last_layer):
            nq = NL if last_layer else NT
            keys_of = lambda t: list(range(NT)) if t < NL else list(range(NL, NT))
            with Scope() as st:
                a = Attention(st, "na", 2, NA_DIM, list(range(nq)), keys_of)
                zrow = sb(st, "rpb_rows", [NA_HEADS * 15, RPBW])
                bias = sb(st, "rpb_spread", [P, NA_HEADS, 14 * GRID_W])
                colmask = sb(st, "colmask", [P, GRID_W])
                bst = sb(st, "bias", [P, 2, 14, GRID_W])
                qst, kst = sb(st, "na_q", [P, nq, 2, 64]), sb(st, "na_k", [P, NT, 2, 64])
                qT, kT = sb(st, "na_qT", [P, T]), sb(st, "na_kT", [P, T])
                score = [sb(st, f"na_scores{s}", [P, T]) for s in range(2)]
                gain = sb(st, "na_gain", [P, 2])
                zeroed, rl, bl, gl, based, gained = (sem(st, q) for q in ("rpb_zeroed", "rpb_loaded", "bias_loaded", "gain_loaded", "bias_ready", "gain_ready"))
                block = st.enter_context(nc.Block())
                U = a.U

                @block.sync
                def _(sp):
                    for n, g in enumerate((na_q_g, na_k_g)):
                        for h in range(2):
                            sp.dma_start(gain[h * 64:(h + 1) * 64, n:n + 1], g[l].rearrange("(d o) -> d o", o=1)).then_inc(gl, 16)
                    sp.dma_start(colmask[:], const["colmask"]).then_inc(bl, 16)
                    sp.wait_ge(zeroed, 1)
                    sp.dma_start(zrow[:, 48:79], na_rpb[l].rearrange("h r c -> (h r) c")).then_inc(rl, 16)
                    sp.wait_ge(rl, 16)
                    sp.dma_start(rpb_pad.rearrange("q r c -> r q c"), zrow[:].unsqueeze(1).to_broadcast([NA_HEADS * 15, GRID_W, RPBW])).then_inc(rl, 16)
                    sp.wait_ge(rl, 32)
                    for h in range(NA_HEADS):
                        for par in range(2):
                            src = bass.AP(tensor=rpb_pad.tensor, offset=(h * 15 + 1 - par) * RPBW + GRID_W - 1,
                                          ap=[[RPBW * 15 * NA_HEADS - 1, GRID_W], [RPBW, 14], [1, GRID_W]])
                            sp.dma_start(bias[par * 64:(par + 1) * 64, h, :].rearrange("p (j k) -> p j k", k=GRID_W), src).then_inc(bl, 16)
                    sp.wait_ge(bl, 16 + 32 * NA_HEADS)

                @block.gpsimd
                def _(pool):
                    nc.gpsimd.memset(zrow[:], 0.0).then_inc(zeroed, 1)
                    pool.wait_ge(bl, 16 + 32 * NA_HEADS)
                    with pool.Fori(0, NA_HEADS // 2) as i:
                        pool.wait_ge(a.maxed, i * U)
                        for h in range(2):
                            last = nc.gpsimd.tensor_tensor(bst[:, h], bias[:, ds(2 * i + h, 1), :].rearrange("p o (j k) -> p (o j) k", k=GRID_W),
                                                           colmask[:].unsqueeze(1).to_broadcast([P, 14, GRID_W]), ALU.add)
                        last.then_inc(based, 1)

                @block.tensor
                def _(pe):
                    with pe.Fori(0, NA_HEADS // 2) as i:
                        pe.wait_ge(a.kept_lo, i * U)
                        pe.wait_ge(a.kept_hi, i * U)
                        pe.wait_ge(a.o_kept, i)
                        for n, (x, bank) in enumerate(((qst, 4), (kst, 6))):
                            pe.wait_ge(a.staged, 2 * i + n + 1)
                            for t in range(x.shape[1]):
                                o = ps[:, bank, t * P:(t + 1) * P] if t < NL else ps[:, bank + 1, (t - NL) * P:(t - NL + 1) * P]
                                mm = nc.tensor.transpose(o, x[:, t].rearrange("p h d -> p (h d)"), ident[:])
                            mm.then_inc(a.q_turned, 1)
                        pe.wait_ge(a.qk_kept, 2 * i + 2)

                        def scores(hh, t, bank):
                            r = slice(hh * 64, (hh + 1) * 64)
                            if t < NL:
                                nc.tensor.matmul(ps[:, bank, 0:S], qT[r, t * P:(t + 1) * P], kT[r, 0:S], start=True, stop=True)
                            return nc.tensor.matmul(ps[:, bank + 1, 0:L], qT[r, t * P:(t + 1) * P], kT[r, S:T], start=True, stop=True)

                        a.pe_units(pe, i, scores, lambda hh, k: proj[:, k, ds(C_NAV + (2 * i + hh) * 64, 64)])

                @block.vector
                def _(dve):
                    dve.wait_ge(gl, 64)
                    nc.vector.tensor_scalar(gain[:, 0:1], gain[:, 0:1], NA_DIM ** -0.5, None, ALU.mult).then_inc(gained, 1)
                    STEPS = 2 * NL + a.U
                    with dve.Fori(0, NA_HEADS // 2) as i:
                        chain = Chain(dve, a.chain, i * STEPS)
                        dve.wait_ge(a.q_turned, 2 * i)
                        for n, (x, nt) in enumerate(((qst, nq), (kst, NT))):
                            nc.vector.tensor_tensor(x[:].rearrange("p t h d -> p t h d"),
                                                    proj[:, 0:nt, ds(n * NA_W + i * P, P)].rearrange("p t (h d) -> p t h d", d=64),
                                                    stat[:, 0:nt, ds(R_NA + 6 * n + 2 * i, 2)].unsqueeze(3).to_broadcast([P, nt, 2, 64]),
                                                    ALU.mult).then_inc(a.staged, 1)
                        dve.wait_ge(based, i + 1)

                        def maximum(hh, t, bank, s):
                            m = a.rowmax[:, s]
                            if t >= NL:
                                return nc.vector.tensor_reduce(m[:, 3:4], ps[:, bank + 1, 0:L], AX.X, ALU.max, negate=True)
                            j0 = 6 - 2 * t
                            nc.vector.tensor_scalar(score[s][:, S:T], ps[:, bank + 1, 0:L], 0.0, 3 * MASKED,
                                                    ALU.add, ALU.max, accum_out=m[:, 0:1])
                            chain.link(nc.vector.tensor_tensor_reduce(
                                score[s][:, 0:S], ps[:, bank, 0:S], bst[:, hh, j0:j0 + 8, :].rearrange("p j k -> p (j k)"),
                                1.0, 3 * MASKED, ALU.add, ALU.max, m[:, 1:2]))
                            return nc.vector.tensor_reduce(m[:, 3:4], m[:, 0:2], AX.X, ALU.max, negate=True)

                        a.dve_units(dve, i, chain, maximum)
                        assert chain.n == STEPS, chain.n

                @block.scalar
                def _(act):
                    act.wait_ge(gained, 1)
                    with act.Fori(0, NA_HEADS // 2) as i:
                        for n, (xT_, bank, w) in enumerate(((qT, 4, nq * P), (kT, 6, T))):
                            act.wait_ge(a.q_turned, 2 * i + n + 1)
                            last = nc.scalar.mul(xT_[:, 0:S], ps[:, bank, 0:S], gain[:, n:n + 1])
                            if w > S:
                                last = nc.scalar.mul(xT_[:, S:T], ps[:, bank + 1, 0:L], gain[:, n:n + 1])
                            last.then_inc(a.qk_kept, 1)
                        a.act_units(act, i, lambda t, bank, s: score[s][:] if t < NL else ps[:, bank + 1, 0:L], oT)

        def windowed(l, proj, stat, oT, last_layer):
            nq = NL if last_layer else NT
            G = SWA_HEADS // SWA_KV_HEADS
            near = lambda t: list(range(max(t - 1, 0), min(t + 2, NL)))
            keys_of = lambda t: (near(t) if t < NL else []) + list(range(NL, NT))
            with Scope() as st:
                a = Attention(st, "sw", 2, SWA_DIM, list(range(nq)), keys_of)
                band = sb(st, "band", [P, 3 * P])
                cg, sg = [sb(st, f"sw_cos{n}", [P, NT, 64]) for n in range(2)], [sb(st, f"sw_sin{n}", [P, NT, 64]) for n in range(2)]
                g = [sb(st, f"sw_gain{n}", [P, 64]) for n in range(2)]
                sink, sink2 = sb(st, "sink", [P, SWA_HEADS]), sb(st, "sink_pair", [P, 2])
                raw, part, turn = (sb(st, f"sw_{q}", [P, NT, 2, 64]) for q in ("raw", "part", "roped"))
                qT, kT = sb(st, "sw_qT", [P, T]), sb(st, "sw_kT", [P, T])
                score = [sb(st, f"sw_scores{s}", [P, T]) for s in range(2)]
                gl = sem(st, "sw_consts_loaded")
                block = st.enter_context(nc.Block())
                U = a.U

                @block.sync
                def _(sp):
                    sp.dma_start(band[:], const["band"]).then_inc(gl, 16)
                    for n, v in enumerate((swa_q_g, swa_k_g)):
                        sp.dma_start(g[n][:], v[l:l + 1, :].to_broadcast([P, 64])).then_inc(gl, 16)
                    sp.dma_start(sink[:], swa_sink[l:l + 1, :].to_broadcast([P, SWA_HEADS])).then_inc(gl, 16)
                    sp.wait_ge(gl, 64)

                def turned(pe, nt):
                    for t in range(nt):
                        o = ps[:, 4, t * P:(t + 1) * P] if t < NL else ps[:, 5, (t - NL) * P:(t - NL + 1) * P]
                        mm = nc.tensor.transpose(o, turn[:, t].rearrange("p h d -> p (h d)"), ident[:])
                    mm.then_inc(a.q_turned, 1)

                @block.tensor
                def _(pe):
                    pe.wait_ge(a.staged, 1)
                    turned(pe, NT)
                    pe.wait_ge(a.qk_kept, 1)
                    with pe.Fori(0, G) as i:
                        pe.wait_ge(a.kept_lo, i * U)
                        pe.wait_ge(a.kept_hi, i * U)
                        pe.wait_ge(a.o_kept, i)
                        pe.wait_ge(a.staged, i + 2)
                        turned(pe, nq)
                        pe.wait_ge(a.qk_kept, i + 2)

                        def scores(hh, t, bank):
                            r = slice(hh * 64, (hh + 1) * 64)
                            if t < NL:
                                k = near(t)
                                nc.tensor.matmul(ps[:, bank, 0:len(k) * P], qT[r, t * P:(t + 1) * P],
                                                 kT[r, k[0] * P:(k[-1] + 1) * P], start=True, stop=True)
                            return nc.tensor.matmul(ps[:, bank + 1, 0:L], qT[r, t * P:(t + 1) * P], kT[r, S:T], start=True, stop=True)

                        a.pe_units(pe, i, scores, lambda hh, k: proj[:, k, C_SV + hh * 64:C_SV + (hh + 1) * 64])

                @block.vector
                def _(dve):
                    pre = Chain(dve, gl, 64)
                    dve.wait_ge(gl, 64)
                    rope_tables(pre, cg[0], sg[0], g[0], SWA_DIM ** -0.5)
                    rope_tables(pre, cg[1], sg[1], g[1], 1.0)
                    pre.link(nc.vector.tensor_tensor(raw[:], proj[:, :, C_SK:C_SV].rearrange("p t (h d) -> p t h d", d=64),
                                                     stat[:, :, R_SW + 6:R_SW + 8].unsqueeze(3).to_broadcast([P, NT, 2, 64]), ALU.mult))
                    rope(pre, turn[:], raw[:], part[:], cg[1], sg[1], NT, 2).then_inc(a.staged, 1)
                    STEPS = 2 + 3 * a.U
                    with dve.Fori(0, G) as i:
                        chain = Chain(dve, a.chain, i * STEPS)
                        q = proj[:, 0:nq, C_SQ:C_SK].rearrange("p t (g j) -> p t g j", g=2)
                        r = stat[:, 0:nq, R_SW:R_SW + 6].rearrange("p t (g j) -> p t g j", g=2)
                        nc.vector.tensor_copy(sink2[:], sink[:].rearrange("p (g j) -> p g j", g=2)[:, :, ds(i, 1)].rearrange("p g j -> p (g j)"))
                        chain.link(nc.vector.tensor_tensor(raw[:, 0:nq], q[:, :, :, ds(i * 64, 64)],
                                                           r[:, :, :, ds(i, 1)].to_broadcast([P, nq, 2, 64]), ALU.mult))
                        dve.wait_ge(a.q_turned, i + 1)
                        rope(chain, turn[:, 0:nq], raw[:, 0:nq], part[:, 0:nq], cg[0], sg[0], nq, 2).then_inc(a.staged, 1)

                        def maximum(hh, t, bank, s):
                            m = a.rowmax[:, s]
                            k = near(t) if t < NL else []
                            n = len(k) * P
                            last = nc.vector.tensor_scalar(score[s][:, n:n + L], ps[:, bank + 1, 0:L], 0.0, sink2[:, hh:hh + 1],
                                                           ALU.add, ALU.max, accum_out=m[:, 0:1])
                            if k:
                                b0 = (k[0] - t + 1) * P
                                last = nc.vector.tensor_tensor_reduce(score[s][:, 0:n], ps[:, bank, 0:n], band[:, b0:b0 + n],
                                                                      1.0, 3 * MASKED, ALU.add, ALU.max, m[:, 1:2])
                            chain.link(last)
                            return nc.vector.tensor_reduce(m[:, 3:4], m[:, 0:2 if k else 1], AX.X, ALU.max, negate=True)

                        a.dve_units(dve, i, chain, maximum, True)
                        assert chain.n == STEPS, (chain.n, STEPS)

                @block.scalar
                def _(act):
                    act.wait_ge(a.q_turned, 1)
                    nc.scalar.copy(kT[:, 0:S], ps[:, 4, 0:S])
                    nc.scalar.copy(kT[:, S:T], ps[:, 5, 0:L]).then_inc(a.qk_kept, 1)
                    with act.Fori(0, G) as i:
                        act.wait_ge(a.q_turned, i + 2)
                        last = nc.scalar.copy(qT[:, 0:S], ps[:, 4, 0:S])
                        if nq > NL:
                            last = nc.scalar.copy(qT[:, S:T], ps[:, 5, 0:L])
                        last.then_inc(a.qk_kept, 1)

                        def sink_exp(hh, s):
                            nc.scalar.activation(a.rowsum[:, s, 2:3], sink2[:, hh:hh + 1], ACT.Exp, bias=a.rowmax[:, s, 3:4])

                        a.act_units(act, i, lambda t, bank, s: score[s][:, 0:len(keys_of(t)) * P], oT, sink_exp)

        def latent(l, proj, stat, oT, last_layer):
            nq = NL if last_layer else NT
            keys_of = lambda t: (list(range(NL)) if t < NL else []) + list(range(NL, NT))
            QC = MLA_Q_RANK // P
            with Scope() as st:
                a = Attention(st, "mla", 1, MLA_V, list(range(nq)), keys_of)
                wuq, wukv = sb(st, "w_uq", [P, QC, MLA_HEADS * MLA_QK]), sb(st, "w_ukv", [P, MLA_HEADS * 256])
                cg, sg = [sb(st, f"mla_cos{n}", [P, NT, 64]) for n in range(2)], [sb(st, f"mla_sin{n}", [P, NT, 64]) for n in range(2)]
                g = [sb(st, f"mla_gain{n}", [P, 64]) for n in range(2)]
                gain = sb(st, "mla_gains", [P, 2 + QC + 1])
                shared = sb(st, "mla_shared", [P, max(NT * (QC + 1) * P, (NT + nq) * MLA_QK)])
                rank = shared[:, 0:NT * (QC + 1) * P].rearrange("p (t w) -> p t w", t=NT)
                sq = shared[:, 0:NT * MLA_QK].rearrange("p (t w) -> p t w", t=NT)
                qst = shared[:, NT * MLA_QK:(NT + nq) * MLA_QK].rearrange("p (t w) -> p t w", t=nq)
                cT_ = sb(st, "rank_T", [P, QC + 1, T])
                krope = sb(st, "k_roped", [P, NT, 1, 64])
                kst, vst = sb(st, "mla_k", [P, NT, P]), sb(st, "mla_v", [P, NT, P])
                part, kr = sq[:, :, 0:64].unsqueeze(2), sq[:, :, P:MLA_QK]
                r2 = sb(st, "mla_rstd", [P, 2, NT])
                qr = sb(st, "mla_q_rope", [P, nq, 1, 64])
                qT, kT = sb(st, "mla_qT", [P, T]), sb(st, "mla_kT", [P, T])
                qrT, krT = sb(st, "mla_qrT", [64, T]), sb(st, "mla_krT", [64, T])
                gl, wl, rt, root, upped, unpacked = (sem(st, q) for q in ("mla_consts_loaded", "w_u_loaded", "ranks_turned", "mla_root", "upped", "unpacked"))
                rk = [sem(st, "ranks_kept_act"), sem(st, "ranks_kept_dve")]
                kept_k = sem(st, "k_kept")
                block = st.enter_context(nc.Block())
                U = a.U
                ctx_kept = lambda q: sum(1 for c in range(q + 1) if c == QC or nq > NL)

                @block.sync
                def _(sp):
                    col = lambda v: v.rearrange("(d o) -> d o", o=1)
                    sp.dma_start(gain[:, 0:1], col(mla_q_g[l, 0:P])).then_inc(gl, 16)
                    sp.dma_start(gain[:, 1:2], col(mla_k_g[l, 0:P])).then_inc(gl, 16)
                    for q in range(QC):
                        sp.dma_start(gain[:, 2 + q:3 + q], col(mla_q_norm[l, q * P:(q + 1) * P])).then_inc(gl, 16)
                    sp.dma_start(gain[:, 2 + QC:3 + QC], col(mla_kv_norm[l])).then_inc(gl, 16)
                    for n, v in enumerate((mla_q_g, mla_k_g)):
                        sp.dma_start(g[n][:], v[l:l + 1, P:MLA_QK].to_broadcast([P, 64])).then_inc(gl, 16)
                    sp.dma_start(wuq[:], mla_w_uq[l].rearrange("(k p) n -> p k n", p=P)).then_inc(wl, 16)
                    sp.dma_start(wukv[:], mla_w_ukv[l]).then_inc(wl, 16)
                    sp.wait_ge(gl, 16 * (5 + QC))

                @block.tensor
                def _(pe):
                    pe.wait_ge(a.staged, 1)
                    for q in range(QC + 1):
                        b = 2 * (q % 2)
                        if q >= 2:
                            pe.wait_ge(rk[0], q - 1)
                            if ctx_kept(q - 2):
                                pe.wait_ge(rk[1], ctx_kept(q - 2))
                        for t in range(nq if q < QC else NT):
                            mm = nc.tensor.transpose(ps[:, b + t // NL, (t % NL) * P:(t % NL + 1) * P],
                                                     rank[:, t, q * P:(q + 1) * P], ident[:])
                        mm.then_inc(rt, 1)
                    pe.wait_ge(wl, 32)
                    pe.wait_ge(rk[0], QC + 1)
                    pe.wait_ge(rk[1], ctx_kept(QC))
                    with pe.Fori(0, MLA_HEADS) as i:
                        pe.wait_ge(a.exped, i * U)
                        pe.wait_ge(a.kept_lo, i * U)
                        pe.wait_ge(a.kept_hi, i * U)
                        pe.wait_ge(a.o_kept, i)
                        for t in range(nq):
                            for q in range(QC):
                                mm = nc.tensor.matmul(ps[:, t // 2, (t % 2) * MLA_QK:(t % 2 + 1) * MLA_QK],
                                                      cT_[:, q, t * P:(t + 1) * P], wuq[:, q, ds(i * MLA_QK, MLA_QK)],
                                                      start=(q == 0), stop=(q == QC - 1))
                        mm.then_inc(upped, 1)
                        for t in range(NT):
                            mm = nc.tensor.matmul(ps[:, 3 + t // 2, (t % 2) * 256:(t % 2 + 1) * 256],
                                                  cT_[:, QC, t * P:(t + 1) * P], wukv[:, ds(i * 256, 256)], start=True, stop=True)
                        mm.then_inc(upped, 1)
                        pe.wait_ge(unpacked, 2 * i + 2)
                        for n, (x, bank) in enumerate(((qst[:, :, 0:P], 4), (kst[:], 6), (qr[:, :, 0, :], 0), (kr, 2))):
                            if n < 2:
                                pe.wait_ge(a.staged, 4 * i + (2, 5)[n])
                            w = x.shape[2]
                            for t in range(x.shape[1]):
                                mm = nc.tensor.transpose(ps[0:w, bank + t // NL, (t % NL) * P:(t % NL + 1) * P], x[:, t, :], ident[:])
                            mm.then_inc(a.q_turned, 1)
                        pe.wait_ge(a.qk_kept, 2 * i + 2)
                        pe.wait_ge(kept_k, 2 * i + 2)

                        def scores(hh, t, bank):
                            q0 = slice(t * P, (t + 1) * P)
                            for b, c0, n in ([(bank, 0, S)] if t < NL else []) + [(bank + 1, S, L)]:
                                nc.tensor.matmul(ps[:, b, 0:n], qT[:, q0], kT[:, c0:c0 + n], start=True, stop=False)
                                mm = nc.tensor.matmul(ps[:, b, 0:n], qrT[:, q0], krT[:, c0:c0 + n], start=False, stop=True)
                            return mm

                        a.pe_units(pe, i, scores, lambda hh, k: vst[:, k, :])

                @block.vector
                def _(dve):
                    pre = Chain(dve, gl, 16 * (5 + QC))
                    dve.wait_ge(gl, 16 * (5 + QC))
                    pre.link(nc.vector.tensor_scalar(gain[:, 0:1], gain[:, 0:1], MLA_QK ** -0.5, None, ALU.mult))
                    rope_tables(pre, cg[0], sg[0], g[0], MLA_QK ** -0.5)
                    rope_tables(pre, cg[1], sg[1], g[1], 1.0)
                    for t in range(NT):
                        if t < nq:
                            nc.vector.tensor_scalar(rank[:, t, 0:QC * P], proj[:, t, C_CQ:C_CKV], stat[:, t, R_CQ:R_CQ + 1], None, ALU.mult)
                        last = nc.vector.tensor_scalar(rank[:, t, QC * P:], proj[:, t, C_CKV:C_KR], stat[:, t, R_CKV:R_CKV + 1], None, ALU.mult)
                    last.then_inc(a.staged, 1)
                    rope(pre, krope[:], proj[:, :, C_KR:C_SQ].rearrange("p t (o d) -> p t o d", o=1), vst[:, :, 0:64].unsqueeze(2), cg[1], sg[1], NT, 1)\
                        .then_inc(gl, 1)
                    pre.n += 1
                    for q in range(QC + 1):
                        dve.wait_ge(rt, q + 1)
                        b = 2 * (q % 2)
                        if q == QC or nq > NL:
                            nc.vector.tensor_scalar(cT_[:, q, S:T], ps[:, b + 1, 0:L], gain[:, 2 + q:3 + q], None, ALU.mult).then_inc(rk[1], 1)
                    dve.wait_ge(gl, 16 * (5 + QC) + pre.n)
                    dve.wait_ge(rk[1], ctx_kept(QC))
                    STEPS = 7 + a.U
                    with dve.Fori(0, MLA_HEADS) as i:
                        chain = Chain(dve, a.chain, i * STEPS)
                        dve.wait_ge(upped, 2 * i + 2)
                        for b in range(3):
                            kv = ps[:, 3 + b, :].rearrange("p (t w) -> p t w", w=256)
                            nc.vector.tensor_copy(kst[:, 2 * b:2 * b + 2, :], kv[:, :, 0:P])
                            last = nc.vector.tensor_copy(vst[:, 2 * b:2 * b + 2, :], kv[:, :, P:256])
                        last.then_inc(unpacked, 1)
                        chain.link(nc.vector.tensor_copy(r2[:, 0], stat[:, :, 0]))
                        dve.wait_ge(unpacked, 2 * i + 2)
                        chain.link(nc.vector.tensor_tensor(sq[:, 0:nq, :], qst, qst, ALU.mult))
                        chain.link(nc.vector.tensor_reduce(r2[:, 0, 0:nq], sq[:, 0:nq, :], AX.X, ALU.add))
                        chain.link(nc.vector.tensor_tensor(sq[:, :, 0:P], kst[:], kst[:], ALU.mult))
                        chain.link(nc.vector.tensor_reduce(r2[:, 1], sq[:, :, 0:P], AX.X, ALU.add))
                        chain.link(nc.vector.tensor_tensor(r2[:, 1], r2[:, 1], stat[:, :, R_KR], ALU.add))
                        nc.vector.tensor_scalar(r2[:], r2[:], 1.0 / MLA_QK, EPS, ALU.mult, ALU.add).then_inc(root, 1)
                        dve.wait_ge(root, 3 * i + 2)
                        nc.vector.reciprocal(r2[:], r2[:]).then_inc(root, 1)
                        dve.wait_ge(root, 3 * i + 3)
                        nc.vector.tensor_tensor(kst[:], kst[:], r2[:, 1].unsqueeze(2).to_broadcast([P, NT, P]), ALU.mult)
                        nc.vector.tensor_tensor(kr, krope[:, :, 0, :], r2[:, 1].unsqueeze(2).to_broadcast([P, NT, 64]), ALU.mult)
                        nc.vector.tensor_tensor(qst, qst, r2[:, 0, 0:nq].unsqueeze(2).to_broadcast([P, nq, MLA_QK]), ALU.mult).then_inc(a.staged, 1)
                        dve.wait_ge(a.staged, 4 * i + 2)
                        rope(chain, qr[:], qst[:, :, P:MLA_QK].unsqueeze(2), part[:, 0:nq], cg[0], sg[0], nq, 1).then_inc(a.staged, 3)
                        for n, (w, x_, bank) in enumerate(((P, kT, 6), (64, krT, 2))):
                            dve.wait_ge(a.q_turned, 4 * i + 2 * n + 2)
                            for c0, m, b in ((0, S, bank), (S, L, bank + 1)):
                                if n == 0:
                                    last = nc.vector.tensor_scalar(x_[:, c0:c0 + m], ps[:, b, 0:m], gain[:, 1:2], None, ALU.mult)
                                else:
                                    last = nc.vector.tensor_copy(x_[:, c0:c0 + m], ps[0:w, b, 0:m])
                            last.then_inc(kept_k, 1)

                        def maximum(hh, t, bank, s):
                            src = ps[:, bank:bank + 2, :].rearrange("p a b -> p (a b)")[:, 0:T] if t < NL else ps[:, bank + 1, 0:L]
                            return nc.vector.tensor_reduce(a.rowmax[:, s, 3:4], src, AX.X, ALU.max, negate=True)

                        a.dve_units(dve, i, chain, maximum)
                        assert chain.n == STEPS, chain.n

                @block.scalar
                def _(act):
                    for q in range(QC + 1):
                        act.wait_ge(rt, q + 1)
                        if q == 0:
                            act.wait_ge(gl, 16 * (5 + QC))
                        nc.scalar.mul(cT_[:, q, 0:S], ps[:, 2 * (q % 2), 0:S], gain[:, 2 + q:3 + q]).then_inc(rk[0], 1)
                    with act.Fori(0, MLA_HEADS) as i:
                        act.wait_ge(upped, 2 * i + 1)
                        for b in range(nq // 2):
                            last = nc.scalar.copy(qst[:, 2 * b:2 * b + 2, :], ps[:, b, 0:2 * MLA_QK].rearrange("p (t w) -> p t w", w=MLA_QK))
                        last.then_inc(unpacked, 1)
                        act.wait_ge(root, 3 * i + 1)
                        nc.scalar.activation(r2[:], r2[:], ACT.Sqrt).then_inc(root, 1)
                        for n, (w, x_, bank) in enumerate(((P, qT, 4), (64, qrT, 0))):
                            act.wait_ge(a.q_turned, 4 * i + 2 * n + 1)
                            for c0, m, b in ((0, S, bank), (S, L, bank + 1))[:1 if nq == NL else 2]:
                                if n == 0:
                                    last = nc.scalar.mul(x_[:, c0:c0 + m], ps[:, b, 0:m], gain[:, 0:1])
                                else:
                                    last = nc.scalar.copy(x_[:, c0:c0 + m], ps[0:w, b, 0:m])
                            last.then_inc(a.qk_kept, 1)
                        a.act_units(act, i, lambda t, bank, s: ps[:, bank:bank + 2, :].rearrange("p a b -> p (a b)")[:, 0:T]
                                    if t < NL else ps[:, bank + 1, 0:L], oT)

        def merge(l, hT, oT, mT, ctx_too):
            W = T if ctx_too else S
            CW = 256
            rows = ((w_na_o, 0, 3), (w_mla_o, 6, 4), (w_swa_o, 3, 3))
            with Scope() as st:
                wg = [sb(st, f"w_gate_logits{s}", [P, 3, KD, CW]) for s in range(2)]
                wy = [sb(st, f"w_branch{s}", [P, 10, CW]) for s in range(2)]
                sig = [sb(st, f"gate{s}", [P, W]) for s in range(2)]
                prod = sb(st, "gated", [P, W])
                wl = [sem(st, f"w_merge_loaded{s}") for s in range(2)]
                logits, ys, sigs, gated, ch = (sem(st, q) for q in ("logits", "branch_out", "gates", "gated", "merge_chain"))
                block = st.enter_context(nc.Block())
                LOADS = 7
                UN = 2 * 2 * 3
                units = [(s, dc, b) for s in range(2) for dc in range(2) for b in range(3)]

                @block.sync
                def _(sp):
                    def load(s, c0):
                        for b in range(3):
                            sp.dma_start(wg[s][:, b], w_in[l].rearrange("(k p) n -> p k n", p=P)[:, :, ds(C_GL + b * D + c0, CW)]).then_inc(wl[s], 16)
                        for w, q0, nq in rows[:2]:
                            sp.dma_start(wy[s][:, q0:q0 + nq], w[l].rearrange("(k p) n -> p k n", p=P)[:, :, ds(c0, CW)]).then_inc(wl[s], 16)
                        for g in range(2):
                            sp.dma_start(wy[s][g * 64:(g + 1) * 64, 3:6],
                                         w_swa_o[l].rearrange("(g j d) n -> g d j n", g=2, d=64)[g][:, :, ds(c0, CW)]).then_inc(wl[s], 16)
                    for s in range(2):
                        load(s, s * CW)
                    with sp.Fori(0, D // CW // 2 - 1) as i:
                        for s in range(2):
                            sp.wait_ge(ys, i * UN + 6 * (s + 1))
                            load(s, (2 * i + 2 + s) * CW)

                @block.tensor
                def _(pe):
                    with pe.Fori(0, D // CW // 2) as i:
                        for u, (s, dc, b) in enumerate(units):
                            if u % 6 == 0:
                                pe.wait_ge(wl[s], 16 * LOADS * i + 16 * LOADS)
                            pe.wait_ge(gated, i * UN + u - 1 if u >= 1 else i * UN)
                            b0 = 4 * (u % 2)
                            for z, t0, m in streams(ctx_too):
                                for k in range(KD):
                                    mm = nc.tensor.matmul(ps[:, b0 + z, 0:m], wg[s][:, b, k, dc * P:(dc + 1) * P], hT[:, k, t0:t0 + m],
                                                          start=(k == 0), stop=(k == KD - 1))
                            mm.then_inc(logits, 1)
                            _, q0, n = rows[b]
                            for z, t0, m in streams(ctx_too):
                                for q in range(n):
                                    mm = nc.tensor.matmul(ps[:, b0 + 2 + z, 0:m], wy[s][:, q0 + q, dc * P:(dc + 1) * P], oT[:, q0 + q, t0:t0 + m],
                                                          start=(q == 0), stop=(q == n - 1))
                            mm.then_inc(ys, 1)

                @block.scalar
                def _(act):
                    with act.Fori(0, D // CW // 2) as i:
                        for u in range(UN):
                            act.wait_ge(logits, i * UN + u + 1)
                            act.wait_ge(gated, i * UN + u - 1 if u >= 1 else i * UN)
                            for z, t0, m in streams(ctx_too):
                                last = nc.scalar.activation(sig[u % 2][:, t0:t0 + m], ps[:, 4 * (u % 2) + z, 0:m], ACT.Sigmoid)
                            last.then_inc(sigs, 1)

                @block.vector
                def _(dve):
                    STEPS = 8
                    with dve.Fori(0, D // CW // 2) as i:
                        chain = Chain(dve, ch, i * STEPS)
                        for u, (s, dc, b) in enumerate(units):
                            dve.wait_ge(sigs, i * UN + u + 1)
                            dve.wait_ge(ys, i * UN + u + 1)
                            m_ = mT[:, ds((2 * i + s) * 2 + dc, 1), :].rearrange("p o t -> p (o t)")
                            if b > 0:
                                dve.wait_ge(gated, i * UN + u)
                            for z, t0, m in streams(ctx_too):
                                last = nc.vector.tensor_tensor(m_[:, t0:t0 + m] if b == 0 else prod[:, t0:t0 + m], sig[u % 2][:, t0:t0 + m],
                                                               ps[:, 4 * (u % 2) + 2 + z, 0:m], ALU.mult)
                            if b > 0:
                                chain.link(last)
                                last = nc.vector.tensor_tensor(m_[:, 0:W], m_[:, 0:W], prod[:], ALU.add)
                            last.then_inc(gated, 1)
                        assert chain.n == STEPS

        def output_projection(l, mT, ctx_too):
            with Scope() as st:
                w = sb(st, "w_o", [P, KD, D])
                wl, mm_done, added = sem(st, "w_o_loaded"), sem(st, "w_o_mm"), sem(st, "w_o_added")
                block = st.enter_context(nc.Block())

                @block.sync
                def _(sp):
                    sp.dma_start(w[:], w_o[l].rearrange("(k p) n -> p k n", p=P)).then_inc(wl, 16)
                    sp.wait_ge(wl, 16)

                @block.tensor
                def _(pe):
                    pe.wait_ge(wl, 16)
                    for d in range(KD):
                        if d >= 2:
                            pe.wait_ge(added, d - 1)
                        for z, t0, m in streams(ctx_too):
                            for k in range(KD):
                                mm = nc.tensor.matmul(ps[:, 2 * (d % 2) + z, 0:m], w[:, k, d * P:(d + 1) * P], mT[:, k, t0:t0 + m],
                                                      start=(k == 0), stop=(k == KD - 1))
                        mm.then_inc(mm_done, 1)

                @block.vector
                def _(dve):
                    for d in range(KD):
                        dve.wait_ge(mm_done, d + 1)
                        for z, t0, m in streams(ctx_too):
                            last = nc.vector.scalar_tensor_tensor(xT[:, d, t0:t0 + m], ps[:, 2 * (d % 2) + z, 0:m],
                                                                  modT[:, 2 * KD + d, z:z + 1], xT[:, d, t0:t0 + m], ALU.mult, ALU.add)
                        last.then_inc(added, 1)

        def route(l, h2T, h2, posm, posT, affT, ctx_too):
            nt = NT if ctx_too else NL
            E = N_EXPERTS
            with Scope() as st:
                wr = sb(st, "router", [P, KD, E])
                aff = sb(st, "affinity", [P, nt, E])
                small = sb(st, "route_small", [P, 2, nt])
                left = sb(st, "left", [E, T])
                top8 = sb(st, "top8", [E, 8])
                zero = sb(st, "zero", [E, S])
                wl, lg, ch, ex, at, hk, ht, kept, pt, zs = (sem(st, q) for q in (
                    "router_loaded", "logits", "route_chain", "aff_exp", "aff_turned", "tokens_kept", "tokens_turned", "aff_kept", "pos_turned", "zeroed"))
                block = st.enter_context(nc.Block())

                @block.sync
                def _(sp):
                    sp.dma_start(wr[:], router[l].rearrange("(k p) e -> p k e", p=P)).then_inc(wl, 16)
                    sp.wait_ge(wl, 16)

                @block.gpsimd
                def _(pool):
                    nc.gpsimd.memset(zero[:], 0.0).then_inc(zs, 1)
                    nc.gpsimd.memset(posm[:], 0.0).then_inc(zs, 1)

                @block.tensor
                def _(pe):
                    pe.wait_ge(wl, 16)
                    for t in range(nt):
                        for k in range(KD):
                            mm = nc.tensor.matmul(ps[:, 0, t * E:(t + 1) * E], h2T[:, k, t * P:(t + 1) * P], wr[:, k, :],
                                                  start=(k == 0), stop=(k == KD - 1))
                    mm.then_inc(lg, 1)

                    def tokens(g):
                        if g >= 4:
                            pe.wait_ge(hk, g - 3)
                        t, half = g // 2, g % 2
                        for q in range(4):
                            k = 4 * half + q
                            mm = nc.tensor.transpose(ps[:, 2 + g % 4, q * P:(q + 1) * P], h2T[:, k, t * P:(t + 1) * P], ident[:])
                        mm.then_inc(ht, 1)
                    for g in range(4):
                        tokens(g)
                    pe.wait_ge(ex, 2)
                    for t in range(nt):
                        mm = nc.tensor.transpose(ps[0:E, 6 + t // NL, (t % NL) * P:(t % NL + 1) * P], aff[:, t, :], ident[:])
                    mm.then_inc(at, 1)
                    for g in range(4, 2 * nt):
                        tokens(g)
                    pe.wait_ge(pt, 1)
                    for t in range(nt):
                        mm = nc.tensor.transpose(ps[:, 0, t * E:(t + 1) * E], posT[:, t * P:(t + 1) * P], ident[0:E, 0:E])
                    mm.then_inc(at, 1)

                @block.scalar
                def _(act):
                    act.wait_ge(ch, 2)
                    nc.scalar.activation(aff[:], aff[:], ACT.Exp).then_inc(ex, 1)
                    for g in range(2 * nt):
                        act.wait_ge(ht, g + 1)
                        nc.scalar.copy(h2[:, g // 2, (g % 2) * 512:(g % 2 + 1) * 512], ps[:, 2 + g % 4, :]).then_inc(hk, 1)

                @block.vector
                def _(dve):
                    chain = Chain(dve, ch)
                    dve.wait_ge(lg, 1)
                    raw = ps[:, 0, 0:nt * E].rearrange("p (t e) -> p t e", e=E)
                    chain.link(nc.vector.tensor_reduce(small[:, 0], raw, AX.X, ALU.max))
                    nc.vector.tensor_tensor(aff[:], raw, small[:, 0].unsqueeze(2).to_broadcast([P, nt, E]), ALU.subtract).then_inc(ch, 1)
                    dve.wait_ge(ex, 1)
                    chain.n += 1
                    chain.link(nc.vector.tensor_reduce(small[:, 0], aff[:], AX.X, ALU.add))
                    chain.link(nc.vector.reciprocal(small[:, 1], small[:, 0]))
                    nc.vector.tensor_tensor(aff[:], aff[:], small[:, 1].unsqueeze(2).to_broadcast([P, nt, E]), ALU.mult).then_inc(ex, 1)
                    dve.wait_ge(at, 1)
                    for z, t0, m in streams(ctx_too):
                        last = nc.vector.tensor_copy(affT[:, t0:t0 + m], ps[0:E, 6 + z, 0:m])
                    chain.link(last)
                    dve.wait_ge(zs, 2)
                    for z, t0, m in streams(ctx_too):
                        cur, rest = affT[:, t0:t0 + m], left[:, t0:t0 + m]
                        chain.link(nc.vector.max(top8[:], cur))
                        chain.link(nc.vector.match_replace(rest, top8[:], cur, -1.0))
                        rounds = (KL, KC)[z] // 8 - 1
                        for _ in range(rounds):
                            chain.link(nc.vector.max(top8[:], rest))
                            chain.link(nc.vector.match_replace(rest, top8[:], rest, -1.0))
                        chain.link(nc.vector.tensor_tensor(rest, rest, cur, ALU.not_equal))
                        p_ = posT[:, t0:t0 + m]
                        chain.link(nc.vector.tensor_tensor_scan(p_, rest, zero[:, 0:m], 0.0, ALU.add, ALU.add))
                        last = nc.vector.tensor_tensor(p_, p_, rest, ALU.mult)
                        chain.link(last)
                    nc.vector.tensor_copy(small[:, 0, 0:1], small[:, 1, 0:1]).then_inc(pt, 1)
                    dve.wait_ge(at, 2)
                    nc.vector.tensor_copy(posm[:, 0:nt, 0:E], ps[:, 0, 0:nt * E].rearrange("p (t e) -> p t e", e=E))

        class Ring:
            def __init__(self, st):
                self.slot = [sb(st, f"w_expert{j}", [P, KD, 512]) for j in range(6)]
                self.loaded = [sem(st, f"w_expert_loaded{j}") for j in range(6)]

            def load(self, sp, l, m, j):
                w = (w_gate, w_up, w_gate, w_up, w_down, w_down)[j]
                half = (0, 0, 1, 1, 0, 1)[j]
                src = w[l][ds(m, 1)].rearrange("o (k p) n -> p (o k) n", p=P)[:, :, half * 512:(half + 1) * 512]
                sp.dma_start(self.slot[j][:], src).then_inc(self.loaded[j], 16)

        def experts(l, ring, h2, posm, posT, affT, ctx_too):
            E = N_EXPERTS
            M = MS if ctx_too else KL
            W = T if ctx_too else S
            zs_ = streams(ctx_too)
            KZ = (KL, KC)
            with Scope() as st:
                slots, slot_of = sb(st, "slots", [P, KL]), sb(st, "slot_of", [P, 2])
                pick = sb(st, "pick", [E, E // 2 * 2 * MS])
                sel = sb(st, "pick_pair", [E, 2 * MS])
                oh = [sb(st, f"one_hot{z}", [P, (S, L)[z] // P, 2, KZ[z]]) for z, _, _ in zs_]
                xg = sb(st, "gathered", [P, 2, KD, M])
                act_ = [sb(st, f"hidden{s}", [M, FF]) for s in range(2)]
                actT = [sb(st, f"hidden_T{s}", [P, FF // P, M]) for s in range(2)]
                Y = [sb(st, f"expert_out{z}", [2 * KZ[z], D]) for z, _, _ in zs_]
                affb = sb(st, "affinity_rows", [P, W])
                G = sb(st, "scatter", [P, W])
                names = "consts_loaded picked one_hot gathered xg_dve xg_act multiplied silued hidden turned kept_act kept_dve down y_act y_dve spread aff_copied scatter scattered added"
                s_ = {q: sem(st, "moe_" + q) for q in names.split()}
                block = st.enter_context(nc.Block())
                NP = E // 2
                NS = KD * len(zs_)

                def ungather(eng, copy, i, banks, signal):
                    for b in banks:
                        eng.wait_ge(s_["gathered"], 4 * i + b + 1)
                        src = ps[:, 4 + b, 0:4 * M].rearrange("p (d c) -> p d c", d=2)
                        for z, _, _ in zs_:
                            k, c0 = KZ[z], KL * z
                            for e in range(2):
                                last = copy(xg[:, e, 2 * b:2 * b + 2, c0:c0 + k], src[:, :, 2 * c0 + e * k:2 * c0 + (e + 1) * k])
                    last.then_inc(signal, 1)

                def keep_turned(eng, copy, i, s, bank, signal):
                    eng.wait_ge(s_["turned"], 2 * i + s + 1)
                    copy(actT[s][:, 4 * bank:4 * bank + 4, :].rearrange("p k m -> p (k m)"), ps[:, 4 + bank, 0:4 * M]).then_inc(signal, 1)

                def keep_down(eng, copy, i, s, h, signal):
                    eng.wait_ge(s_["down"], 4 * i + 2 * s + h + 1)
                    for z, _, _ in zs_:
                        k, r0 = KZ[z], KL * z
                        last = copy(Y[z][s * k:(s + 1) * k, h * 512:(h + 1) * 512], ps[r0:r0 + k, 6 + h, :])
                    last.then_inc(signal, 1)

                @block.sync
                def _(sp):
                    sp.dma_start(slots[:], const["slots"]).then_inc(s_["consts_loaded"], 16)
                    sp.dma_start(slot_of[:], const["slot_of"]).then_inc(s_["consts_loaded"], 16)
                    sp.dma_start(pick[:], const["pick"]).then_inc(s_["consts_loaded"], 16)

                    def following(i, s):
                        m = 2 * i + s
                        for j in range(6):
                            if j < 4:
                                sp.wait_ge(s_["multiplied"], 4 * m + j + 1)
                            else:
                                sp.wait_ge(s_["down"], 2 * m + j - 3)
                            ring.load(sp, l, m + 1, j)
                    with sp.Fori(0, NP - 1) as i:
                        following(i, 0)
                        following(i, 1)
                    following(NP - 1, 0)

                @block.gpsimd
                def _(pool):
                    pool.wait_ge(s_["consts_loaded"], 48)
                    with pool.Fori(0, NP) as i:
                        pool.wait_ge(s_["spread"], i)
                        nc.gpsimd.tensor_copy(sel[:], pick[:, ds(i * 2 * MS, 2 * MS)]).then_inc(s_["picked"], 1)

                @block.tensor
                def _(pe):
                    with pe.Fori(0, NP) as i:
                        pe.wait_ge(s_["one_hot"], i + 1)
                        for b in range(4):
                            for d in range(2 * b, 2 * b + 2):
                                c0 = (d % 2) * 2 * M
                                for z, t0, m in zs_:
                                    o = ps[:, 4 + b, c0 + 2 * KL * z:c0 + 2 * KL * z + 2 * KZ[z]]
                                    for t in range(m // P):
                                        mm = nc.tensor.matmul(o, h2[:, t0 // P + t, d * P:(d + 1) * P], oh[z][:, t].rearrange("p e s -> p (e s)"),
                                                              start=(t == 0), stop=(t == m // P - 1))
                            mm.then_inc(s_["gathered"], 1)
                        pe.wait_ge(s_["xg_dve"], i + 1)
                        pe.wait_ge(s_["xg_act"], i + 1)

                        def gate_up(s):
                            for j in range(4):
                                pe.wait_ge(ring.loaded[j], 16 * (2 * i + s) + 16)
                                if s == 0 and j == 0:
                                    pe.wait_ge(s_["added"], i * NS)
                                if s == 1 and j % 2 == 0:
                                    pe.wait_ge(s_["hidden"], 4 * i + 1 + j // 2)
                                for k in range(KD):
                                    mm = nc.tensor.matmul(ps[0:M, j, :], xg[:, s, k, :], ring.slot[j][:, k, :],
                                                          start=(k == 0), stop=(k == KD - 1))
                                mm.then_inc(s_["multiplied"], 1)

                        def turn(s):
                            pe.wait_ge(s_["consts_loaded"], 48)
                            pe.wait_ge(s_["hidden"], 4 * i + 2 * s + 2)
                            for k in range(KD):
                                mm = nc.tensor.transpose(ps[:, 4 + k // 4, (k % 4) * M:(k % 4 + 1) * M], act_[s][:, k * P:(k + 1) * P], ident[0:M, 0:M])
                            mm.then_inc(s_["turned"], 1)

                        def down(s):
                            pe.wait_ge(s_["kept_act"], 2 * i + s + 1)
                            pe.wait_ge(s_["kept_dve"], 2 * i + s + 1)
                            if s == 1:
                                pe.wait_ge(s_["y_act"], 2 * i + 1)
                                pe.wait_ge(s_["y_dve"], 2 * i + 1)
                            for h in range(2):
                                pe.wait_ge(ring.loaded[4 + h], 16 * (2 * i + s) + 16)
                                for k in range(KD):
                                    mm = nc.tensor.matmul(ps[0:M, 6 + h, :], actT[s][:, k, :], ring.slot[4 + h][:, k, :],
                                                          start=(k == 0), stop=(k == KD - 1))
                                mm.then_inc(s_["down"], 1)

                        gate_up(0)
                        gate_up(1)
                        turn(0)
                        down(0)
                        pe.wait_ge(s_["hidden"], 4 * i + 4)
                        pe.wait_ge(s_["picked"], i + 1)
                        for z, t0, m in zs_:
                            w = 2 * KZ[z]
                            c0 = 2 * KL * z
                            nc.tensor.matmul(ps[0:w, 2 * z, 0:m], sel[:, c0:c0 + w], posT[:, t0:t0 + m], start=True, stop=True)
                            mm = nc.tensor.matmul(ps[0:w, 2 * z + 1, 0:m], sel[:, c0:c0 + w], affT[:, t0:t0 + m], start=True, stop=True)
                        mm.then_inc(s_["spread"], 1)
                        turn(1)
                        down(1)
                        pe.wait_ge(s_["scatter"], i + 1)
                        pe.wait_ge(s_["y_act"], 2 * i + 2)
                        pe.wait_ge(s_["y_dve"], 2 * i + 2)
                        for n in range(NS):
                            z, t0, m = zs_[n // KD]
                            d, w = n % KD, 2 * KZ[n // KD]
                            if n >= 4:
                                pe.wait_ge(s_["added"], i * NS + n - 3)
                            nc.tensor.matmul(ps[:, n % 4, 0:m], Y[z][:, d * P:(d + 1) * P], G[0:w, t0:t0 + m],
                                             start=True, stop=True).then_inc(s_["scattered"], 1)

                @block.vector
                def _(dve):
                    def one_hots(i):
                        for z, t0, m in zs_:
                            k = KZ[z]
                            for t in range(m // P):
                                last = nc.vector.tensor_tensor(oh[z][:, t], posm[:, t0 // P + t, ds(2 * i, 2)].unsqueeze(2).to_broadcast([P, 2, k]),
                                                               slots[:, 0:k].unsqueeze(1).to_broadcast([P, 2, k]), ALU.is_equal)
                        last.then_inc(s_["one_hot"], 1)

                    dve.wait_ge(s_["consts_loaded"], 48)
                    one_hots(0)
                    with dve.Fori(0, NP) as i:
                        ungather(dve, nc.vector.tensor_copy, i, (0, 1), s_["xg_dve"])
                        for s in range(2):
                            for h in range(2):
                                dve.wait_ge(s_["silued"], 4 * i + 2 * s + h + 1)
                                dve.wait_ge(s_["multiplied"], 8 * i + 4 * s + 2 * h + 2)
                                a_ = act_[s][:, h * 512:(h + 1) * 512]
                                nc.vector.tensor_tensor(a_, a_, ps[0:M, 2 * h + 1, :], ALU.mult).then_inc(s_["hidden"], 1)
                        one_hots(i + 1)
                        keep_turned(dve, nc.vector.tensor_copy, i, 0, 1, s_["kept_dve"])
                        keep_down(dve, nc.vector.tensor_copy, i, 0, 1, s_["y_dve"])
                        dve.wait_ge(s_["aff_copied"], i + 1)
                        for z, t0, m in zs_:
                            w = 2 * KZ[z]
                            last = nc.vector.scalar_tensor_tensor(G[0:w, t0:t0 + m], ps[0:w, 2 * z, 0:m], slot_of[0:w, z:z + 1],
                                                                  affb[0:w, t0:t0 + m], ALU.is_equal, ALU.mult)
                        last.then_inc(s_["scatter"], 1)
                        keep_turned(dve, nc.vector.tensor_copy, i, 1, 1, s_["kept_dve"])
                        keep_down(dve, nc.vector.tensor_copy, i, 1, 1, s_["y_dve"])
                        for n in range(NS):
                            z, t0, m = zs_[n // KD]
                            d = n % KD
                            dve.wait_ge(s_["scattered"], i * NS + n + 1)
                            nc.vector.scalar_tensor_tensor(xT[:, d, t0:t0 + m], ps[:, n % 4, 0:m], modT[:, 5 * KD + d, z:z + 1],
                                                           xT[:, d, t0:t0 + m], ALU.mult, ALU.add).then_inc(s_["added"], 1)

                @block.scalar
                def _(act):
                    with act.Fori(0, NP) as i:
                        ungather(act, nc.scalar.copy, i, (2, 3), s_["xg_act"])
                        for s in range(2):
                            for h in range(2):
                                act.wait_ge(s_["multiplied"], 8 * i + 4 * s + 2 * h + 1)
                                nc.scalar.activation(act_[s][:, h * 512:(h + 1) * 512], ps[0:M, 2 * h, :], ACT.Silu).then_inc(s_["silued"], 1)
                        keep_turned(act, nc.scalar.copy, i, 0, 0, s_["kept_act"])
                        keep_down(act, nc.scalar.copy, i, 0, 0, s_["y_act"])
                        act.wait_ge(s_["spread"], i + 1)
                        for z, t0, m in zs_:
                            w = 2 * KZ[z]
                            last = nc.scalar.copy(affb[0:w, t0:t0 + m], ps[0:w, 2 * z + 1, 0:m])
                        last.then_inc(s_["aff_copied"], 1)
                        keep_turned(act, nc.scalar.copy, i, 1, 0, s_["kept_act"])
                        keep_down(act, nc.scalar.copy, i, 1, 0, s_["y_act"])

        def store():
            with Scope() as st:
                rows = sb(st, "out_rows", [P, NL, D])
                turned, stored = sem(st, "out_turned"), sem(st, "stored")
                kept = [sem(st, "out_kept_dve"), sem(st, "out_kept_act")]
                block = st.enter_context(nc.Block())

                @block.tensor
                def _(pe):
                    for j in range(2 * NL):
                        if j >= 4:
                            pe.wait_ge(kept[j % 2], (j - 4) // 2 + 1)
                        for q in range(4):
                            mm = nc.tensor.transpose(ps[:, j % 4, q * P:(q + 1) * P], xT[:, 4 * (j % 2) + q, (j // 2) * P:(j // 2 + 1) * P], ident[:])
                        mm.then_inc(turned, 1)

                def keep(eng, copy, parity):
                    for t in range(NL):
                        eng.wait_ge(turned, 2 * t + parity + 1)
                        copy(rows[:, t, parity * 512:(parity + 1) * 512], ps[:, (2 * t + parity) % 4, :]).then_inc(kept[parity], 1)

                @block.vector
                def _(dve):
                    keep(dve, nc.vector.tensor_copy, 0)

                @block.scalar
                def _(act):
                    keep(act, nc.scalar.copy, 1)

                @block.sync
                def _(sp):
                    for t in range(NL):
                        for parity in range(2):
                            sp.wait_ge(kept[parity], t + 1)
                        sp.dma_start(out[0, t * P:(t + 1) * P, :], rows[:, t, :]).then_inc(stored, 16)
                    sp.wait_ge(stored, 16 * NL)

        setup()
        for l in range(DEPTH):
            last = l == DEPTH - 1
            modulation(l)
            with Scope() as mixed:
                mT = None
                with Scope() as mixers:
                    hT = sb(mixers, "hT", [P, KD, T])
                    oT = sb(mixers, "oT", [P, 10, T])
                    norm(0, hT, True)
                    with Scope() as heads:
                        proj = sb(heads, "proj", [P, NT, C_GL])
                        stat = sb(heads, "stat", [P, NT, N_STATS])
                        projection(l, hT, proj, last)
                        statistics(proj, stat, last)
                        neighbourhood(l, proj, stat, oT[:, 0:3], last)
                        windowed(l, proj, stat, oT[:, 3:6], last)
                        latent(l, proj, stat, oT[:, 6:10], last)
                    mT = sb(mixers, "mT", [P, KD, T])
                    merge(l, hT, oT, mT, not last)
                    output_projection(l, mT, not last)
            with Scope() as moe:
                nt = NL if last else NT
                ring = Ring(moe)
                h2 = sb(moe, "h2", [P, nt, D])
                posm = sb(moe, "slot_by_token", [P, nt, N_EXPERTS + 2])
                posT, affT = sb(moe, "slot_by_expert", [N_EXPERTS, T]), sb(moe, "affinity_by_expert", [N_EXPERTS, T])
                with Scope() as normed:
                    h2T = sb(normed, "h2T", [P, KD, T])
                    norm(1, h2T, not last, lambda sp: [ring.load(sp, l, 0, j) for j in range(6)])
                    route(l, h2T, h2, posm, posT, affT, not last)
                experts(l, ring, h2, posm, posT, affT, not last)
        store()


_INS = ["x", "c", "ctx", "c_ctx", "norm1_g", "norm2_g", "w_ada", "b_ada", "w_in", "na_q_g", "na_k_g", "na_rpb",
        "mla_q_norm", "mla_w_uq", "mla_kv_norm", "mla_w_ukv", "mla_q_g", "mla_k_g", "swa_q_g", "swa_k_g", "swa_sink",
        "w_na_o", "w_mla_o", "w_swa_o", "w_o", "router", "w_gate", "w_up", "w_down"]


def kernel(**inputs):
    import numpy as _np
    import concourse.bacc as _bacc
    from concourse import mybir as _mybir
    from concourse.bass_utils import run_bass_kernel_spmd as _run

    nc = _bacc.Bacc("TRN2", target_bir_lowering=False, num_devices=1)
    arrays, args = {}, {}
    for name in _INS:
        a = _np.ascontiguousarray(inputs[name])
        arrays[f"in_{name}"] = a
        args[name] = nc.dram_tensor(f"in_{name}", a.shape, _mybir.dt.from_np(a.dtype), kind="ExternalInput").ap()
    out = nc.dram_tensor("out_x", inputs["x"].shape, F32, kind="ExternalOutput").ap()
    build(nc, out=out, **args)
    return _run(nc, [arrays], core_ids=[0]).results[0]["out_x"]
```

```python
from contextlib import ExitStack

import numpy as np

import concourse.bass as bass
from concourse import mybir

F32, F32R = mybir.dt.float32, mybir.dt.float32r
ALU = mybir.AluOpType
ACT = mybir.ActivationFunctionType
AX = mybir.AxisListType
ds = bass.ds

P = 128
GRID_W = 64
NA_HEADS, NA_DIM, NA_WIN_COLS = 6, 64, 16
MLA_HEADS, MLA_Q_RANK, MLA_KV_RANK, MLA_NOPE, MLA_ROPE, MLA_V = 4, 256, 128, 128, 64, 128
MLA_QK = MLA_NOPE + MLA_ROPE
SWA_HEADS, SWA_KV_HEADS, SWA_DIM, SWA_WINDOW = 6, 2, 64, 128
N_EXPERTS, EXPERT_FF, CAPACITY_FACTOR = 16, 1024, 2
ROPE_BASE = 10000.0
EPS = 1e-6
MASKED = -1e30

NA_W = NA_HEADS * NA_DIM
C_NAQ, C_NAK, C_NAV = 0, NA_W, 2 * NA_W
C_CQ = 3 * NA_W
C_CKV = C_CQ + MLA_Q_RANK
C_KR = C_CKV + MLA_KV_RANK
C_SQ = C_KR + MLA_ROPE
C_SK = C_SQ + SWA_HEADS * SWA_DIM
C_SV = C_SK + SWA_KV_HEADS * SWA_DIM
C_GL = C_SV + SWA_KV_HEADS * SWA_DIM
GROUPS = [(C_NAQ, NA_W, False), (C_NAK, NA_W, True), (C_NAV, NA_W, True),
          (C_CQ, C_SQ - C_CQ, True), (C_SQ, C_SK - C_SQ, False), (C_SK, C_GL - C_SK, True)]

R_NA, R_SW, R_CQ, R_CKV, R_KR, N_STATS = 0, 12, 20, 21, 22, 23


class Chain:

    def __init__(self, eng, sem, base=0):
        self.eng, self.sem, self.base, self.n = eng, sem, base, 0

    def link(self, instruction):
        self.n += 1
        instruction.then_inc(self.sem, 1)
        self.eng.wait_ge(self.sem, self.base + self.n)


def constants(S, L):
    nt, nl = (S + L) // P, S // P
    t = np.arange(S)
    f = SWA_DIM // 4
    inv = (np.float32(ROPE_BASE) ** (-np.arange(f, dtype=np.float32) / np.float32(f))).astype(np.float32)
    ar = ((t // GRID_W).astype(np.float32)[:, None] * inv).astype(np.float32)
    ac = ((t % GRID_W).astype(np.float32)[:, None] * inv).astype(np.float32)
    cos = np.concatenate([np.cos(ar), np.cos(ar), np.cos(ac), np.cos(ac)], 1)
    sin = np.concatenate([-np.sin(ar), np.sin(ar), -np.sin(ac), np.sin(ac)], 1)
    cos = np.concatenate([cos, np.ones((L, 64))]).reshape(nt, P, 64).transpose(1, 0, 2)
    sin = np.concatenate([sin, np.zeros((L, 64))]).reshape(nt, P, 64).transpose(1, 0, 2)
    i, j = np.arange(P)[:, None], np.arange(P)[None, :]
    band = np.concatenate([np.where(j >= i, 0, MASKED), np.zeros((P, P)), np.where(j <= i, 0, MASKED)], 1)
    col = np.arange(GRID_W)
    c0 = np.clip(col - NA_WIN_COLS // 2, 0, GRID_W - NA_WIN_COLS)
    ok = (col[None] >= c0[:, None]) & (col[None] < c0[:, None] + NA_WIN_COLS)
    colmask = np.tile(np.where(ok, 0, MASKED), (2, 1))
    kl, kc = CAPACITY_FACTOR * S // N_EXPERTS, CAPACITY_FACTOR * L // N_EXPERTS
    slots = np.tile(np.arange(1, kl + 1), (P, 1))
    p = np.arange(P)
    slot_of = np.stack([p % kl + 1, p % kc + 1], 1)
    return {n: np.ascontiguousarray(a, np.float32) for n, a in dict(
        ident=np.eye(P), cos=cos.reshape(P, -1), sin=sin.reshape(P, -1), band=band, colmask=colmask,
        slots=slots, slot_of=slot_of).items()}


def build(nc, x, c, ctx, c_ctx, norm1_g, norm2_g, w_ada, b_ada, w_in, na_q_g, na_k_g, na_rpb,
          mla_q_norm, mla_w_uq, mla_kv_norm, mla_w_ukv, mla_q_g, mla_k_g, swa_q_g, swa_k_g, swa_sink,
          w_na_o, w_mla_o, w_swa_o, w_o, router, w_gate, w_up, w_down, out, dbg=None, stop=None):
    _, S, D = x.shape
    L = ctx.shape[1]
    DEPTH = w_in.shape[0]
    T = S + L
    NT, NL = T // P, S // P
    KD = D // P
    NM = 6 * KD
    KL, KC = CAPACITY_FACTOR * S // N_EXPERTS, CAPACITY_FACTOR * L // N_EXPERTS
    MS = KL + KC
    FF = EXPERT_FF
    nsem = [0]

    class Scope(ExitStack):

        def __init__(self):
            super().__init__()
            self.sems = []
            self.callback(self.clear)

        def clear(self):
            if self.sems:
                nc.clear_and_free_semaphores(self.sems)
                nc.all_engine_barrier()

    def sem(stack, name):
        nsem[0] += 1
        stack.sems.append(nc.alloc_semaphore(f"{name}_{nsem[0]}"))
        return stack.sems[-1]

    def sb(stack, name, shape, dtype=F32):
        nsem[0] += 1
        return stack.enter_context(nc.sbuf_tensor(f"{name}_{nsem[0]}", shape, dtype))

    top = Scope()
    const = {n: nc.inline_tensor(a, name=f"const_{n}") for n, a in constants(S, L).items()}
    const = {n: (a.ap() if hasattr(a, "ap") else a) for n, a in const.items()}
    RPBW = 2 * GRID_W - 1
    rpb_pad = nc.dram_tensor("rpb_padded", [DEPTH, GRID_W, NA_HEADS * 15, RPBW], F32, kind="Internal").ap()

    with top:
        xT = sb(top, "xT", [P, KD, T])
        ident = sb(top, "ident", [P, P])
        ones = sb(top, "ones", [P, P])
        cos = sb(top, "cos", [P, NT, 64])
        sin = sb(top, "sin", [P, NT, 64])
        cT = sb(top, "cT", [P, 2, KD])
        modT = sb(top, "modT", [P, NM, 2])
        vecT = sb(top, "vecT", [P, NM + 2 * KD])
        coef = sb(top, "coef", [P, 2, KD, 2])
        ps = top.enter_context(nc.psum_tensor("ps", [P, 8, 512], F32))

        def streams(ctx_too):
            return [(0, 0, S), (1, S, L)][:1 + ctx_too]

        def finish(name):
            return stop == name

        def setup():
            with Scope() as st:
                rows = sb(st, "rows", [P, NT, D])
                crow = sb(st, "crow", [2 * KD, P])
                loaded, cl, ready = sem(st, "loaded"), sem(st, "c_loaded"), sem(st, "ones_ready")
                turned, kept_v, kept_a = sem(st, "turned"), sem(st, "kept_by_dve"), sem(st, "kept_by_act")
                block = st.enter_context(nc.Block())

                @block.sync
                def _(sp):
                    sp.dma_start(ident[:], const["ident"]).then_inc(cl, 16)
                    sp.dma_start(crow[0:KD, :], c.rearrange("b (k p) -> (b k) p", p=P)).then_inc(cl, 16)
                    sp.dma_start(crow[KD:2 * KD, :], c_ctx.rearrange("(k p) -> k p", p=P)).then_inc(cl, 16)
                    sp.dma_start(rows[:, 0:NL, :], x[0].rearrange("(t p) d -> p t d", p=P)).then_inc(loaded, 16)
                    sp.dma_start(rows[:, NL:NT, :], ctx[0].rearrange("(t p) d -> p t d", p=P)).then_inc(loaded, 16)
                    sp.dma_start(cos[:].rearrange("p a b -> p (a b)"), const["cos"]).then_inc(cl, 16)
                    sp.dma_start(sin[:].rearrange("p a b -> p (a b)"), const["sin"]).then_inc(cl, 16)
                    sp.wait_ge(cl, 80)

                @block.gpsimd
                def _(pool):
                    nc.gpsimd.memset(ones[:], 1.0).then_inc(ready, 1)

                @block.tensor
                def _(pe):
                    pe.wait_ge(cl, 80)
                    nc.tensor.transpose(ps[:, 7, 0:2 * KD], crow[:], ident[0:2 * KD, 0:2 * KD]).then_inc(turned, 1)
                    pe.wait_ge(loaded, 32)
                    for k in range(KD):
                        for s, t0, n in streams(True):
                            b = 2 * (k % 2) + s
                            if k >= 2:
                                pe.wait_ge((kept_v, kept_a)[s], k - 1)
                            for t in range(n // P):
                                mm = nc.tensor.transpose(ps[:, b, t * P:(t + 1) * P],
                                                         rows[:, t0 // P + t, k * P:(k + 1) * P], ident[:])
                            mm.then_inc(turned, 1)

                @block.vector
                def _(dve):
                    for k in range(KD):
                        dve.wait_ge(turned, 2 * k + 2)
                        nc.vector.tensor_copy(xT[:, k, 0:S], ps[:, 2 * (k % 2), 0:S]).then_inc(kept_v, 1)

                @block.scalar
                def _(act):
                    act.wait_ge(turned, 1)
                    nc.scalar.activation(cT[:].rearrange("p s k -> p (s k)"), ps[:, 7, 0:2 * KD], ACT.Silu)
                    for k in range(KD):
                        act.wait_ge(turned, 2 * k + 3)
                        nc.scalar.copy(xT[:, k, S:T], ps[:, 2 * (k % 2) + 1, 0:L]).then_inc(kept_a, 1)

        def modulation(l):
            NB = 6 * D // 512
            with Scope() as st:
                wbuf = [sb(st, f"w_ada{s}", [P, KD, 512]) for s in range(2)]
                row = [sb(st, f"mod_row{s}", [P, 512]) for s in range(2)]
                vrow = sb(st, "vec_rows", [NM + 2 * KD, P])
                wl = [sem(st, f"w_ada_loaded{s}") for s in range(2)]
                vl, mm_done, row_done = sem(st, "vec_loaded"), sem(st, "mod_mm"), sem(st, "mod_row")
                turned, kept, vt, ch = sem(st, "mod_turned"), sem(st, "mod_kept"), sem(st, "vec_turned"), sem(st, "mod_chain")
                block = st.enter_context(nc.Block())
                wv = w_ada[l].rearrange("(k p) n -> p k n", p=P)

                @block.sync
                def _(sp):
                    sp.dma_start(vrow[0:NM, :], b_ada[l].rearrange("(k p) -> k p", p=P)).then_inc(vl, 16)
                    sp.dma_start(vrow[NM:NM + KD, :], norm1_g[l].rearrange("(k p) -> k p", p=P)).then_inc(vl, 16)
                    sp.dma_start(vrow[NM + KD:, :], norm2_g[l].rearrange("(k p) -> k p", p=P)).then_inc(vl, 16)
                    for s in range(2):
                        sp.dma_start(wbuf[s][:], wv[:, :, s * 512:(s + 1) * 512]).then_inc(wl[s], 16)
                    with sp.Fori(0, NB // 2 - 1) as i:
                        for s in range(2):
                            sp.wait_ge(mm_done, 2 * i + s + 1)
                            sp.dma_start(wbuf[s][:], wv[:, :, ds((2 * i + s + 2) * 512, 512)]).then_inc(wl[s], 16)

                @block.tensor
                def _(pe):
                    pe.wait_ge(vl, 48)
                    nc.tensor.transpose(ps[:, 4, 0:NM + 2 * KD], vrow[:], ident[0:NM + 2 * KD, 0:NM + 2 * KD]).then_inc(vt, 1)
                    with pe.Fori(0, NB // 2) as i:
                        for s in range(2):
                            pe.wait_ge(wl[s], 16 * i + 16)
                            pe.wait_ge(row_done, 2 * i)
                            for k in range(KD):
                                mm = nc.tensor.matmul(ps[0:2, s, :], cT[:, :, k], wbuf[s][:, k, :],
                                                      start=(k == 0), stop=(k == KD - 1))
                            mm.then_inc(mm_done, 1)
                        for s in range(2):
                            pe.wait_ge(row_done, 2 * i + s + 1)
                            pe.wait_ge(kept, 2 * i)
                            for j in range(4):
                                mm = nc.tensor.transpose(ps[:, 2 + s, j * P:(j + 1) * P], row[s][:, j * P:(j + 1) * P], ident[:])
                            mm.then_inc(turned, 1)

                @block.vector
                def _(dve):
                    for s in range(2):
                        nc.vector.memset(row[s][:], 0.0).then_inc(ch, 1)
                    dve.wait_ge(ch, 2)
                    dve.wait_ge(vt, 1)
                    nc.vector.tensor_copy(vecT[:], ps[:, 4, 0:NM + 2 * KD]).then_inc(ch, 1)
                    with dve.Fori(0, NB // 2) as i:
                        for s in range(2):
                            dve.wait_ge(mm_done, 2 * i + s + 1)
                            dve.wait_ge(turned, 2 * i)
                            nc.vector.tensor_copy(row[s][0:2, :], ps[0:2, s, :]).then_inc(row_done, 1)
                        for s in range(2):
                            dve.wait_ge(turned, 2 * i + s + 1)
                            nc.vector.tensor_copy(modT[:, ds((2 * i + s) * 4, 4), :],
                                                  ps[:, 2 + s, :].rearrange("p (a b) -> p a b", b=P)[:, :, 0:2]).then_inc(kept, 1)
                    dve.wait_ge(kept, NB)
                    dve.wait_ge(ch, 3)
                    chain = Chain(dve, ch, 3)
                    chain.link(nc.vector.tensor_tensor(modT[:], modT[:],
                                                       vecT[:, 0:NM].unsqueeze(2).to_broadcast([P, NM, 2]), ALU.add))
                    for n in range(2):
                        m = (1 + 3 * n) * KD
                        chain.link(nc.vector.tensor_scalar(coef[:, n], modT[:, m:m + KD, :], 1.0, None, ALU.add))
                        g = vecT[:, NM + n * KD:NM + (n + 1) * KD]
                        chain.link(nc.vector.tensor_tensor(coef[:, n], coef[:, n],
                                                           g.unsqueeze(2).to_broadcast([P, KD, 2]), ALU.mult))

        def norm(n, hT, ctx_too, ahead=None):
            W = T if ctx_too else S
            with Scope() as st:
                sq = [sb(st, f"sq{s}", [P, W]) for s in range(2)]
                rs = sb(st, "rs", [P, W])
                tmp = [sb(st, f"scaled{s}", [P, W]) for s in range(2)]
                squared, summed, root, scaled, done = (sem(st, q) for q in ("squared", "summed", "root", "scaled", "normed"))
                ch = sem(st, "norm_chain")
                block = st.enter_context(nc.Block())

                @block.sync
                def _(sp):
                    if ahead:
                        ahead(sp)

                @block.scalar
                def _(act):
                    for k in range(KD):
                        if k >= 2:
                            act.wait_ge(summed, k - 1)
                        nc.scalar.activation(sq[k % 2][:], xT[:, k, 0:W], ACT.Square).then_inc(squared, 1)
                    act.wait_ge(ch, 1)
                    nc.scalar.activation(rs[:], rs[:], ACT.Sqrt).then_inc(root, 1)
                    for k in range(KD):
                        act.wait_ge(scaled, k + 1)
                        for s, t0, m in streams(ctx_too):
                            last = nc.scalar.activation(hT[:, k, t0:t0 + m], tmp[k % 2][:, t0:t0 + m], ACT.Identity,
                                                        bias=modT[:, 3 * n * KD + k, s:s + 1], scale=coef[:, n, k, s:s + 1])
                        last.then_inc(done, 1)

                @block.tensor
                def _(pe):
                    for k in range(KD):
                        pe.wait_ge(squared, k + 1)
                        for s, t0, m in streams(ctx_too):
                            mm = nc.tensor.matmul(ps[:, s, 0:m], ones[:], sq[k % 2][:, t0:t0 + m],
                                                  start=(k == 0), stop=(k == KD - 1))
                        mm.then_inc(summed, 1)

                @block.vector
                def _(dve):
                    dve.wait_ge(summed, KD)
                    for s, t0, m in streams(ctx_too):
                        last = nc.vector.tensor_scalar(rs[:, t0:t0 + m], ps[:, s, 0:m], 1.0 / D, EPS, ALU.mult, ALU.add)
                    last.then_inc(ch, 1)
                    dve.wait_ge(root, 1)
                    nc.vector.reciprocal(rs[:], rs[:]).then_inc(ch, 1)
                    dve.wait_ge(ch, 2)
                    for k in range(KD):
                        if k >= 2:
                            dve.wait_ge(done, k - 1)
                        nc.vector.tensor_tensor(tmp[k % 2][:], xT[:, k, 0:W], rs[:], ALU.mult).then_inc(scaled, 1)

        def projection(l, hT, proj, last_layer):
            NK, SLOTS = 2, 2
            with Scope() as st:
                h_hi, h_lo = (sb(st, f"h_{q}", [P, KD, T], F32R) for q in ("hi", "lo"))
                wbuf = [sb(st, f"w_in{s}", [P, NK, 448]) for s in range(SLOTS)]
                w_hi, w_lo = ([sb(st, f"w_in_{q}{s}", [P, NK, 448], F32R) for s in range(SLOTS)] for q in ("hi", "lo"))
                zrow = sb(st, "rpb_rows", [NA_HEADS * 15, DEPTH, RPBW]) if l == 0 else None
                zeroed, padded = sem(st, "rpb_zeroed"), sem(st, "rpb_padded")
                wl = [sem(st, f"w_in_loaded{s}") for s in range(SLOTS)]
                h_hi_made, h_lo_made, w_hi_made, w_lo_made = (sem(st, q) for q in ("h_hi", "h_lo", "w_in_hi", "w_in_lo"))
                multiplied, finished = sem(st, "proj_multiplied"), sem(st, "proj_finished")
                kept = [sem(st, "proj_kept_dve"), sem(st, "proj_kept_act")]
                block = st.enter_context(nc.Block())
                wv = w_in[l].rearrange("(k p) n -> p k n", p=P)
                work = [(g, t) for g in range(len(GROUPS)) for t in range(NT if not last_layer or GROUPS[g][2] else NL)]
                done_by = [sum(w[0] < g for w in work) for g in range(len(GROUPS) + 1)]
                UG = KD // NK
                N = UG * len(GROUPS)

                def unit_done(eng, n):
                    g, u = n // UG, n % UG
                    if u == UG - 1:
                        eng.wait_ge(finished, done_by[g + 1])
                    else:
                        eng.wait_ge(multiplied, g * (UG - 1) + u + 1)

                @block.sync
                def _(sp):
                    for n in range(N):
                        if n == 4 and l == 0:
                            sp.wait_ge(zeroed, 1)
                            for m in range(DEPTH):
                                sp.dma_start(zrow[:, m, 48:79], na_rpb[m].rearrange("h r c -> (h r) c")).then_inc(padded, 16)
                        if n == 8 and l == 0:
                            sp.wait_ge(padded, 16 * DEPTH)
                            for m in range(DEPTH):
                                sp.dma_start(rpb_pad[m].rearrange("q r c -> r q c"), zrow[:, m].unsqueeze(1).to_broadcast([NA_HEADS * 15, GRID_W, RPBW])).then_inc(padded, 16)
                        g, u = n // UG, n % UG
                        c0, w, _ = GROUPS[g]
                        if n >= SLOTS:
                            sp.wait_ge(w_lo_made, n - SLOTS + 1)
                        sp.dma_start(wbuf[n % SLOTS][:, :, 0:w], wv[:, u * NK:(u + 1) * NK, c0:c0 + w]).then_inc(wl[n % SLOTS], 16)
                    if l == 0:
                        sp.wait_ge(padded, 32 * DEPTH)

                @block.gpsimd
                def _(pool):
                    if l == 0:
                        nc.gpsimd.memset(zrow[:], 0.0).then_inc(zeroed, 1)

                @block.tensor
                def _(pe):
                    for n in range(N):
                        g, u = n // UG, n % UG
                        w = GROUPS[g][1]
                        if g == 0:
                            pe.wait_ge(h_hi_made, NK * (u + 1))
                            pe.wait_ge(h_lo_made, NK * (u + 1))
                        pe.wait_ge(w_hi_made, n + 1)
                        pe.wait_ge(w_lo_made, n + 1)
                        for j in range(done_by[g], done_by[g + 1]):
                            t = work[j][1]
                            if u == 0 and j >= 8:
                                pe.wait_ge(kept[j % 2], (j - 8) // 2 + 1)
                            for q in range(NK):
                                k = u * NK + q
                                for h, w_ in ((h_hi, w_hi), (h_hi, w_lo), (h_lo, w_hi)):
                                    mm = nc.tensor.matmul(ps[:, j % 8, 0:w], h[:, k, t * P:(t + 1) * P], w_[n % SLOTS][:, q, 0:w],
                                                          start=(k == 0 and w_ is w_hi and h is h_hi), stop=(k == KD - 1 and h is h_lo))
                            if u == UG - 1:
                                mm.then_inc(finished, 1)
                        if u < UG - 1:
                            mm.then_inc(multiplied, 1)

                def keep(eng, copy, parity, g):
                    for j in range(done_by[g], done_by[g + 1]):
                        if j % 2 == parity:
                            c0, w, _ = GROUPS[g]
                            eng.wait_ge(finished, j + 1)
                            copy(proj[:, work[j][1], c0:c0 + w], ps[:, j % 8, 0:w]).then_inc(kept[parity], 1)

                @block.vector
                def _(dve):
                    for n in range(N):
                        g, w = n // UG, GROUPS[n // UG][1]
                        if g == 0:
                            for k in range(n * NK, (n + 1) * NK):
                                dve.wait_ge(h_hi_made, k + 1)
                                nc.vector.tensor_tensor(h_lo[:, k, :], hT[:, k, :], h_hi[:, k, :].bitcast(F32), ALU.subtract).then_inc(h_lo_made, 1)
                        if n % UG == 1 and g > 0:
                            keep(dve, nc.vector.tensor_copy, 0, g - 1)
                        dve.wait_ge(w_hi_made, n + 1)
                        nc.vector.tensor_tensor(w_lo[n % SLOTS][:, :, 0:w], wbuf[n % SLOTS][:, :, 0:w],
                                                w_hi[n % SLOTS][:, :, 0:w].bitcast(F32), ALU.subtract).then_inc(w_lo_made, 1)
                    keep(dve, nc.vector.tensor_copy, 0, len(GROUPS) - 1)

                @block.scalar
                def _(act):
                    for n in range(N):
                        g, w = n // UG, GROUPS[n // UG][1]
                        if g == 0:
                            for k in range(n * NK, (n + 1) * NK):
                                nc.scalar.copy(h_hi[:, k, :], hT[:, k, :]).then_inc(h_hi_made, 1)
                        if n % UG == 1 and g > 0:
                            keep(act, nc.scalar.copy, 1, g - 1)
                        act.wait_ge(wl[n % SLOTS], 16 * (n // SLOTS + 1))
                        if n >= SLOTS:
                            unit_done(act, n - SLOTS)
                        nc.scalar.copy(w_hi[n % SLOTS][:, :, 0:w], wbuf[n % SLOTS][:, :, 0:w]).then_inc(w_hi_made, 1)
                    keep(act, nc.scalar.copy, 1, len(GROUPS) - 1)

        def statistics(proj, stat, last_layer, ahead):
            full = [(C_NAQ, 64, 12, R_NA), (C_CQ, 256, 1, R_CQ), (C_CKV, 128, 1, R_CKV), (C_KR, 64, 1, R_KR), (C_SQ, 64, 8, R_SW)]
            keys = [(C_NAK, 64, 6, R_NA + 6), (C_CKV, 128, 1, R_CKV), (C_KR, 64, 1, R_KR), (C_SK, 64, 2, R_SW + 6)]
            with Scope() as st:
                sq = [sb(st, f"stat_sq{s}", [P, C_SV]) for s in range(2)]
                squared, summed, root, ch = (sem(st, q) for q in ("stat_squared", "stat_summed", "stat_root", "stat_chain"))
                block = st.enter_context(nc.Block())
                segs = [keys if last_layer and t >= NL else full for t in range(NT)]

                @block.sync
                def _(sp):
                    ahead(sp)

                @block.scalar
                def _(act):
                    for t in range(NT):
                        if t >= 2:
                            act.wait_ge(summed, t - 1)
                        for c0, w, n, _ in segs[t]:
                            last = nc.scalar.activation(sq[t % 2][:, c0:c0 + n * w], proj[:, t, c0:c0 + n * w], ACT.Square)
                        last.then_inc(squared, 1)
                    act.wait_ge(ch, 4)
                    nc.scalar.activation(stat[:, :, 0:R_KR], stat[:, :, 0:R_KR], ACT.Sqrt).then_inc(root, 1)

                @block.vector
                def _(dve):
                    chain = Chain(dve, ch)
                    chain.link(nc.vector.memset(stat[:], 0.0))
                    for t in range(NT):
                        dve.wait_ge(squared, t + 1)
                        for c0, w, n, r in segs[t]:
                            last = nc.vector.tensor_reduce(stat[:, t, r:r + n],
                                                           sq[t % 2][:, c0:c0 + n * w].rearrange("p (h d) -> p h d", d=w),
                                                           AX.X, ALU.add)
                        last.then_inc(summed, 1)
                    dve.wait_ge(summed, NT)
                    for r0, r1, w in ((R_NA, R_CQ, 64), (R_CQ, R_CKV, 256), (R_CKV, R_KR, 128)):
                        nc.vector.tensor_scalar(stat[:, :, r0:r1], stat[:, :, r0:r1], 1.0 / w, EPS,
                                                ALU.mult, ALU.add).then_inc(ch, 1)
                    dve.wait_ge(root, 1)
                    nc.vector.reciprocal(stat[:, :, 0:R_KR], stat[:, :, 0:R_KR])

        SWAP = [(a * 32 + b * 16, a * 32 + (1 - b) * 16) for a in range(2) for b in range(2)]

        def rope_tables(chain, cg, sg, g, scale):
            chain.link(nc.vector.tensor_scalar(g[:], g[:], scale, None, ALU.mult))
            nc.vector.tensor_tensor(cg[:], cos[:], g[:].unsqueeze(1).to_broadcast([P, NT, 64]), ALU.mult)
            for d, o in SWAP:
                last = nc.vector.tensor_tensor(sg[:, :, d:d + 16], sin[:, :, d:d + 16],
                                               g[:, o:o + 16].unsqueeze(1).to_broadcast([P, NT, 16]), ALU.mult)
            chain.link(last)

        def rope(chain, res, x, part, cg, sg, nt, heads):
            nc.vector.tensor_tensor(res, x, cg[:, 0:nt].unsqueeze(2).to_broadcast([P, nt, heads, 64]), ALU.mult)
            for d, o in SWAP:
                last = nc.vector.tensor_tensor(part[:, :, :, d:d + 16], x[:, :, :, o:o + 16],
                                               sg[:, 0:nt, d:d + 16].unsqueeze(2).to_broadcast([P, nt, heads, 16]), ALU.mult)
            chain.link(last)
            return nc.vector.tensor_tensor(res, res, part, ALU.add)

        class Attention:

            def __init__(self, st, name, heads, dv, tiles, key_tiles):
                self.units = [(hh, t) for hh in range(heads) for t in tiles]
                self.U, self.dv, self.key_tiles, self.tiles = len(self.units), dv, key_tiles, tiles
                assert self.U % 2 == 0
                self.pexp = [sb(st, f"{name}_exp{s}", [P, T]) for s in range(2)]
                self.pT = [sb(st, f"{name}_expT{s}", [P, NT, P]) for s in range(2)]
                self.rowmax = sb(st, f"{name}_max", [P, 2, 4])
                self.rowsum = sb(st, f"{name}_sum", [P, 4, 3])
                self.osb = sb(st, f"{name}_o", [P, len(tiles), P])
                self.scored = sem(st, f"{name}_scored")
                self.maxed = sem(st, f"{name}_maxed")
                self.exped = sem(st, f"{name}_exped")
                self.turned = sem(st, f"{name}_turned")
                self.kept_lo = sem(st, f"{name}_kept_lo")
                self.kept_hi = sem(st, f"{name}_kept_hi")
                self.valued = sem(st, f"{name}_valued")
                self.divided = sem(st, f"{name}_divided")
                self.o_turned = sem(st, f"{name}_o_turned")
                self.o_kept = sem(st, f"{name}_o_kept")
                self.staged = sem(st, f"{name}_staged")
                self.q_turned = sem(st, f"{name}_q_turned")
                self.qk_kept = sem(st, f"{name}_qk_kept")
                self.chain = sem(st, f"{name}_chain")

            def pe_units(self, pe, i, score, value):
                def transposes(u):
                    t = self.units[u][1]
                    n = i * self.U + u
                    pe.wait_ge(self.exped, n + 1)
                    pe.wait_ge(self.kept_lo, n)
                    pe.wait_ge(self.kept_hi, n)
                    kt = self.key_tiles(t)
                    for q in range(len(kt)):
                        h = (len(kt) + 1) // 2
                        mm = nc.tensor.transpose(ps[:, 4 + q // h, (q % h) * P:(q % h + 1) * P],
                                                 self.pexp[u % 2][:, q * P:(q + 1) * P], ident[:])
                    mm.then_inc(self.turned, 1)

                def values(u):
                    hh, t = self.units[u]
                    n = i * self.U + u
                    pe.wait_ge(self.kept_lo, n + 1)
                    pe.wait_ge(self.kept_hi, n + 1)
                    pe.wait_ge(self.divided, n - 1 if u >= 1 else n)
                    kt = self.key_tiles(t)
                    o = ps[:, 6 + u % 2, 0:self.dv]
                    for q, k in enumerate(kt):
                        mm = nc.tensor.matmul(o, self.pT[u % 2][:, q, :], value(hh, k), start=(q == 0), stop=(q == len(kt) - 1))
                    mm.then_inc(self.valued, 1)

                def scores(u):
                    hh, t = self.units[u]
                    n = i * self.U + u
                    pe.wait_ge(self.exped, n - 1 if u >= 1 else n)
                    score(hh, t, 2 * (u % 2)).then_inc(self.scored, 1)

                scores(0)
                scores(1)
                transposes(0)
                for u in range(self.U):
                    if u + 2 < self.U:
                        scores(u + 2)
                    if u + 1 < self.U:
                        transposes(u + 1)
                    values(u)
                pe.wait_ge(self.divided, (i + 1) * self.U)
                pe.wait_ge(self.kept_lo, (i + 1) * self.U)
                pe.wait_ge(self.kept_hi, (i + 1) * self.U)
                for q in range(len(self.tiles)):
                    mm = nc.tensor.transpose(ps[:, 4 if q < NL else 5, (q % NL) * P:(q % NL + 1) * P],
                                             self.osb[:, q, :], ident[:])
                mm.then_inc(self.o_turned, 1)

            def dve_units(self, dve, i, chain, maximum, more_sum=None):
                def keep_hi(u):
                    t = self.units[u][1]
                    n = i * self.U + u
                    kt = len(self.key_tiles(t))
                    dve.wait_ge(self.turned, n + 1)
                    dve.wait_ge(self.valued, n - 1 if u >= 1 else n)
                    h = (kt + 1) // 2
                    nc.vector.tensor_copy(self.pT[u % 2][:, h:kt, :].rearrange("p a b -> p (a b)"),
                                          ps[:, 5, 0:(kt - h) * P]).then_inc(self.kept_hi, 1)

                def divide(u):
                    t = self.units[u][1]
                    n = i * self.U + u
                    dve.wait_ge(self.valued, n + 1)
                    s = self.rowsum[:, u % 4]
                    if more_sum:
                        chain.link(nc.vector.tensor_tensor(s[:, 0:1], s[:, 0:1], s[:, 2:3], ALU.add))
                    chain.link(nc.vector.reciprocal(s[:, 1:2], s[:, 0:1]))
                    hh = self.units[u][0]
                    if u == 0:
                        dve.wait_ge(self.o_turned, i)
                    nc.vector.tensor_scalar(self.osb[:, self.tiles.index(t), hh * self.dv:(hh + 1) * self.dv],
                                            ps[:, 6 + u % 2, 0:self.dv], s[:, 1:2], None,
                                            ALU.mult).then_inc(self.divided, 1)

                def maxima(u):
                    hh, t = self.units[u]
                    n = i * self.U + u
                    dve.wait_ge(self.scored, n + 1)
                    dve.wait_ge(self.exped, n - 1 if u >= 1 else n)
                    maximum(hh, t, 2 * (u % 2), u % 2).then_inc(self.maxed, 1)

                maxima(0)
                maxima(1)
                keep_hi(0)
                for u in range(self.U):
                    if u + 2 < self.U:
                        maxima(u + 2)
                    if u + 1 < self.U:
                        keep_hi(u + 1)
                    divide(u)

            def act_units(self, act, i, source, oT, more_exp=None):
                def exponentials(u):
                    hh, t = self.units[u]
                    n = i * self.U + u
                    act.wait_ge(self.maxed, n + 1)
                    act.wait_ge(self.turned, n - 1 if u >= 1 else n)
                    act.wait_ge(self.divided, n - 3 if u >= 4 else i * self.U)
                    if more_exp:
                        more_exp(hh, u)
                    src = source(t, 2 * (u % 2), u % 2)
                    nc.scalar.activation(self.pexp[u % 2][:, 0:src.shape[1]], src, ACT.Exp, bias=self.rowmax[:, u % 2, 3:4],
                                         accum_out=self.rowsum[:, u % 4, 0:1]).then_inc(self.exped, 1)

                def keep_lo(u):
                    t = self.units[u][1]
                    n = i * self.U + u
                    kt = len(self.key_tiles(t))
                    act.wait_ge(self.turned, n + 1)
                    act.wait_ge(self.valued, n - 1 if u >= 1 else n)
                    h = (kt + 1) // 2
                    nc.scalar.copy(self.pT[u % 2][:, 0:h, :].rearrange("p a b -> p (a b)"),
                                   ps[:, 4, 0:h * P]).then_inc(self.kept_lo, 1)

                exponentials(0)
                exponentials(1)
                keep_lo(0)
                for u in range(self.U):
                    if u + 2 < self.U:
                        exponentials(u + 2)
                    if u + 1 < self.U:
                        keep_lo(u + 1)
                act.wait_ge(self.o_turned, i + 1)
                w = min(len(self.tiles), NL) * P
                last = nc.scalar.copy(oT[:, ds(i, 1), 0:w], ps[:, 4:5, 0:w])
                if len(self.tiles) > NL:
                    last = nc.scalar.copy(oT[:, ds(i, 1), w:T], ps[:, 5:6, 0:T - w])
                last.then_inc(self.o_kept, 1)

        def load_bias(sp, l, bias, colmask, bl):
            sp.dma_start(colmask[:], const["colmask"]).then_inc(bl, 16)
            for h in range(NA_HEADS):
                for par in range(2):
                    src = bass.AP(tensor=rpb_pad.tensor, offset=(l * GRID_W * NA_HEADS * 15 + h * 15 + 1 - par) * RPBW + GRID_W - 1,
                                  ap=[[RPBW * 15 * NA_HEADS - 1, GRID_W], [RPBW, 14], [1, GRID_W]])
                    sp.dma_start(bias[par * 64:(par + 1) * 64, h, :].rearrange("p (j k) -> p j k", k=GRID_W), src).then_inc(bl, 16)

        def neighbourhood(l, proj, stat, oT, bias, colmask, bl, last_layer):
            nq = NL if last_layer else NT
            keys_of = lambda t: list(range(NT)) if t < NL else list(range(NL, NT))
            with Scope() as st:
                a = Attention(st, "na", 2, NA_DIM, list(range(nq)), keys_of)
                bst = sb(st, "bias", [P, 2, 14, GRID_W])
                qst, kst = sb(st, "na_q", [P, nq, 2, 64]), sb(st, "na_k", [P, NT, 2, 64])
                qT, kT = sb(st, "na_qT", [P, T]), sb(st, "na_kT", [P, T])
                score = [sb(st, f"na_scores{s}", [P, T]) for s in range(2)]
                gain = sb(st, "na_gain", [P, 2])
                gl, based, gained = (sem(st, q) for q in ("gain_loaded", "bias_ready", "gain_ready"))
                block = st.enter_context(nc.Block())
                U = a.U

                @block.sync
                def _(sp):
                    for n, g in enumerate((na_q_g, na_k_g)):
                        for h in range(2):
                            sp.dma_start(gain[h * 64:(h + 1) * 64, n:n + 1], g[l].rearrange("(d o) -> d o", o=1)).then_inc(gl, 16)
                    sp.wait_ge(gl, 64)

                @block.gpsimd
                def _(pool):
                    pool.wait_ge(bl, 16 + 32 * NA_HEADS)
                    with pool.Fori(0, NA_HEADS // 2) as i:
                        pool.wait_ge(a.maxed, i * U)
                        for h in range(2):
                            last = nc.gpsimd.tensor_tensor(bst[:, h], bias[:, ds(2 * i + h, 1), :].rearrange("p o (j k) -> p (o j) k", k=GRID_W),
                                                           colmask[:].unsqueeze(1).to_broadcast([P, 14, GRID_W]), ALU.add)
                        last.then_inc(based, 1)

                @block.tensor
                def _(pe):
                    with pe.Fori(0, NA_HEADS // 2) as i:
                        pe.wait_ge(a.kept_lo, i * U)
                        pe.wait_ge(a.kept_hi, i * U)
                        pe.wait_ge(a.o_kept, i)
                        for n, (x, bank) in enumerate(((qst, 4), (kst, 6))):
                            pe.wait_ge(a.staged, 2 * i + n + 1)
                            for t in range(x.shape[1]):
                                o = ps[:, bank, t * P:(t + 1) * P] if t < NL else ps[:, bank + 1, (t - NL) * P:(t - NL + 1) * P]
                                mm = nc.tensor.transpose(o, x[:, t].rearrange("p h d -> p (h d)"), ident[:])
                            mm.then_inc(a.q_turned, 1)
                        pe.wait_ge(a.qk_kept, 2 * i + 2)

                        def scores(hh, t, bank):
                            r = slice(hh * 64, (hh + 1) * 64)
                            if t < NL:
                                nc.tensor.matmul(ps[:, bank, 0:S], qT[r, t * P:(t + 1) * P], kT[r, 0:S], start=True, stop=True)
                            return nc.tensor.matmul(ps[:, bank + 1, 0:L], qT[r, t * P:(t + 1) * P], kT[r, S:T], start=True, stop=True)

                        a.pe_units(pe, i, scores, lambda hh, k: proj[:, k, ds(C_NAV + (2 * i + hh) * 64, 64)])

                @block.vector
                def _(dve):
                    dve.wait_ge(gl, 64)
                    nc.vector.tensor_scalar(gain[:, 0:1], gain[:, 0:1], NA_DIM ** -0.5, None, ALU.mult).then_inc(gained, 1)
                    STEPS = 2 * NL + a.U
                    with dve.Fori(0, NA_HEADS // 2) as i:
                        chain = Chain(dve, a.chain, i * STEPS)
                        dve.wait_ge(a.q_turned, 2 * i)
                        for n, (x, nt) in enumerate(((qst, nq), (kst, NT))):
                            nc.vector.tensor_tensor(x[:].rearrange("p t h d -> p t h d"),
                                                    proj[:, 0:nt, ds(n * NA_W + i * P, P)].rearrange("p t (h d) -> p t h d", d=64),
                                                    stat[:, 0:nt, ds(R_NA + 6 * n + 2 * i, 2)].unsqueeze(3).to_broadcast([P, nt, 2, 64]),
                                                    ALU.mult).then_inc(a.staged, 1)
                        dve.wait_ge(based, i + 1)

                        def maximum(hh, t, bank, s):
                            m = a.rowmax[:, s]
                            if t >= NL:
                                return nc.vector.tensor_reduce(m[:, 3:4], ps[:, bank + 1, 0:L], AX.X, ALU.max, negate=True)
                            j0 = 6 - 2 * t
                            nc.vector.tensor_scalar(score[s][:, S:T], ps[:, bank + 1, 0:L], 0.0, 3 * MASKED,
                                                    ALU.add, ALU.max, accum_out=m[:, 0:1])
                            chain.link(nc.vector.tensor_tensor_reduce(
                                score[s][:, 0:S], ps[:, bank, 0:S], bst[:, hh, j0:j0 + 8, :].rearrange("p j k -> p (j k)"),
                                1.0, 3 * MASKED, ALU.add, ALU.max, m[:, 1:2]))
                            return nc.vector.tensor_reduce(m[:, 3:4], m[:, 0:2], AX.X, ALU.max, negate=True)

                        a.dve_units(dve, i, chain, maximum)
                        assert chain.n == STEPS, chain.n

                @block.scalar
                def _(act):
                    act.wait_ge(gained, 1)
                    with act.Fori(0, NA_HEADS // 2) as i:
                        for n, (xT_, bank, w) in enumerate(((qT, 4, nq * P), (kT, 6, T))):
                            act.wait_ge(a.q_turned, 2 * i + n + 1)
                            last = nc.scalar.mul(xT_[:, 0:S], ps[:, bank, 0:S], gain[:, n:n + 1])
                            if w > S:
                                last = nc.scalar.mul(xT_[:, S:T], ps[:, bank + 1, 0:L], gain[:, n:n + 1])
                            last.then_inc(a.qk_kept, 1)
                        a.act_units(act, i, lambda t, bank, s: score[s][:] if t < NL else ps[:, bank + 1, 0:L], oT)

        def windowed(l, proj, stat, oT, last_layer):
            nq = NL if last_layer else NT
            G = SWA_HEADS // SWA_KV_HEADS
            near = lambda t: list(range(max(t - 1, 0), min(t + 2, NL)))
            keys_of = lambda t: (near(t) if t < NL else []) + list(range(NL, NT))
            with Scope() as st:
                a = Attention(st, "sw", 2, SWA_DIM, list(range(nq)), keys_of)
                band = sb(st, "band", [P, 3 * P])
                cg, sg = [sb(st, f"sw_cos{n}", [P, NT, 64]) for n in range(2)], [sb(st, f"sw_sin{n}", [P, NT, 64]) for n in range(2)]
                g = [sb(st, f"sw_gain{n}", [P, 64]) for n in range(2)]
                sink, sink2 = sb(st, "sink", [P, SWA_HEADS]), sb(st, "sink_pair", [P, 2])
                raw, part, turn = (sb(st, f"sw_{q}", [P, NT, 2, 64]) for q in ("raw", "part", "roped"))
                qT, kT = sb(st, "sw_qT", [P, T]), sb(st, "sw_kT", [P, T])
                score = [sb(st, f"sw_scores{s}", [P, T]) for s in range(2)]
                gl = sem(st, "sw_consts_loaded")
                block = st.enter_context(nc.Block())
                U = a.U

                @block.sync
                def _(sp):
                    sp.dma_start(band[:], const["band"]).then_inc(gl, 16)
                    for n, v in enumerate((swa_q_g, swa_k_g)):
                        sp.dma_start(g[n][:], v[l:l + 1, :].to_broadcast([P, 64])).then_inc(gl, 16)
                    sp.dma_start(sink[:], swa_sink[l:l + 1, :].to_broadcast([P, SWA_HEADS])).then_inc(gl, 16)
                    sp.wait_ge(gl, 64)

                def turned(pe, nt):
                    for t in range(nt):
                        o = ps[:, 4, t * P:(t + 1) * P] if t < NL else ps[:, 5, (t - NL) * P:(t - NL + 1) * P]
                        mm = nc.tensor.transpose(o, turn[:, t].rearrange("p h d -> p (h d)"), ident[:])
                    mm.then_inc(a.q_turned, 1)

                @block.tensor
                def _(pe):
                    pe.wait_ge(a.staged, 1)
                    turned(pe, NT)
                    pe.wait_ge(a.qk_kept, 1)
                    with pe.Fori(0, G) as i:
                        pe.wait_ge(a.kept_lo, i * U)
                        pe.wait_ge(a.kept_hi, i * U)
                        pe.wait_ge(a.o_kept, i)
                        pe.wait_ge(a.staged, i + 2)
                        turned(pe, nq)
                        pe.wait_ge(a.qk_kept, i + 2)

                        def scores(hh, t, bank):
                            r = slice(hh * 64, (hh + 1) * 64)
                            if t < NL:
                                k = near(t)
                                nc.tensor.matmul(ps[:, bank, 0:len(k) * P], qT[r, t * P:(t + 1) * P],
                                                 kT[r, k[0] * P:(k[-1] + 1) * P], start=True, stop=True)
                            return nc.tensor.matmul(ps[:, bank + 1, 0:L], qT[r, t * P:(t + 1) * P], kT[r, S:T], start=True, stop=True)

                        a.pe_units(pe, i, scores, lambda hh, k: proj[:, k, C_SV + hh * 64:C_SV + (hh + 1) * 64])

                @block.vector
                def _(dve):
                    pre = Chain(dve, gl, 64)
                    dve.wait_ge(gl, 64)
                    rope_tables(pre, cg[0], sg[0], g[0], SWA_DIM ** -0.5)
                    rope_tables(pre, cg[1], sg[1], g[1], 1.0)
                    pre.link(nc.vector.tensor_tensor(raw[:], proj[:, :, C_SK:C_SV].rearrange("p t (h d) -> p t h d", d=64),
                                                     stat[:, :, R_SW + 6:R_SW + 8].unsqueeze(3).to_broadcast([P, NT, 2, 64]), ALU.mult))
                    rope(pre, turn[:], raw[:], part[:], cg[1], sg[1], NT, 2).then_inc(a.staged, 1)
                    STEPS = 2 + 3 * a.U
                    with dve.Fori(0, G) as i:
                        chain = Chain(dve, a.chain, i * STEPS)
                        q = proj[:, 0:nq, C_SQ:C_SK].rearrange("p t (g j) -> p t g j", g=2)
                        r = stat[:, 0:nq, R_SW:R_SW + 6].rearrange("p t (g j) -> p t g j", g=2)
                        nc.vector.tensor_copy(sink2[:], sink[:].rearrange("p (g j) -> p g j", g=2)[:, :, ds(i, 1)].rearrange("p g j -> p (g j)"))
                        chain.link(nc.vector.tensor_tensor(raw[:, 0:nq], q[:, :, :, ds(i * 64, 64)],
                                                           r[:, :, :, ds(i, 1)].to_broadcast([P, nq, 2, 64]), ALU.mult))
                        dve.wait_ge(a.q_turned, i + 1)
                        rope(chain, turn[:, 0:nq], raw[:, 0:nq], part[:, 0:nq], cg[0], sg[0], nq, 2).then_inc(a.staged, 1)

                        def maximum(hh, t, bank, s):
                            m = a.rowmax[:, s]
                            k = near(t) if t < NL else []
                            n = len(k) * P
                            last = nc.vector.tensor_scalar(score[s][:, n:n + L], ps[:, bank + 1, 0:L], 0.0, sink2[:, hh:hh + 1],
                                                           ALU.add, ALU.max, accum_out=m[:, 0:1])
                            if k:
                                b0 = (k[0] - t + 1) * P
                                last = nc.vector.tensor_tensor_reduce(score[s][:, 0:n], ps[:, bank, 0:n], band[:, b0:b0 + n],
                                                                      1.0, 3 * MASKED, ALU.add, ALU.max, m[:, 1:2])
                            chain.link(last)
                            return nc.vector.tensor_reduce(m[:, 3:4], m[:, 0:2 if k else 1], AX.X, ALU.max, negate=True)

                        a.dve_units(dve, i, chain, maximum, True)
                        assert chain.n == STEPS, (chain.n, STEPS)

                @block.scalar
                def _(act):
                    act.wait_ge(a.q_turned, 1)
                    nc.scalar.copy(kT[:, 0:S], ps[:, 4, 0:S])
                    nc.scalar.copy(kT[:, S:T], ps[:, 5, 0:L]).then_inc(a.qk_kept, 1)
                    with act.Fori(0, G) as i:
                        act.wait_ge(a.q_turned, i + 2)
                        last = nc.scalar.copy(qT[:, 0:S], ps[:, 4, 0:S])
                        if nq > NL:
                            last = nc.scalar.copy(qT[:, S:T], ps[:, 5, 0:L])
                        last.then_inc(a.qk_kept, 1)

                        def sink_exp(hh, u):
                            nc.scalar.activation(a.rowsum[:, u % 4, 2:3], sink2[:, hh:hh + 1], ACT.Exp, bias=a.rowmax[:, u % 2, 3:4])

                        a.act_units(act, i, lambda t, bank, s: score[s][:, 0:len(keys_of(t)) * P], oT, sink_exp)

        def latent(l, proj, stat, oT, last_layer):
            nq = NL if last_layer else NT
            keys_of = lambda t: (list(range(NL)) if t < NL else []) + list(range(NL, NT))
            QC = MLA_Q_RANK // P
            with Scope() as st:
                a = Attention(st, "mla", 1, MLA_V, list(range(nq)), keys_of)
                wuq, wukv = sb(st, "w_uq", [P, QC, MLA_HEADS * MLA_QK]), sb(st, "w_ukv", [P, MLA_HEADS * 256])
                cg, sg = [sb(st, f"mla_cos{n}", [P, NT, 64]) for n in range(2)], [sb(st, f"mla_sin{n}", [P, NT, 64]) for n in range(2)]
                g = [sb(st, f"mla_gain{n}", [P, 64]) for n in range(2)]
                gain = sb(st, "mla_gains", [P, 2 + QC + 1])
                shared = sb(st, "mla_shared", [P, max(NT * (QC + 1) * P, (NT + nq) * MLA_QK)])
                rank = shared[:, 0:NT * (QC + 1) * P].rearrange("p (t w) -> p t w", t=NT)
                sq = shared[:, 0:NT * MLA_QK].rearrange("p (t w) -> p t w", t=NT)
                qst = shared[:, NT * MLA_QK:(NT + nq) * MLA_QK].rearrange("p (t w) -> p t w", t=nq)
                cT_ = sb(st, "rank_T", [P, QC + 1, T])
                krope = sb(st, "k_roped", [P, NT, 1, 64])
                kst, vst = sb(st, "mla_k", [P, NT, P]), sb(st, "mla_v", [P, NT, P])
                part, kr = sq[:, :, 0:64].unsqueeze(2), sq[:, :, P:MLA_QK]
                r2 = sb(st, "mla_rstd", [P, 2, NT])
                qr = sb(st, "mla_q_rope", [P, nq, 1, 64])
                qT, kT = sb(st, "mla_qT", [P, T]), sb(st, "mla_kT", [P, T])
                qrT, krT = sb(st, "mla_qrT", [64, T]), sb(st, "mla_krT", [64, T])
                gl, wl, rt, root, upped, unpacked = (sem(st, q) for q in ("mla_consts_loaded", "w_u_loaded", "ranks_turned", "mla_root", "upped", "unpacked"))
                rk = [sem(st, "ranks_kept_act"), sem(st, "ranks_kept_dve")]
                kept_k = sem(st, "k_kept")
                block = st.enter_context(nc.Block())
                U = a.U
                ctx_kept = lambda q: sum(1 for c in range(q + 1) if c == QC or nq > NL)

                @block.sync
                def _(sp):
                    col = lambda v: v.rearrange("(d o) -> d o", o=1)
                    sp.dma_start(gain[:, 0:1], col(mla_q_g[l, 0:P])).then_inc(gl, 16)
                    sp.dma_start(gain[:, 1:2], col(mla_k_g[l, 0:P])).then_inc(gl, 16)
                    for q in range(QC):
                        sp.dma_start(gain[:, 2 + q:3 + q], col(mla_q_norm[l, q * P:(q + 1) * P])).then_inc(gl, 16)
                    sp.dma_start(gain[:, 2 + QC:3 + QC], col(mla_kv_norm[l])).then_inc(gl, 16)
                    for n, v in enumerate((mla_q_g, mla_k_g)):
                        sp.dma_start(g[n][:], v[l:l + 1, P:MLA_QK].to_broadcast([P, 64])).then_inc(gl, 16)
                    sp.dma_start(wuq[:], mla_w_uq[l].rearrange("(k p) n -> p k n", p=P)).then_inc(wl, 16)
                    sp.dma_start(wukv[:], mla_w_ukv[l]).then_inc(wl, 16)
                    sp.wait_ge(gl, 16 * (5 + QC))

                @block.tensor
                def _(pe):
                    pe.wait_ge(a.staged, 1)
                    for q in range(QC + 1):
                        b = 2 * (q % 2)
                        if q >= 2:
                            pe.wait_ge(rk[0], q - 1)
                            if ctx_kept(q - 2):
                                pe.wait_ge(rk[1], ctx_kept(q - 2))
                        for t in range(nq if q < QC else NT):
                            mm = nc.tensor.transpose(ps[:, b + t // NL, (t % NL) * P:(t % NL + 1) * P],
                                                     rank[:, t, q * P:(q + 1) * P], ident[:])
                        mm.then_inc(rt, 1)
                    pe.wait_ge(wl, 32)
                    pe.wait_ge(rk[0], QC + 1)
                    pe.wait_ge(rk[1], ctx_kept(QC))
                    with pe.Fori(0, MLA_HEADS) as i:
                        pe.wait_ge(a.exped, i * U)
                        pe.wait_ge(a.kept_lo, i * U)
                        pe.wait_ge(a.kept_hi, i * U)
                        pe.wait_ge(a.o_kept, i)
                        for t in range(nq):
                            for q in range(QC):
                                mm = nc.tensor.matmul(ps[:, t // 2, (t % 2) * MLA_QK:(t % 2 + 1) * MLA_QK],
                                                      cT_[:, q, t * P:(t + 1) * P], wuq[:, q, ds(i * MLA_QK, MLA_QK)],
                                                      start=(q == 0), stop=(q == QC - 1))
                        mm.then_inc(upped, 1)
                        for t in range(NT):
                            mm = nc.tensor.matmul(ps[:, 3 + t // 2, (t % 2) * 256:(t % 2 + 1) * 256],
                                                  cT_[:, QC, t * P:(t + 1) * P], wukv[:, ds(i * 256, 256)], start=True, stop=True)
                        mm.then_inc(upped, 1)
                        pe.wait_ge(unpacked, 2 * i + 2)
                        for n, (x, bank) in enumerate(((qst[:, :, 0:P], 4), (kst[:], 6), (qr[:, :, 0, :], 0), (kr, 2))):
                            if n < 2:
                                pe.wait_ge(a.staged, 4 * i + (2, 5)[n])
                            w = x.shape[2]
                            for t in range(x.shape[1]):
                                mm = nc.tensor.transpose(ps[0:w, bank + t // NL, (t % NL) * P:(t % NL + 1) * P], x[:, t, :], ident[:])
                            mm.then_inc(a.q_turned, 1)
                        pe.wait_ge(a.qk_kept, 2 * i + 2)
                        pe.wait_ge(kept_k, 2 * i + 2)

                        def scores(hh, t, bank):
                            q0 = slice(t * P, (t + 1) * P)
                            for b, c0, n in ([(bank, 0, S)] if t < NL else []) + [(bank + 1, S, L)]:
                                nc.tensor.matmul(ps[:, b, 0:n], qT[:, q0], kT[:, c0:c0 + n], start=True, stop=False)
                                mm = nc.tensor.matmul(ps[:, b, 0:n], qrT[:, q0], krT[:, c0:c0 + n], start=False, stop=True)
                            return mm

                        a.pe_units(pe, i, scores, lambda hh, k: vst[:, k, :])

                @block.vector
                def _(dve):
                    pre = Chain(dve, gl, 16 * (5 + QC))
                    dve.wait_ge(gl, 16 * (5 + QC))
                    pre.link(nc.vector.tensor_scalar(gain[:, 0:1], gain[:, 0:1], MLA_QK ** -0.5, None, ALU.mult))
                    rope_tables(pre, cg[0], sg[0], g[0], MLA_QK ** -0.5)
                    rope_tables(pre, cg[1], sg[1], g[1], 1.0)
                    for t in range(NT):
                        if t < nq:
                            nc.vector.tensor_scalar(rank[:, t, 0:QC * P], proj[:, t, C_CQ:C_CKV], stat[:, t, R_CQ:R_CQ + 1], None, ALU.mult)
                        last = nc.vector.tensor_scalar(rank[:, t, QC * P:], proj[:, t, C_CKV:C_KR], stat[:, t, R_CKV:R_CKV + 1], None, ALU.mult)
                    last.then_inc(a.staged, 1)
                    rope(pre, krope[:], proj[:, :, C_KR:C_SQ].rearrange("p t (o d) -> p t o d", o=1), vst[:, :, 0:64].unsqueeze(2), cg[1], sg[1], NT, 1)\
                        .then_inc(gl, 1)
                    pre.n += 1
                    for q in range(QC + 1):
                        dve.wait_ge(rt, q + 1)
                        b = 2 * (q % 2)
                        if q == QC or nq > NL:
                            nc.vector.tensor_scalar(cT_[:, q, S:T], ps[:, b + 1, 0:L], gain[:, 2 + q:3 + q], None, ALU.mult).then_inc(rk[1], 1)
                    dve.wait_ge(gl, 16 * (5 + QC) + pre.n)
                    dve.wait_ge(rk[1], ctx_kept(QC))
                    STEPS = 7 + a.U
                    with dve.Fori(0, MLA_HEADS) as i:
                        chain = Chain(dve, a.chain, i * STEPS)
                        dve.wait_ge(upped, 2 * i + 2)
                        for b in range(3):
                            kv = ps[:, 3 + b, :].rearrange("p (t w) -> p t w", w=256)
                            nc.vector.tensor_copy(kst[:, 2 * b:2 * b + 2, :], kv[:, :, 0:P])
                            last = nc.vector.tensor_copy(vst[:, 2 * b:2 * b + 2, :], kv[:, :, P:256])
                        last.then_inc(unpacked, 1)
                        chain.link(nc.vector.tensor_copy(r2[:, 0], stat[:, :, 0]))
                        dve.wait_ge(unpacked, 2 * i + 2)
                        chain.link(nc.vector.tensor_tensor(sq[:, 0:nq, :], qst, qst, ALU.mult))
                        chain.link(nc.vector.tensor_reduce(r2[:, 0, 0:nq], sq[:, 0:nq, :], AX.X, ALU.add))
                        chain.link(nc.vector.tensor_tensor(sq[:, :, 0:P], kst[:], kst[:], ALU.mult))
                        chain.link(nc.vector.tensor_reduce(r2[:, 1], sq[:, :, 0:P], AX.X, ALU.add))
                        chain.link(nc.vector.tensor_tensor(r2[:, 1], r2[:, 1], stat[:, :, R_KR], ALU.add))
                        nc.vector.tensor_scalar(r2[:], r2[:], 1.0 / MLA_QK, EPS, ALU.mult, ALU.add).then_inc(root, 1)
                        dve.wait_ge(root, 3 * i + 2)
                        nc.vector.reciprocal(r2[:], r2[:]).then_inc(root, 1)
                        dve.wait_ge(root, 3 * i + 3)
                        nc.vector.tensor_tensor(kst[:], kst[:], r2[:, 1].unsqueeze(2).to_broadcast([P, NT, P]), ALU.mult)
                        nc.vector.tensor_tensor(kr, krope[:, :, 0, :], r2[:, 1].unsqueeze(2).to_broadcast([P, NT, 64]), ALU.mult)
                        nc.vector.tensor_tensor(qst, qst, r2[:, 0, 0:nq].unsqueeze(2).to_broadcast([P, nq, MLA_QK]), ALU.mult).then_inc(a.staged, 1)
                        dve.wait_ge(a.staged, 4 * i + 2)
                        rope(chain, qr[:], qst[:, :, P:MLA_QK].unsqueeze(2), part[:, 0:nq], cg[0], sg[0], nq, 1).then_inc(a.staged, 3)
                        for n, (w, x_, bank) in enumerate(((P, kT, 6), (64, krT, 2))):
                            dve.wait_ge(a.q_turned, 4 * i + 2 * n + 2)
                            for c0, m, b in ((0, S, bank), (S, L, bank + 1)):
                                if n == 0:
                                    last = nc.vector.tensor_scalar(x_[:, c0:c0 + m], ps[:, b, 0:m], gain[:, 1:2], None, ALU.mult)
                                else:
                                    last = nc.vector.tensor_copy(x_[:, c0:c0 + m], ps[0:w, b, 0:m])
                            last.then_inc(kept_k, 1)

                        def maximum(hh, t, bank, s):
                            src = ps[:, bank:bank + 2, :].rearrange("p a b -> p (a b)")[:, 0:T] if t < NL else ps[:, bank + 1, 0:L]
                            return nc.vector.tensor_reduce(a.rowmax[:, s, 3:4], src, AX.X, ALU.max, negate=True)

                        a.dve_units(dve, i, chain, maximum)
                        assert chain.n == STEPS, chain.n

                @block.scalar
                def _(act):
                    for q in range(QC + 1):
                        act.wait_ge(rt, q + 1)
                        if q == 0:
                            act.wait_ge(gl, 16 * (5 + QC))
                        nc.scalar.mul(cT_[:, q, 0:S], ps[:, 2 * (q % 2), 0:S], gain[:, 2 + q:3 + q]).then_inc(rk[0], 1)
                    with act.Fori(0, MLA_HEADS) as i:
                        act.wait_ge(upped, 2 * i + 1)
                        for b in range(nq // 2):
                            last = nc.scalar.copy(qst[:, 2 * b:2 * b + 2, :], ps[:, b, 0:2 * MLA_QK].rearrange("p (t w) -> p t w", w=MLA_QK))
                        last.then_inc(unpacked, 1)
                        act.wait_ge(root, 3 * i + 1)
                        nc.scalar.activation(r2[:], r2[:], ACT.Sqrt).then_inc(root, 1)
                        for n, (w, x_, bank) in enumerate(((P, qT, 4), (64, qrT, 0))):
                            act.wait_ge(a.q_turned, 4 * i + 2 * n + 1)
                            for c0, m, b in ((0, S, bank), (S, L, bank + 1))[:1 if nq == NL else 2]:
                                if n == 0:
                                    last = nc.scalar.mul(x_[:, c0:c0 + m], ps[:, b, 0:m], gain[:, 0:1])
                                else:
                                    last = nc.scalar.copy(x_[:, c0:c0 + m], ps[0:w, b, 0:m])
                            last.then_inc(a.qk_kept, 1)
                        a.act_units(act, i, lambda t, bank, s: ps[:, bank:bank + 2, :].rearrange("p a b -> p (a b)")[:, 0:T]
                                    if t < NL else ps[:, bank + 1, 0:L], oT)

        def merge(l, hT, oT, mT, ctx_too):
            W = T if ctx_too else S
            rows = ((w_na_o, 0, 3), (w_mla_o, 6, 4), (w_swa_o, 3, 3))
            RAW, SPLIT = 3, 2
            with Scope() as st:
                h_hi, h_lo = (sb(st, f"hm_{q}", [P, KD, W], F32R) for q in ("hi", "lo"))
                wg = [sb(st, f"w_gates{s}", [P, KD, P]) for s in range(RAW)]
                w_hi, w_lo = ([sb(st, f"w_gates_{q}{s}", [P, KD, P], F32R) for s in range(SPLIT)] for q in ("hi", "lo"))
                wy = [sb(st, f"w_branch{s}", [P, 10, P]) for s in range(2)]
                sig = [sb(st, f"gate{s}", [P, W]) for s in range(2)]
                prod = sb(st, "gated", [P, W])
                gl = [sem(st, f"w_gates_loaded{s}") for s in range(RAW)]
                yl = [sem(st, f"w_branch_loaded{s}") for s in range(2)]
                h_hi_made, h_lo_made, w_hi_made, w_lo_made = (sem(st, "merge_" + q) for q in ("h_hi", "h_lo", "w_hi", "w_lo"))
                logits, ys, sigs, gated, ch = (sem(st, q) for q in ("logits", "branch_out", "gates", "gated", "merge_chain"))
                block = st.enter_context(nc.Block())
                UN = 2 * 3
                NI = KD // 2
                units = [(dc, b) for dc in range(2) for b in range(3)]

                @block.sync
                def _(sp):
                    def load(i, u):
                        dc, b = units[u]
                        n = i * UN + u
                        c0 = i * 2 * P + dc * P
                        if b == 0:
                            if not isinstance(i, int):
                                sp.wait_ge(ys, n - 3)
                            for w, q0, nq in rows[:2]:
                                sp.dma_start(wy[dc][:, q0:q0 + nq], w[l].rearrange("(k p) n -> p k n", p=P)[:, :, ds(c0, P)]).then_inc(yl[dc], 16)
                            for g in range(2):
                                sp.dma_start(wy[dc][g * 64:(g + 1) * 64, 3:6],
                                             w_swa_o[l].rearrange("(g j d) n -> g d j n", g=2, d=64)[g][:, :, ds(c0, P)]).then_inc(yl[dc], 16)
                        if not isinstance(i, int) or u >= RAW:
                            sp.wait_ge(w_lo_made, n - RAW + 1)
                        sp.dma_start(wg[u % RAW][:], w_in[l].rearrange("(k p) n -> p k n", p=P)[:, :, ds(C_GL + b * D + c0, P)]).then_inc(gl[u % RAW], 16)
                    for u in range(UN):
                        load(0, u)
                    with sp.Fori(1, NI) as i:
                        for u in range(UN):
                            load(i, u)

                @block.tensor
                def _(pe):
                    with pe.Fori(0, NI) as i:
                        for u, (dc, b) in enumerate(units):
                            n = i * UN + u
                            pe.wait_ge(gated, n - 1 if u >= 1 else n)
                            pe.wait_ge(w_hi_made, n + 1)
                            pe.wait_ge(w_lo_made, n + 1)
                            b0 = 4 * (u % 2)
                            for k in range(KD):
                                if u == 0:
                                    pe.wait_ge(h_hi_made, k + 1)
                                    pe.wait_ge(h_lo_made, k + 1)
                                for w, h in ((w_hi, h_hi), (w_hi, h_lo), (w_lo, h_hi)):
                                    for z, t0, m in streams(ctx_too):
                                        mm = nc.tensor.matmul(ps[:, b0 + z, 0:m], w[u % SPLIT][:, k, :], h[:, k, t0:t0 + m],
                                                              start=(k == 0 and w is w_hi and h is h_hi), stop=(k == KD - 1 and w is w_lo))
                            mm.then_inc(logits, 1)
                            if b == 0:
                                pe.wait_ge(yl[dc], 64 * i + 64)
                            _, q0, nq = rows[b]
                            for z, t0, m in streams(ctx_too):
                                for q in range(nq):
                                    mm = nc.tensor.matmul(ps[:, b0 + 2 + z, 0:m], wy[dc][:, q0 + q, :], oT[:, q0 + q, t0:t0 + m],
                                                          start=(q == 0), stop=(q == nq - 1))
                            mm.then_inc(ys, 1)

                @block.scalar
                def _(act):
                    for k in range(KD):
                        nc.scalar.copy(h_hi[:, k, :], hT[:, k, 0:W]).then_inc(h_hi_made, 1)
                    with act.Fori(0, NI) as i:
                        for u in range(UN):
                            n = i * UN + u
                            act.wait_ge(gl[u % RAW], 16 * (UN // RAW * i + u // RAW + 1))
                            act.wait_ge(logits, n - 1 if u >= 1 else n)
                            nc.scalar.copy(w_hi[u % SPLIT][:], wg[u % RAW][:]).then_inc(w_hi_made, 1)
                            act.wait_ge(logits, n + 1)
                            act.wait_ge(gated, n - 1 if u >= 1 else n)
                            for z, t0, m in streams(ctx_too):
                                last = nc.scalar.activation(sig[u % 2][:, t0:t0 + m], ps[:, 4 * (u % 2) + z, 0:m], ACT.Sigmoid)
                            last.then_inc(sigs, 1)

                @block.vector
                def _(dve):
                    for k in range(KD):
                        dve.wait_ge(h_hi_made, k + 1)
                        nc.vector.tensor_tensor(h_lo[:, k, :], hT[:, k, 0:W], h_hi[:, k, :].bitcast(F32), ALU.subtract).then_inc(h_lo_made, 1)
                    STEPS = 4
                    with dve.Fori(0, NI) as i:
                        chain = Chain(dve, ch, i * STEPS)

                        def split(u):
                            dve.wait_ge(w_hi_made, i * UN + u + 1)
                            nc.vector.tensor_tensor(w_lo[u % SPLIT][:], wg[u % RAW][:], w_hi[u % SPLIT][:].bitcast(F32), ALU.subtract).then_inc(w_lo_made, 1)

                        def gate(u):
                            dc, b = units[u]
                            dve.wait_ge(sigs, i * UN + u + 1)
                            dve.wait_ge(ys, i * UN + u + 1)
                            m_ = mT[:, ds(2 * i + dc, 1), :].rearrange("p o t -> p (o t)")
                            if b > 0:
                                dve.wait_ge(gated, i * UN + u)
                            for z, t0, m in streams(ctx_too):
                                last = nc.vector.tensor_tensor(m_[:, t0:t0 + m] if b == 0 else prod[:, t0:t0 + m], sig[u % 2][:, t0:t0 + m],
                                                               ps[:, 4 * (u % 2) + 2 + z, 0:m], ALU.mult)
                            if b > 0:
                                chain.link(last)
                                last = nc.vector.tensor_tensor(m_[:, 0:W], m_[:, 0:W], prod[:], ALU.add)
                            last.then_inc(gated, 1)

                        for u in range(UN):
                            split(u)
                            if u >= 1:
                                gate(u - 1)
                        gate(UN - 1)
                        assert chain.n == STEPS

        def output_projection(l, mT, ctx_too):
            W = T if ctx_too else S
            RAW, SPLIT = 3, 2
            with Scope() as st:
                m_hi, m_lo = (sb(st, f"m_{q}", [P, KD, W], F32R) for q in ("hi", "lo"))
                w = [sb(st, f"w_o{s}", [P, KD, P]) for s in range(RAW)]
                w_hi, w_lo = ([sb(st, f"w_o_{q}{s}", [P, KD, P], F32R) for s in range(SPLIT)] for q in ("hi", "lo"))
                wl = [sem(st, f"w_o_loaded{s}") for s in range(RAW)]
                m_hi_made, m_lo_made, w_hi_made, w_lo_made = (sem(st, "w_o_" + q) for q in ("m_hi", "m_lo", "w_hi", "w_lo"))
                multiplied, added = sem(st, "w_o_multiplied"), sem(st, "w_o_added")
                block = st.enter_context(nc.Block())

                @block.sync
                def _(sp):
                    for d in range(KD):
                        if d >= RAW:
                            sp.wait_ge(w_lo_made, d - RAW + 1)
                        sp.dma_start(w[d % RAW][:], w_o[l].rearrange("(k p) n -> p k n", p=P)[:, :, d * P:(d + 1) * P]).then_inc(wl[d % RAW], 16)

                @block.tensor
                def _(pe):
                    for d in range(KD):
                        if d >= 2:
                            pe.wait_ge(added, d - 1)
                        pe.wait_ge(w_hi_made, d + 1)
                        pe.wait_ge(w_lo_made, d + 1)
                        for k in range(KD):
                            if d == 0:
                                pe.wait_ge(m_hi_made, k + 1)
                                pe.wait_ge(m_lo_made, k + 1)
                            for w_, x in ((w_hi, m_hi), (w_hi, m_lo), (w_lo, m_hi)):
                                for z, t0, m in streams(ctx_too):
                                    mm = nc.tensor.matmul(ps[:, 2 * (d % 2) + z, 0:m], w_[d % SPLIT][:, k, :], x[:, k, t0:t0 + m],
                                                          start=(k == 0 and w_ is w_hi and x is m_hi), stop=(k == KD - 1 and w_ is w_lo))
                        mm.then_inc(multiplied, 1)

                @block.scalar
                def _(act):
                    def round_(d):
                        act.wait_ge(wl[d % RAW], 16 * (d // RAW + 1))
                        if d >= SPLIT:
                            act.wait_ge(multiplied, d - SPLIT + 1)
                        nc.scalar.copy(w_hi[d % SPLIT][:], w[d % RAW][:]).then_inc(w_hi_made, 1)

                    for k in range(KD):
                        nc.scalar.copy(m_hi[:, k, :], mT[:, k, 0:W]).then_inc(m_hi_made, 1)
                        if k in (3, 4):
                            round_(k - 3)
                    for d in range(SPLIT, KD):
                        round_(d)

                @block.vector
                def _(dve):
                    def add(d):
                        dve.wait_ge(multiplied, d + 1)
                        for z, t0, m in streams(ctx_too):
                            last = nc.vector.scalar_tensor_tensor(xT[:, d, t0:t0 + m], ps[:, 2 * (d % 2) + z, 0:m],
                                                                  modT[:, 2 * KD + d, z:z + 1], xT[:, d, t0:t0 + m], ALU.mult, ALU.add)
                        last.then_inc(added, 1)

                    def split(d):
                        dve.wait_ge(w_hi_made, d + 1)
                        nc.vector.tensor_tensor(w_lo[d % SPLIT][:], w[d % RAW][:], w_hi[d % SPLIT][:].bitcast(F32), ALU.subtract).then_inc(w_lo_made, 1)

                    for k in range(KD):
                        dve.wait_ge(m_hi_made, k + 1)
                        nc.vector.tensor_tensor(m_lo[:, k, :], mT[:, k, 0:W], m_hi[:, k, :].bitcast(F32), ALU.subtract).then_inc(m_lo_made, 1)
                        if k in (3, 4):
                            split(k - 3)
                    for d in range(SPLIT, KD):
                        split(d)
                        add(d - SPLIT)
                    for d in range(KD - SPLIT, KD):
                        add(d)

        def route(l, h2T, h2, posm, posT, affT, ctx_too):
            nt = NT if ctx_too else NL
            E = N_EXPERTS
            with Scope() as st:
                wr = sb(st, "router", [P, KD, E])
                aff = sb(st, "affinity", [P, nt, E])
                small = sb(st, "route_small", [P, 2, nt])
                left = sb(st, "left", [E, T])
                top8 = sb(st, "top8", [E, 8])
                zero = sb(st, "zero", [E, S])
                wl, lg, ch, ex, at, hk, ht, kept, pt, zs = (sem(st, q) for q in (
                    "router_loaded", "logits", "route_chain", "aff_exp", "aff_turned", "tokens_kept", "tokens_turned", "aff_kept", "pos_turned", "zeroed"))
                block = st.enter_context(nc.Block())

                @block.sync
                def _(sp):
                    sp.dma_start(wr[:], router[l].rearrange("(k p) e -> p k e", p=P)).then_inc(wl, 16)
                    sp.wait_ge(wl, 16)

                @block.gpsimd
                def _(pool):
                    nc.gpsimd.memset(zero[:], 0.0).then_inc(zs, 1)
                    nc.gpsimd.memset(posm[:], 0.0).then_inc(zs, 1)

                @block.tensor
                def _(pe):
                    pe.wait_ge(wl, 16)
                    for t in range(nt):
                        for k in range(KD):
                            mm = nc.tensor.matmul(ps[:, 0, t * E:(t + 1) * E], h2T[:, k, t * P:(t + 1) * P], wr[:, k, :],
                                                  start=(k == 0), stop=(k == KD - 1))
                    mm.then_inc(lg, 1)

                    def tokens(g):
                        if g >= 4:
                            pe.wait_ge(hk, g - 3)
                        t, half = g // 2, g % 2
                        for q in range(4):
                            k = 4 * half + q
                            mm = nc.tensor.transpose(ps[:, 2 + g % 4, q * P:(q + 1) * P], h2T[:, k, t * P:(t + 1) * P], ident[:])
                        mm.then_inc(ht, 1)
                    for g in range(4):
                        tokens(g)
                    pe.wait_ge(ex, 2)
                    for t in range(nt):
                        mm = nc.tensor.transpose(ps[0:E, 6 + t // NL, (t % NL) * P:(t % NL + 1) * P], aff[:, t, :], ident[:])
                    mm.then_inc(at, 1)
                    for g in range(4, 2 * nt):
                        tokens(g)
                    pe.wait_ge(pt, 1)
                    for t in range(nt):
                        mm = nc.tensor.transpose(ps[:, 0, t * E:(t + 1) * E], posT[:, t * P:(t + 1) * P], ident[0:E, 0:E])
                    mm.then_inc(at, 1)

                @block.scalar
                def _(act):
                    act.wait_ge(ch, 2)
                    nc.scalar.activation(aff[:], aff[:], ACT.Exp).then_inc(ex, 1)
                    for g in range(2 * nt):
                        act.wait_ge(ht, g + 1)
                        nc.scalar.copy(h2[:, g // 2, (g % 2) * 512:(g % 2 + 1) * 512], ps[:, 2 + g % 4, :]).then_inc(hk, 1)

                @block.vector
                def _(dve):
                    chain = Chain(dve, ch)
                    dve.wait_ge(lg, 1)
                    raw = ps[:, 0, 0:nt * E].rearrange("p (t e) -> p t e", e=E)
                    chain.link(nc.vector.tensor_reduce(small[:, 0], raw, AX.X, ALU.max))
                    nc.vector.tensor_tensor(aff[:], raw, small[:, 0].unsqueeze(2).to_broadcast([P, nt, E]), ALU.subtract).then_inc(ch, 1)
                    dve.wait_ge(ex, 1)
                    chain.n += 1
                    chain.link(nc.vector.tensor_reduce(small[:, 0], aff[:], AX.X, ALU.add))
                    chain.link(nc.vector.reciprocal(small[:, 1], small[:, 0]))
                    nc.vector.tensor_tensor(aff[:], aff[:], small[:, 1].unsqueeze(2).to_broadcast([P, nt, E]), ALU.mult).then_inc(ex, 1)
                    dve.wait_ge(at, 1)
                    for z, t0, m in streams(ctx_too):
                        last = nc.vector.tensor_copy(affT[:, t0:t0 + m], ps[0:E, 6 + z, 0:m])
                    chain.link(last)
                    dve.wait_ge(zs, 2)
                    for z, t0, m in streams(ctx_too):
                        cur, rest = affT[:, t0:t0 + m], left[:, t0:t0 + m]
                        chain.link(nc.vector.max(top8[:], cur))
                        chain.link(nc.vector.match_replace(rest, top8[:], cur, -1.0))
                        rounds = (KL, KC)[z] // 8 - 1
                        for _ in range(rounds):
                            chain.link(nc.vector.max(top8[:], rest))
                            chain.link(nc.vector.match_replace(rest, top8[:], rest, -1.0))
                        chain.link(nc.vector.tensor_tensor(rest, rest, cur, ALU.not_equal))
                        p_ = posT[:, t0:t0 + m]
                        chain.link(nc.vector.tensor_tensor_scan(p_, rest, zero[:, 0:m], 0.0, ALU.add, ALU.add))
                        last = nc.vector.tensor_tensor(p_, p_, rest, ALU.mult)
                        chain.link(last)
                    nc.vector.tensor_copy(small[:, 0, 0:1], small[:, 1, 0:1]).then_inc(pt, 1)
                    dve.wait_ge(at, 2)
                    nc.vector.tensor_copy(posm[:, 0:nt, 0:E], ps[:, 0, 0:nt * E].rearrange("p (t e) -> p t e", e=E))

        class Ring:
            UNITS, SLOTS = 24, 6
            ORDER = [(s, j, kh) for s in range(2) for j in range(4) for kh in range(2)] + \
                    [(s, j, kh) for s in range(2) for j in range(4, 6) for kh in range(2)]

            def __init__(self, st):
                self.slot = [sb(st, f"w_expert{j}", [P, KD // 2, 512]) for j in range(self.SLOTS)]
                self.loaded = [sem(st, f"w_expert_loaded{j}") for j in range(self.SLOTS)]

            def load(self, sp, l, chunk, q):
                s, j, kh = self.ORDER[q % self.UNITS]
                w = (w_gate, w_up, w_gate, w_up, w_down, w_down)[j]
                half = (0, 0, 1, 1, 0, 1)[j]
                src = w[l].rearrange("e (k p) n -> p (e k) n", p=P)
                sp.dma_start(self.slot[q % self.SLOTS][:], src[:, ds(chunk[2 * s + kh], KD // 2), half * 512:(half + 1) * 512])\
                    .then_inc(self.loaded[q % self.SLOTS], 16)

        def experts(l, ring, h2, posm, posT, affT, ctx_too):
            E = N_EXPERTS
            M = MS if ctx_too else KL
            W = T if ctx_too else S
            zs_ = streams(ctx_too)
            KZ = (KL, KC)
            Q, AHEAD = ring.UNITS, 3
            with Scope() as st:
                slots, slot_of = sb(st, "slots", [P, KL]), sb(st, "slot_of", [P, 2])
                sel = sb(st, "pick_pair", [E, 2 * MS])
                w_hi, w_lo = ([sb(st, f"w_{q}{s}", [P, KD // 2, 512], F32R) for s in range(AHEAD)] for q in ("hi", "lo"))
                oh = [sb(st, f"one_hot{z}", [P, (S, L)[z] // P, 2, KZ[z]]) for z, _, _ in zs_]
                xg_hi, xg_lo = (sb(st, f"gathered_{q}", [P, KD, 2, M], F32R) for q in ("hi", "lo"))
                act_ = [sb(st, f"hidden{s}", [M, FF]) for s in range(2)]
                aT_hi, aT_lo = ([sb(st, f"hidden_T_{q}{s}", [P, FF // P, M], F32R) for s in range(2)] for q in ("hi", "lo"))
                Y = [sb(st, f"expert_out{z}", [2 * KZ[z], D]) for z, _, _ in zs_]
                affb = sb(st, "affinity_rows", [P, W])
                G = sb(st, "scatter", [P, W])
                consts, picked, one_hot, gathered = (sem(st, "moe_" + q) for q in ("consts_loaded", "picked", "one_hot", "gathered"))
                xg_hi_made, xg_lo_made, w_hi_made, w_lo_made = (sem(st, "moe_" + q) for q in ("xg_hi", "xg_lo", "w_hi", "w_lo"))
                multiplied, silued, hidden, turned = (sem(st, "moe_" + q) for q in ("multiplied", "silued", "hidden", "turned"))
                aT_hi_made, aT_lo_made, y_act, y_dve = (sem(st, "moe_" + q) for q in ("aT_hi", "aT_lo", "y_act", "y_dve"))
                spread, aff_copied, scatter, scattered, added = (sem(st, "moe_" + q) for q in ("spread", "aff_copied", "scatter", "scattered", "added"))
                block = st.enter_context(nc.Block())
                NP = E // 2
                order = [(z, t0, m, d) for d in range(KD) for z, t0, m in zs_]
                NS = len(order)

                def pairs(eng, body):
                    with eng.Fori(0, NP - 1) as i:
                        body(i, Q + AHEAD)
                    body(NP - 1, Q)

                def keep_down(eng, copy, i, s, h, signal):
                    eng.wait_ge(multiplied, Q * i + 16 + 4 * s + 2 * h + 2)
                    for z, _, _ in zs_:
                        k, r0 = KZ[z], KL * z
                        last = copy(Y[z][s * k:(s + 1) * k, h * 512:(h + 1) * 512], ps[r0:r0 + k, 6 + h, :])
                    last.then_inc(signal, 1)

                @block.sync
                def _(sp):
                    sp.dma_start(slots[:], const["slots"]).then_inc(consts, 16)
                    sp.dma_start(slot_of[:], const["slot_of"]).then_inc(consts, 16)

                    def load(i, q):
                        sp.wait_ge(w_lo_made, Q * i + q - ring.SLOTS + 1)
                        ring.load(sp, l, [2 * KD * i + c * KD // 2 for c in range(4)], q)
                    for q in range(ring.SLOTS, Q):
                        load(0, q)
                    with sp.Fori(1, NP) as i:
                        for q in range(Q):
                            load(i, q)

                @block.gpsimd
                def _(pool):
                    def prepare(i, end):
                        pool.wait_ge(spread, i)
                        for z, _, _ in zs_:
                            k, c0 = KZ[z], 2 * KL * z
                            last = nc.gpsimd.tensor_copy(sel[:, c0:c0 + 2 * k].rearrange("e (a b) -> e a b", b=k),
                                                         ident[0:E, ds(2 * i, 2)].unsqueeze(2).to_broadcast([E, 2, k]))
                        last.then_inc(picked, 1)
                    pairs(pool, prepare)

                @block.tensor
                def _(pe):
                    def gather(i, banks):
                        pe.wait_ge(one_hot, i + 1)
                        for b in banks:
                            if b >= 2:
                                pe.wait_ge(xg_hi_made, 4 * i + b - 1)
                                pe.wait_ge(xg_lo_made, 4 * i + b - 1)
                            for d in range(2):
                                chunk = ps[:, 4 + b % 2, d * 2 * M:(d + 1) * 2 * M].rearrange("p (e c) -> p e c", e=2)
                                for z, t0, m in zs_:
                                    for t in range(m // P):
                                        mm = nc.tensor.matmul(chunk[:, :, KL * z:KL * z + KZ[z]],
                                                              h2[:, t0 // P + t, (2 * b + d) * P:(2 * b + d + 1) * P], oh[z][:, t],
                                                              start=(t == 0), stop=(t == m // P - 1))
                            mm.then_inc(gathered, 1)

                    def turn(i, s):
                        pe.wait_ge(consts, 32)
                        pe.wait_ge(hidden, 4 * i + 2 * s + 2)
                        for k in range(KD):
                            mm = nc.tensor.transpose(ps[:, 4 + k // 4, (k % 4) * M:(k % 4 + 1) * M], act_[s][:, k * P:(k + 1) * P], ident[0:M, 0:M])
                        mm.then_inc(turned, 1)

                    def unit(i, q):
                        s, j, kh = ring.ORDER[q]
                        n = Q * i + q
                        if q == 0:
                            pe.wait_ge(xg_hi_made, 4 * i + 4)
                            pe.wait_ge(xg_lo_made, 4 * i + 4)
                            pe.wait_ge(added, i * NS)
                        if s == 1 and j in (0, 2) and kh == 0:
                            pe.wait_ge(hidden, 4 * i + 1 + j // 2)
                        if j == 4 and kh == 0:
                            pe.wait_ge(aT_hi_made, 4 * i + 2 * s + 2)
                            pe.wait_ge(aT_lo_made, 4 * i + 2 * s + 2)
                        if s == 1 and j >= 4 and kh == 0:
                            pe.wait_ge((y_act, y_dve)[j - 4], 2 * i + 1)
                        b = j if j < 4 else j + 2
                        src = (xg_hi, xg_lo) if j < 4 else (aT_hi[s], aT_lo[s])
                        x_hi, x_lo = [[x[:, k, s, :] if j < 4 else x[:, k, :] for k in range(4 * kh, 4 * kh + 4)] for x in src]
                        pe.wait_ge(w_hi_made, n + 1)
                        for k in range(4):
                            nc.tensor.matmul(ps[0:M, b, :], x_hi[k], w_hi[q % AHEAD][:, k, :], start=(kh == 0 and k == 0), stop=False)
                            nc.tensor.matmul(ps[0:M, b, :], x_lo[k], w_hi[q % AHEAD][:, k, :], start=False, stop=False)
                        pe.wait_ge(w_lo_made, n + 1)
                        for k in range(4):
                            mm = nc.tensor.matmul(ps[0:M, b, :], x_hi[k], w_lo[q % AHEAD][:, k, :], start=False, stop=(kh == 1 and k == 3))
                        mm.then_inc(multiplied, 1)

                    def pair(i, end):
                        for q in range(Q):
                            unit(i, q)
                            if q == 13:
                                turn(i, 0)
                            if q == 17:
                                turn(i, 1)
                                pe.wait_ge(picked, i + 1)
                                for z, t0, m in zs_:
                                    w = 2 * KZ[z]
                                    c0 = 2 * KL * z
                                    nc.tensor.matmul(ps[0:w, 2 * z, 0:m], sel[:, c0:c0 + w], posT[:, t0:t0 + m], start=True, stop=True)
                                    mm = nc.tensor.matmul(ps[0:w, 2 * z + 1, 0:m], sel[:, c0:c0 + w], affT[:, t0:t0 + m], start=True, stop=True)
                                mm.then_inc(spread, 1)
                            if q in (19, 21) and end > Q:
                                if q == 19:
                                    pe.wait_ge(aT_hi_made, 4 * i + 4)
                                    pe.wait_ge(aT_lo_made, 4 * i + 4)
                                gather(i + 1, (0, 1) if q == 19 else (2, 3))
                        pe.wait_ge(scatter, i + 1)
                        pe.wait_ge(y_act, 2 * i + 2)
                        for n, (z, t0, m, d) in enumerate(order):
                            if n == NS // 2:
                                pe.wait_ge(y_dve, 2 * i + 2)
                            if n >= 4:
                                pe.wait_ge(added, i * NS + n - 3)
                            nc.tensor.matmul(ps[:, n % 4, 0:m], Y[z][:, d * P:(d + 1) * P], G[0:2 * KZ[z], t0:t0 + m],
                                             start=True, stop=True).then_inc(scattered, 1)

                    pe.wait_ge(consts, 32)
                    gather(0, range(4))
                    pairs(pe, pair)

                @block.vector
                def _(dve):
                    def split(i, q):
                        dve.wait_ge(w_hi_made, Q * i + q + 1)
                        nc.vector.tensor_tensor(w_lo[q % AHEAD][:], ring.slot[q % ring.SLOTS][:], w_hi[q % AHEAD][:].bitcast(F32),
                                                ALU.subtract).then_inc(w_lo_made, 1)

                    def one_hots(i):
                        for z, t0, m in zs_:
                            k = KZ[z]
                            for t in range(m // P):
                                last = nc.vector.tensor_tensor(oh[z][:, t], posm[:, t0 // P + t, ds(2 * i, 2)].unsqueeze(2).to_broadcast([P, 2, k]),
                                                               slots[:, 0:k].unsqueeze(1).to_broadcast([P, 2, k]), ALU.is_equal)
                        last.then_inc(one_hot, 1)

                    def rest(i, banks):
                        for b in banks:
                            dve.wait_ge(xg_hi_made, 4 * i + b + 1)
                            x = xg_hi[:, 2 * b:2 * b + 2].rearrange("p k e m -> p (k e m)")
                            nc.vector.tensor_tensor(xg_lo[:, 2 * b:2 * b + 2].rearrange("p k e m -> p (k e m)"),
                                                    ps[:, 4 + b % 2, 0:4 * M], x.bitcast(F32), ALU.subtract).then_inc(xg_lo_made, 1)

                    def pair(i, end):
                        for q in range(AHEAD, end):
                            if q in (6, 10, 14, 18):
                                s, h = (q - 6) // 8, (q - 6) // 4 % 2
                                dve.wait_ge(silued, 4 * i + 2 * s + h + 1)
                                dve.wait_ge(multiplied, Q * i + q - 2)
                                a_ = act_[s][:, h * 512:(h + 1) * 512]
                                nc.vector.tensor_tensor(a_, a_, ps[0:M, 2 * h + 1, :], ALU.mult).then_inc(hidden, 1)
                            if q == 22:
                                keep_down(dve, nc.vector.tensor_copy, i, 0, 1, y_dve)
                            if q == 26:
                                keep_down(dve, nc.vector.tensor_copy, i, 1, 1, y_dve)
                                for n in range(4):
                                    add(i, n)
                            split(i, q)
                            if q in (16, 20):
                                s = (q - 16) // 4
                                for b in range(2):
                                    dve.wait_ge(aT_hi_made, 4 * i + 2 * s + b + 1)
                                    c = slice(4 * b, 4 * b + 4)
                                    nc.vector.tensor_tensor(aT_lo[s][:, c].rearrange("p k m -> p (k m)"), ps[:, 4 + b, 0:4 * M],
                                                            aT_hi[s][:, c].rearrange("p k m -> p (k m)").bitcast(F32),
                                                            ALU.subtract).then_inc(aT_lo_made, 1)
                            if q == 12 and end > Q:
                                dve.wait_ge(gathered, 4 * i + 4)
                                one_hots(i + 1)
                            if q == 21:
                                dve.wait_ge(aff_copied, i + 1)
                                for z, t0, m in zs_:
                                    w = 2 * KZ[z]
                                    last = nc.vector.scalar_tensor_tensor(G[0:w, t0:t0 + m], ps[0:w, 2 * z, 0:m], slot_of[0:w, z:z + 1],
                                                                          affb[0:w, t0:t0 + m], ALU.is_equal, ALU.mult)
                                last.then_inc(scatter, 1)
                            if q in (22, 24) and end > Q:
                                rest(i + 1, (0, 1) if q == 22 else (2, 3))
                        if end == Q:
                            keep_down(dve, nc.vector.tensor_copy, i, 1, 1, y_dve)
                            for n in range(4):
                                add(i, n)
                        for n in range(4, NS):
                            add(i, n)

                    def add(i, n):
                        z, t0, m, d = order[n]
                        dve.wait_ge(scattered, i * NS + n + 1)
                        nc.vector.scalar_tensor_tensor(xT[:, d, t0:t0 + m], ps[:, n % 4, 0:m], modT[:, 5 * KD + d, z:z + 1],
                                                       xT[:, d, t0:t0 + m], ALU.mult, ALU.add).then_inc(added, 1)

                    dve.wait_ge(consts, 32)
                    one_hots(0)
                    for q in range(AHEAD):
                        split(0, q)
                    rest(0, range(4))
                    pairs(dve, pair)

                @block.scalar
                def _(act):
                    def round_(i, q):
                        act.wait_ge(ring.loaded[q % ring.SLOTS], 16 * (Q // ring.SLOTS * i + q // ring.SLOTS + 1))
                        if q >= AHEAD:
                            act.wait_ge(multiplied, Q * i + q - AHEAD + 1)
                        nc.scalar.copy(w_hi[q % AHEAD][:], ring.slot[q % ring.SLOTS][:]).then_inc(w_hi_made, 1)

                    def gathered_hi(i, banks):
                        for b in banks:
                            act.wait_ge(gathered, 4 * i + b + 1)
                            nc.scalar.copy(xg_hi[:, 2 * b:2 * b + 2].rearrange("p k e m -> p (k e m)"), ps[:, 4 + b % 2, 0:4 * M]).then_inc(xg_hi_made, 1)

                    def pair(i, end):
                        for q in range(AHEAD, end):
                            if q in (4, 8, 12, 16):
                                s, h = (q - 4) // 8, (q - 4) // 4 % 2
                                act.wait_ge(multiplied, Q * i + q - 2)
                                nc.scalar.activation(act_[s][:, h * 512:(h + 1) * 512], ps[0:M, 2 * h, :], ACT.Silu).then_inc(silued, 1)
                            if q in (20, 24):
                                keep_down(act, nc.scalar.copy, i, (q - 20) // 4, 0, y_act)
                            round_(i, q)
                            if q in (16, 20):
                                s = (q - 16) // 4
                                act.wait_ge(turned, 2 * i + s + 1)
                                for b in range(2):
                                    nc.scalar.copy(aT_hi[s][:, 4 * b:4 * b + 4].rearrange("p k m -> p (k m)"), ps[:, 4 + b, 0:4 * M]).then_inc(aT_hi_made, 1)
                            if q == 20:
                                act.wait_ge(spread, i + 1)
                                for z, t0, m in zs_:
                                    w = 2 * KZ[z]
                                    last = nc.scalar.copy(affb[0:w, t0:t0 + m], ps[0:w, 2 * z + 1, 0:m])
                                last.then_inc(aff_copied, 1)
                            if q in (22, 24) and end > Q:
                                gathered_hi(i + 1, (0, 1) if q == 22 else (2, 3))
                        if end == Q:
                            keep_down(act, nc.scalar.copy, i, 1, 0, y_act)

                    for q in range(AHEAD):
                        round_(0, q)
                    gathered_hi(0, range(4))
                    pairs(act, pair)

        def store():
            with Scope() as st:
                rows = sb(st, "out_rows", [P, NL, D])
                turned, stored = sem(st, "out_turned"), sem(st, "stored")
                kept = [sem(st, "out_kept_dve"), sem(st, "out_kept_act")]
                block = st.enter_context(nc.Block())

                @block.tensor
                def _(pe):
                    for j in range(2 * NL):
                        if j >= 4:
                            pe.wait_ge(kept[j % 2], (j - 4) // 2 + 1)
                        for q in range(4):
                            mm = nc.tensor.transpose(ps[:, j % 4, q * P:(q + 1) * P], xT[:, 4 * (j % 2) + q, (j // 2) * P:(j // 2 + 1) * P], ident[:])
                        mm.then_inc(turned, 1)

                def keep(eng, copy, parity):
                    for t in range(NL):
                        eng.wait_ge(turned, 2 * t + parity + 1)
                        copy(rows[:, t, parity * 512:(parity + 1) * 512], ps[:, (2 * t + parity) % 4, :]).then_inc(kept[parity], 1)

                @block.vector
                def _(dve):
                    keep(dve, nc.vector.tensor_copy, 0)

                @block.scalar
                def _(act):
                    keep(act, nc.scalar.copy, 1)

                @block.sync
                def _(sp):
                    for t in range(NL):
                        for parity in range(2):
                            sp.wait_ge(kept[parity], t + 1)
                        sp.dma_start(out[0, t * P:(t + 1) * P, :], rows[:, t, :]).then_inc(stored, 16)
                    sp.wait_ge(stored, 16 * NL)

        setup()
        for l in range(DEPTH):
            last = l == DEPTH - 1
            modulation(l)
            with Scope() as mixed:
                mT = None
                with Scope() as mixers:
                    hT = sb(mixers, "hT", [P, KD, T])
                    oT = sb(mixers, "oT", [P, 10, T])
                    norm(0, hT, True)
                    with Scope() as heads:
                        proj = sb(heads, "proj", [P, NT, C_GL])
                        stat = sb(heads, "stat", [P, NT, N_STATS])
                        projection(l, hT, proj, last)
                        with Scope() as biased:
                            bias = sb(biased, "rpb_spread", [P, NA_HEADS, 14 * GRID_W])
                            colmask = sb(biased, "colmask", [P, GRID_W])
                            bl = sem(biased, "bias_loaded")
                            statistics(proj, stat, last, lambda sp: load_bias(sp, l, bias, colmask, bl))
                            neighbourhood(l, proj, stat, oT[:, 0:3], bias, colmask, bl, last)
                        windowed(l, proj, stat, oT[:, 3:6], last)
                        latent(l, proj, stat, oT[:, 6:10], last)
                    mT = sb(mixers, "mT", [P, KD, T])
                    merge(l, hT, oT, mT, not last)
                    output_projection(l, mT, not last)
            with Scope() as moe:
                nt = NL if last else NT
                ring = Ring(moe)
                h2 = sb(moe, "h2", [P, nt, D])
                posm = sb(moe, "slot_by_token", [P, nt, N_EXPERTS])
                posT, affT = sb(moe, "slot_by_expert", [N_EXPERTS, T]), sb(moe, "affinity_by_expert", [N_EXPERTS, T])
                with Scope() as normed:
                    h2T = sb(normed, "h2T", [P, KD, T])
                    norm(1, h2T, not last, lambda sp: [ring.load(sp, l, (0, KD // 2), q) for q in range(ring.SLOTS)])
                    route(l, h2T, h2, posm, posT, affT, not last)
                experts(l, ring, h2, posm, posT, affT, not last)
        store()


_INS = ["x", "c", "ctx", "c_ctx", "norm1_g", "norm2_g", "w_ada", "b_ada", "w_in", "na_q_g", "na_k_g", "na_rpb",
        "mla_q_norm", "mla_w_uq", "mla_kv_norm", "mla_w_ukv", "mla_q_g", "mla_k_g", "swa_q_g", "swa_k_g", "swa_sink",
        "w_na_o", "w_mla_o", "w_swa_o", "w_o", "router", "w_gate", "w_up", "w_down"]


def kernel(**inputs):
    import numpy as _np
    import concourse.bacc as _bacc
    from concourse import mybir as _mybir
    from concourse.bass_utils import run_bass_kernel_spmd as _run

    nc = _bacc.Bacc("TRN2", target_bir_lowering=False, num_devices=1)
    arrays, args = {}, {}
    for name in _INS:
        a = _np.ascontiguousarray(inputs[name])
        arrays[f"in_{name}"] = a
        args[name] = nc.dram_tensor(f"in_{name}", a.shape, _mybir.dt.from_np(a.dtype), kind="ExternalInput").ap()
    out = nc.dram_tensor("out_x", inputs["x"].shape, F32, kind="ExternalOutput").ap()
    build(nc, out=out, **args)
    return _run(nc, [arrays], core_ids=[0]).results[0]["out_x"]
```

```python
from contextlib import ExitStack

import numpy as np

import concourse.bass as bass
from concourse import mybir

F32, F32R = mybir.dt.float32, mybir.dt.float32r
ALU = mybir.AluOpType
ACT = mybir.ActivationFunctionType
AX = mybir.AxisListType
ds = bass.ds

P = 128
GRID_W = 64
NA_HEADS, NA_DIM, NA_WIN_COLS = 6, 64, 16
MLA_HEADS, MLA_Q_RANK, MLA_KV_RANK, MLA_NOPE, MLA_ROPE, MLA_V = 4, 256, 128, 128, 64, 128
MLA_QK = MLA_NOPE + MLA_ROPE
SWA_HEADS, SWA_KV_HEADS, SWA_DIM, SWA_WINDOW = 6, 2, 64, 128
N_EXPERTS, EXPERT_FF, CAPACITY_FACTOR = 16, 1024, 2
ROPE_BASE = 10000.0
EPS = 1e-6
MASKED = -1e30

NA_W = NA_HEADS * NA_DIM
C_NAQ, C_NAK, C_NAV = 0, NA_W, 2 * NA_W
C_CQ = 3 * NA_W
C_CKV = C_CQ + MLA_Q_RANK
C_KR = C_CKV + MLA_KV_RANK
C_SQ = C_KR + MLA_ROPE
C_SK = C_SQ + SWA_HEADS * SWA_DIM
C_SV = C_SK + SWA_KV_HEADS * SWA_DIM
C_GL = C_SV + SWA_KV_HEADS * SWA_DIM
GROUPS = [(C_NAQ, NA_W, False), (C_NAK, NA_W, True), (C_CQ, C_SQ - C_CQ, True),
          (C_SQ, C_SK - C_SQ, False), (C_SK, C_GL - C_SK, True), (C_NAV, NA_W, True)]

R_NA, R_SW, R_CQ, R_CKV, R_KR, N_STATS = 0, 12, 20, 21, 22, 23


NORMED = [[(C_NAQ, 64, 6, R_NA)], [(C_NAK, 64, 6, R_NA + 6)],
          [(C_CQ, 256, 1, R_CQ), (C_CKV, 128, 1, R_CKV), (C_KR, 64, 1, R_KR)],
          [(C_SQ, 64, 6, R_SW)], [(C_SK, 64, 2, R_SW + 6)], []]


class Chain:

    def __init__(self, eng, sem, base=0):
        self.eng, self.sem, self.base, self.n = eng, sem, base, 0

    def link(self, instruction):
        self.n += 1
        instruction.then_inc(self.sem, 1)
        self.eng.wait_ge(self.sem, self.base + self.n)


def constants(S, L):
    nt, nl = (S + L) // P, S // P
    t = np.arange(S)
    f = SWA_DIM // 4
    inv = (np.float32(ROPE_BASE) ** (-np.arange(f, dtype=np.float32) / np.float32(f))).astype(np.float32)
    ar = ((t // GRID_W).astype(np.float32)[:, None] * inv).astype(np.float32)
    ac = ((t % GRID_W).astype(np.float32)[:, None] * inv).astype(np.float32)
    cos = np.concatenate([np.cos(ar), np.cos(ar), np.cos(ac), np.cos(ac)], 1)
    sin = np.concatenate([-np.sin(ar), np.sin(ar), -np.sin(ac), np.sin(ac)], 1)
    cos = np.concatenate([cos, np.ones((L, 64))]).reshape(nt, P, 64).transpose(1, 0, 2)
    sin = np.concatenate([sin, np.zeros((L, 64))]).reshape(nt, P, 64).transpose(1, 0, 2)
    i, j = np.arange(P)[:, None], np.arange(P)[None, :]
    band = np.concatenate([np.where(j >= i, 0, MASKED), np.zeros((P, P)), np.where(j <= i, 0, MASKED)], 1)
    col = np.arange(GRID_W)
    c0 = np.clip(col - NA_WIN_COLS // 2, 0, GRID_W - NA_WIN_COLS)
    ok = (col[None] >= c0[:, None]) & (col[None] < c0[:, None] + NA_WIN_COLS)
    colmask = np.tile(np.where(ok, 0, MASKED), (2, 1))
    kl, kc = CAPACITY_FACTOR * S // N_EXPERTS, CAPACITY_FACTOR * L // N_EXPERTS
    slots = np.tile(np.arange(1, kl + 1), (P, 1))
    p = np.arange(P)
    slot_of = np.stack([p % kl + 1, p % kc + 1], 1)
    return {n: np.ascontiguousarray(a, np.float32) for n, a in dict(
        ident=np.eye(P), cos=cos.reshape(P, -1), sin=sin.reshape(P, -1), band=band, colmask=colmask,
        slots=slots, slot_of=slot_of).items()}


def build(nc, x, c, ctx, c_ctx, norm1_g, norm2_g, w_ada, b_ada, w_in, na_q_g, na_k_g, na_rpb,
          mla_q_norm, mla_w_uq, mla_kv_norm, mla_w_ukv, mla_q_g, mla_k_g, swa_q_g, swa_k_g, swa_sink,
          w_na_o, w_mla_o, w_swa_o, w_o, router, w_gate, w_up, w_down, out):
    _, S, D = x.shape
    L = ctx.shape[1]
    DEPTH = w_in.shape[0]
    T = S + L
    NT, NL = T // P, S // P
    KD = D // P
    NM = 6 * KD
    KL, KC = CAPACITY_FACTOR * S // N_EXPERTS, CAPACITY_FACTOR * L // N_EXPERTS
    MS = KL + KC
    FF = EXPERT_FF
    nsem = [0]

    class Scope(ExitStack):

        def __init__(self):
            super().__init__()
            self.sems = []
            self.callback(self.clear)

        def clear(self):
            if self.sems:
                nc.clear_and_free_semaphores(self.sems)
                nc.all_engine_barrier()

    def sem(stack, name):
        nsem[0] += 1
        stack.sems.append(nc.alloc_semaphore(f"{name}_{nsem[0]}"))
        return stack.sems[-1]

    def sb(stack, name, shape, dtype=F32):
        nsem[0] += 1
        return stack.enter_context(nc.sbuf_tensor(f"{name}_{nsem[0]}", shape, dtype))

    top = Scope()
    const = {n: nc.inline_tensor(a, name=f"const_{n}") for n, a in constants(S, L).items()}
    const = {n: (a.ap() if hasattr(a, "ap") else a) for n, a in const.items()}
    RPBW = 2 * GRID_W - 1
    rpb_pad = nc.dram_tensor("rpb_padded", [DEPTH, GRID_W, NA_HEADS * 15, RPBW], F32, kind="Internal").ap()

    with top:
        xT = sb(top, "xT", [P, KD, T])
        ident = sb(top, "ident", [P, P])
        ones = sb(top, "ones", [P, P])
        cos = sb(top, "cos", [P, NT, 64])
        sin = sb(top, "sin", [P, NT, 64])
        cT = sb(top, "cT", [P, 2, KD])
        modT = sb(top, "modT", [P, NM, 2])
        vecT = sb(top, "vecT", [P, NM + 2 * KD])
        coef = sb(top, "coef", [P, 2, KD, 2])
        ps = top.enter_context(nc.psum_tensor("ps", [P, 8, 512], F32))

        def streams(ctx_too):
            return [(0, 0, S), (1, S, L)][:1 + ctx_too]

        def setup():
            with Scope() as st:
                rows = sb(st, "rows", [P, NT, D])
                crow = sb(st, "crow", [2 * KD, P])
                loaded, cl, ready = sem(st, "loaded"), sem(st, "c_loaded"), sem(st, "ones_ready")
                turned, kept_v, kept_a = sem(st, "turned"), sem(st, "kept_by_dve"), sem(st, "kept_by_act")
                block = st.enter_context(nc.Block())

                @block.sync
                def _(sp):
                    sp.dma_start(ident[:], const["ident"]).then_inc(cl, 16)
                    sp.dma_start(crow[0:KD, :], c.rearrange("b (k p) -> (b k) p", p=P)).then_inc(cl, 16)
                    sp.dma_start(crow[KD:2 * KD, :], c_ctx.rearrange("(k p) -> k p", p=P)).then_inc(cl, 16)
                    sp.dma_start(rows[:, 0:NL, :], x[0].rearrange("(t p) d -> p t d", p=P)).then_inc(loaded, 16)
                    sp.dma_start(rows[:, NL:NT, :], ctx[0].rearrange("(t p) d -> p t d", p=P)).then_inc(loaded, 16)
                    sp.dma_start(cos[:].rearrange("p a b -> p (a b)"), const["cos"]).then_inc(cl, 16)
                    sp.dma_start(sin[:].rearrange("p a b -> p (a b)"), const["sin"]).then_inc(cl, 16)
                    sp.wait_ge(cl, 80)

                @block.gpsimd
                def _(pool):
                    nc.gpsimd.memset(ones[:], 1.0).then_inc(ready, 1)

                @block.tensor
                def _(pe):
                    pe.wait_ge(cl, 80)
                    nc.tensor.transpose(ps[:, 7, 0:2 * KD], crow[:], ident[0:2 * KD, 0:2 * KD]).then_inc(turned, 1)
                    pe.wait_ge(loaded, 32)
                    for k in range(KD):
                        for s, t0, n in streams(True):
                            b = 2 * (k % 2) + s
                            if k >= 2:
                                pe.wait_ge((kept_v, kept_a)[s], k - 1)
                            for t in range(n // P):
                                mm = nc.tensor.transpose(ps[:, b, t * P:(t + 1) * P],
                                                         rows[:, t0 // P + t, k * P:(k + 1) * P], ident[:])
                            mm.then_inc(turned, 1)

                @block.vector
                def _(dve):
                    for k in range(KD):
                        dve.wait_ge(turned, 2 * k + 2)
                        nc.vector.tensor_copy(xT[:, k, 0:S], ps[:, 2 * (k % 2), 0:S]).then_inc(kept_v, 1)

                @block.scalar
                def _(act):
                    act.wait_ge(turned, 1)
                    nc.scalar.activation(cT[:].rearrange("p s k -> p (s k)"), ps[:, 7, 0:2 * KD], ACT.Silu)
                    for k in range(KD):
                        act.wait_ge(turned, 2 * k + 3)
                        nc.scalar.copy(xT[:, k, S:T], ps[:, 2 * (k % 2) + 1, 0:L]).then_inc(kept_a, 1)

        def modulation(l):
            NB, RAW, SPLIT = 6 * D // 512, 4, 2
            with Scope() as st:
                wbuf = [sb(st, f"w_ada{s}", [P, KD, 512]) for s in range(RAW)]
                w_hi, w_lo = ([sb(st, f"w_ada_{q}{s}", [P, KD, 512], F32R) for s in range(SPLIT)] for q in ("hi", "lo"))
                c_hl = sb(st, "c_hi_lo", [P, KD, 4], F32R)
                row = [sb(st, f"mod_row{s}", [P, 512]) for s in range(RAW)]
                vrow = sb(st, "vec_rows", [NM + 2 * KD, P])
                mod4 = sb(st, "mod_hi_lo", [P, NM, 4])
                wl = [sem(st, f"w_ada_loaded{s}") for s in range(RAW)]
                vl, mm_done, row_done = sem(st, "vec_loaded"), sem(st, "mod_mm"), sem(st, "mod_row")
                turned, kept, vt, ch = sem(st, "mod_turned"), sem(st, "mod_kept"), sem(st, "vec_turned"), sem(st, "mod_chain")
                c_split, w_hi_made, w_lo_made = sem(st, "c_split"), sem(st, "w_ada_hi"), sem(st, "w_ada_lo")
                block = st.enter_context(nc.Block())
                wv = w_ada[l].rearrange("(k p) n -> p k n", p=P)

                @block.sync
                def _(sp):
                    for u in range(RAW):
                        sp.dma_start(wbuf[u][:], wv[:, :, u * 512:(u + 1) * 512]).then_inc(wl[u], 16)
                    sp.dma_start(vrow[0:NM, :], b_ada[l].rearrange("(k p) -> k p", p=P)).then_inc(vl, 16)
                    sp.dma_start(vrow[NM:NM + KD, :], norm1_g[l].rearrange("(k p) -> k p", p=P)).then_inc(vl, 16)
                    sp.dma_start(vrow[NM + KD:, :], norm2_g[l].rearrange("(k p) -> k p", p=P)).then_inc(vl, 16)
                    with sp.Fori(1, NB // RAW) as i:
                        for u in range(RAW):
                            sp.wait_ge(w_lo_made, RAW * i + u - RAW + 1)
                            sp.dma_start(wbuf[u][:], wv[:, :, ds((RAW * i + u) * 512, 512)]).then_inc(wl[u], 16)

                @block.tensor
                def _(pe):
                    pe.wait_ge(c_split, 2)
                    with pe.Fori(0, NB // RAW) as i:
                        def turn(u):
                            pe.wait_ge(row_done, RAW * i + u + 1)
                            pe.wait_ge(kept, RAW * i)
                            for j in range(4):
                                mm = nc.tensor.transpose(ps[:, 4 + u, j * P:(j + 1) * P], row[u][:, j * P:(j + 1) * P], ident[:])
                            mm.then_inc(turned, 1)

                        for u in range(RAW):
                            n = RAW * i + u
                            pe.wait_ge(row_done, RAW * i)
                            for made, w in ((w_hi_made, w_hi), (w_lo_made, w_lo)):
                                pe.wait_ge(made, n + 1)
                                for k in range(KD):
                                    mm = nc.tensor.matmul(ps[0:4, u, :], c_hl[:, k, :], w[u % SPLIT][:, k, :],
                                                          start=(w is w_hi and k == 0), stop=(w is w_lo and k == KD - 1))
                            mm.then_inc(mm_done, 1)
                            if u >= 1:
                                turn(u - 1)
                        turn(RAW - 1)
                    pe.wait_ge(vl, 48)
                    pe.wait_ge(row_done, NB)
                    nc.tensor.transpose(ps[:, 0, 0:NM + 2 * KD], vrow[:], ident[0:NM + 2 * KD, 0:NM + 2 * KD]).then_inc(vt, 1)

                @block.scalar
                def _(act):
                    nc.scalar.copy(c_hl[:, :, 0:2], cT[:].rearrange("p s k -> p k s")).then_inc(c_split, 1)
                    act.wait_ge(ch, 1)
                    with act.Fori(0, NB // RAW) as i:
                        def rows_out(u):
                            act.wait_ge(mm_done, RAW * i + u + 1)
                            act.wait_ge(turned, RAW * i)
                            nc.scalar.copy(row[u][0:4, :], ps[0:4, u, :]).then_inc(row_done, 1)

                        def keep(u):
                            act.wait_ge(turned, RAW * i + u + 1)
                            nc.scalar.copy(mod4[:, ds((RAW * i + u) * 4, 4), :],
                                           ps[:, 4 + u, :].rearrange("p (a b) -> p a b", b=P)[:, :, 0:4]).then_inc(kept, 1)

                        for u in range(RAW):
                            act.wait_ge(wl[u], 16 * i + 16)
                            act.wait_ge(mm_done, RAW * i + u - SPLIT + 1 if u >= SPLIT else RAW * i)
                            nc.scalar.copy(w_hi[u % SPLIT][:], wbuf[u][:]).then_inc(w_hi_made, 1)
                            if u >= 1:
                                rows_out(u - 1)
                            if u >= 2:
                                keep(u - 2)
                        rows_out(RAW - 1)
                        keep(RAW - 2)
                        keep(RAW - 1)

                @block.vector
                def _(dve):
                    dve.wait_ge(c_split, 1)
                    nc.vector.tensor_tensor(c_hl[:, :, 2:4], cT[:].rearrange("p s k -> p k s"), c_hl[:, :, 0:2].bitcast(F32),
                                            ALU.subtract).then_inc(c_split, 1)
                    for u in range(RAW):
                        last = nc.vector.memset(row[u][:], 0.0)
                    last.then_inc(ch, 1)
                    with dve.Fori(0, NB // RAW) as i:
                        for u in range(RAW):
                            dve.wait_ge(w_hi_made, RAW * i + u + 1)
                            nc.vector.tensor_tensor(w_lo[u % SPLIT][:], wbuf[u][:], w_hi[u % SPLIT][:].bitcast(F32),
                                                    ALU.subtract).then_inc(w_lo_made, 1)
                    chain = Chain(dve, ch, 1)
                    dve.wait_ge(vt, 1)
                    chain.link(nc.vector.tensor_copy(vecT[:], ps[:, 0, 0:NM + 2 * KD]))
                    dve.wait_ge(kept, NB)
                    chain.link(nc.vector.tensor_tensor(modT[:], mod4[:, :, 0:2], mod4[:, :, 2:4], ALU.add))
                    chain.link(nc.vector.tensor_tensor(modT[:], modT[:],
                                                       vecT[:, 0:NM].unsqueeze(2).to_broadcast([P, NM, 2]), ALU.add))
                    for n in range(2):
                        m = (1 + 3 * n) * KD
                        chain.link(nc.vector.tensor_scalar(coef[:, n], modT[:, m:m + KD, :], 1.0, None, ALU.add))
                        g = vecT[:, NM + n * KD:NM + (n + 1) * KD]
                        chain.link(nc.vector.tensor_tensor(coef[:, n], coef[:, n],
                                                           g.unsqueeze(2).to_broadcast([P, KD, 2]), ALU.mult))

        def norm(n, hT, ctx_too, ahead=None):
            W = T if ctx_too else S
            with Scope() as st:
                sq = [sb(st, f"sq{s}", [P, W]) for s in range(2)]
                rs = sb(st, "rs", [P, W])
                tmp = [sb(st, f"scaled{s}", [P, W]) for s in range(2)]
                squared, summed, root, scaled, done = (sem(st, q) for q in ("squared", "summed", "root", "scaled", "normed"))
                ch = sem(st, "norm_chain")
                block = st.enter_context(nc.Block())

                @block.sync
                def _(sp):
                    if ahead:
                        ahead(sp)

                @block.scalar
                def _(act):
                    for k in range(KD):
                        if k >= 2:
                            act.wait_ge(summed, k - 1)
                        nc.scalar.activation(sq[k % 2][:], xT[:, k, 0:W], ACT.Square).then_inc(squared, 1)
                    act.wait_ge(ch, 1)
                    nc.scalar.activation(rs[:], rs[:], ACT.Sqrt).then_inc(root, 1)
                    for k in range(KD):
                        act.wait_ge(scaled, k + 1)
                        for s, t0, m in streams(ctx_too):
                            last = nc.scalar.activation(hT[:, k, t0:t0 + m], tmp[k % 2][:, t0:t0 + m], ACT.Identity,
                                                        bias=modT[:, 3 * n * KD + k, s:s + 1], scale=coef[:, n, k, s:s + 1])
                        last.then_inc(done, 1)

                @block.tensor
                def _(pe):
                    for k in range(KD):
                        pe.wait_ge(squared, k + 1)
                        for s, t0, m in streams(ctx_too):
                            mm = nc.tensor.matmul(ps[:, s, 0:m], ones[:], sq[k % 2][:, t0:t0 + m],
                                                  start=(k == 0), stop=(k == KD - 1))
                        mm.then_inc(summed, 1)

                @block.vector
                def _(dve):
                    dve.wait_ge(summed, KD)
                    for s, t0, m in streams(ctx_too):
                        last = nc.vector.tensor_scalar(rs[:, t0:t0 + m], ps[:, s, 0:m], 1.0 / D, EPS, ALU.mult, ALU.add)
                    last.then_inc(ch, 1)
                    dve.wait_ge(root, 1)
                    nc.vector.reciprocal(rs[:], rs[:]).then_inc(ch, 1)
                    dve.wait_ge(ch, 2)
                    for k in range(KD):
                        if k >= 2:
                            dve.wait_ge(done, k - 1)
                        nc.vector.tensor_tensor(tmp[k % 2][:], xT[:, k, 0:W], rs[:], ALU.mult).then_inc(scaled, 1)

        def projection(l, hT, proj, stat, last_layer):
            NK, SLOTS = 2, 2
            with Scope() as st:
                h_hi, h_lo = (sb(st, f"h_{q}", [P, KD, T], F32R) for q in ("hi", "lo"))
                wbuf = [sb(st, f"w_in{s}", [P, NK, 448]) for s in range(SLOTS)]
                w_hi, w_lo = ([sb(st, f"w_in_{q}{s}", [P, NK, 448], F32R) for s in range(SLOTS)] for q in ("hi", "lo"))
                sq = sb(st, "stat_squares", [P, 448])
                squared, summed, root, ch = (sem(st, q) for q in ("stat_squared", "stat_summed", "stat_root", "stat_chain"))
                zrow = sb(st, "rpb_rows", [NA_HEADS * 15, DEPTH, RPBW]) if l == 0 else None
                zeroed, padded = sem(st, "rpb_zeroed"), sem(st, "rpb_padded")
                wl = [sem(st, f"w_in_loaded{s}") for s in range(SLOTS)]
                h_hi_made, h_lo_made, w_hi_made, w_lo_made = (sem(st, q) for q in ("h_hi", "h_lo", "w_in_hi", "w_in_lo"))
                multiplied, finished = sem(st, "proj_multiplied"), sem(st, "proj_finished")
                kept = [sem(st, "proj_kept_dve"), sem(st, "proj_kept_act")]
                block = st.enter_context(nc.Block())
                wv = w_in[l].rearrange("(k p) n -> p k n", p=P)
                work = [(g, t) for g in range(len(GROUPS)) for t in range(NT if not last_layer or GROUPS[g][2] else NL)]
                done_by = [sum(w[0] < g for w in work) for g in range(len(GROUPS) + 1)]
                UG = KD // NK
                N = UG * len(GROUPS)

                def unit_done(eng, n):
                    g, u = n // UG, n % UG
                    if u == UG - 1:
                        eng.wait_ge(finished, done_by[g + 1])
                    else:
                        eng.wait_ge(multiplied, g * (UG - 1) + u + 1)

                @block.sync
                def _(sp):
                    for n in range(N):
                        if n == 4 and l == 0:
                            sp.wait_ge(zeroed, 1)
                            for m in range(DEPTH):
                                sp.dma_start(zrow[:, m, 48:79], na_rpb[m].rearrange("h r c -> (h r) c")).then_inc(padded, 16)
                        if n == 8 and l == 0:
                            sp.wait_ge(padded, 16 * DEPTH)
                            for m in range(DEPTH):
                                sp.dma_start(rpb_pad[m].rearrange("q r c -> r q c"), zrow[:, m].unsqueeze(1).to_broadcast([NA_HEADS * 15, GRID_W, RPBW])).then_inc(padded, 16)
                        g, u = n // UG, n % UG
                        c0, w, _ = GROUPS[g]
                        if n >= SLOTS:
                            sp.wait_ge(w_lo_made, n - SLOTS + 1)
                        sp.dma_start(wbuf[n % SLOTS][:, :, 0:w], wv[:, u * NK:(u + 1) * NK, c0:c0 + w]).then_inc(wl[n % SLOTS], 16)
                    if l == 0:
                        sp.wait_ge(padded, 32 * DEPTH)

                @block.gpsimd
                def _(pool):
                    if l == 0:
                        nc.gpsimd.memset(zrow[:], 0.0).then_inc(zeroed, 1)

                @block.tensor
                def _(pe):
                    for n in range(N):
                        g, u = n // UG, n % UG
                        w = GROUPS[g][1]
                        if g == 0:
                            pe.wait_ge(h_hi_made, NK * (u + 1))
                            pe.wait_ge(h_lo_made, NK * (u + 1))
                        pe.wait_ge(w_hi_made, n + 1)
                        pe.wait_ge(w_lo_made, n + 1)
                        for j in range(done_by[g], done_by[g + 1]):
                            t = work[j][1]
                            if u == 0 and j >= 8:
                                pe.wait_ge(kept[j % 2], (j - 8) // 2 + 1)
                            for q in range(NK):
                                k = u * NK + q
                                for h, w_ in ((h_hi, w_hi), (h_hi, w_lo), (h_lo, w_hi)):
                                    mm = nc.tensor.matmul(ps[:, j % 8, 0:w], h[:, k, t * P:(t + 1) * P], w_[n % SLOTS][:, q, 0:w],
                                                          start=(k == 0 and w_ is w_hi and h is h_hi), stop=(k == KD - 1 and h is h_lo))
                            if u == UG - 1:
                                mm.then_inc(finished, 1)
                        if u < UG - 1:
                            mm.then_inc(multiplied, 1)

                def keep(eng, copy, parity, g):
                    for j in range(done_by[g], done_by[g + 1]):
                        if j % 2 == parity:
                            c0, w, _ = GROUPS[g]
                            eng.wait_ge(finished, j + 1)
                            copy(proj[:, work[j][1], c0:c0 + w], ps[:, j % 8, 0:w]).then_inc(kept[parity], 1)

                def stat_tiles(n):
                    g, u = n // UG - 1, n % UG
                    if g < 0 or u == 0 or not NORMED[g]:
                        return []
                    return list(range(done_by[g], done_by[g + 1]))[2 * u - 2:2 * u]
                tiles_before = lambda n: sum(len(stat_tiles(m)) for m in range(n))

                @block.vector
                def _(dve):
                    nc.vector.memset(stat[:], 0.0).then_inc(ch, 1)
                    dve.wait_ge(ch, 1)
                    for n in range(N):
                        g, w = n // UG, GROUPS[n // UG][1]
                        if g == 0:
                            for k in range(n * NK, (n + 1) * NK):
                                dve.wait_ge(h_hi_made, k + 1)
                                nc.vector.tensor_tensor(h_lo[:, k, :], hT[:, k, :], h_hi[:, k, :].bitcast(F32), ALU.subtract).then_inc(h_lo_made, 1)
                        if n % UG == 1 and g > 0:
                            keep(dve, nc.vector.tensor_copy, 0, g - 1)
                        dve.wait_ge(w_hi_made, n + 1)
                        nc.vector.tensor_tensor(w_lo[n % SLOTS][:, :, 0:w], wbuf[n % SLOTS][:, :, 0:w],
                                                w_hi[n % SLOTS][:, :, 0:w].bitcast(F32), ALU.subtract).then_inc(w_lo_made, 1)
                        for m, j in enumerate(stat_tiles(n), tiles_before(n)):
                            dve.wait_ge(squared, m + 1)
                            for c0, d, heads, r in NORMED[g - 1]:
                                o = c0 - GROUPS[g - 1][0]
                                last = nc.vector.tensor_reduce(stat[:, work[j][1], r:r + heads],
                                                               sq[:, o:o + heads * d].rearrange("p (h d) -> p h d", d=d), AX.X, ALU.add)
                            last.then_inc(summed, 1)
                    dve.wait_ge(summed, tiles_before(N))
                    for r0, r1, w in ((R_NA, R_CQ, 64), (R_CQ, R_CKV, 256), (R_CKV, R_KR, 128)):
                        nc.vector.tensor_scalar(stat[:, :, r0:r1], stat[:, :, r0:r1], 1.0 / w, EPS,
                                                ALU.mult, ALU.add).then_inc(ch, 1)
                    dve.wait_ge(root, 1)
                    nc.vector.reciprocal(stat[:, :, 0:R_KR], stat[:, :, 0:R_KR])
                    keep(dve, nc.vector.tensor_copy, 0, len(GROUPS) - 1)

                @block.scalar
                def _(act):
                    for n in range(N):
                        g, w = n // UG, GROUPS[n // UG][1]
                        if g == 0:
                            for k in range(n * NK, (n + 1) * NK):
                                nc.scalar.copy(h_hi[:, k, :], hT[:, k, :]).then_inc(h_hi_made, 1)
                        if n % UG == 1 and g > 0:
                            keep(act, nc.scalar.copy, 1, g - 1)
                        act.wait_ge(wl[n % SLOTS], 16 * (n // SLOTS + 1))
                        if n >= SLOTS:
                            unit_done(act, n - SLOTS)
                        nc.scalar.copy(w_hi[n % SLOTS][:, :, 0:w], wbuf[n % SLOTS][:, :, 0:w]).then_inc(w_hi_made, 1)
                        for m, j in enumerate(stat_tiles(n), tiles_before(n)):
                            act.wait_ge(kept[j % 2], j // 2 + 1)
                            if m >= 1:
                                act.wait_ge(summed, m)
                            c0, d, _ = GROUPS[g - 1]
                            nc.scalar.activation(sq[:, 0:d], proj[:, work[j][1], c0:c0 + d], ACT.Square).then_inc(squared, 1)
                    act.wait_ge(ch, 4)
                    nc.scalar.activation(stat[:, :, 0:R_KR], stat[:, :, 0:R_KR], ACT.Sqrt).then_inc(root, 1)
                    keep(act, nc.scalar.copy, 1, len(GROUPS) - 1)

        SWAP = [(a * 32 + b * 16, a * 32 + (1 - b) * 16) for a in range(2) for b in range(2)]

        def rope_tables(chain, cg, sg, g, scale):
            chain.link(nc.vector.tensor_scalar(g[:], g[:], scale, None, ALU.mult))
            nc.vector.tensor_tensor(cg[:], cos[:], g[:].unsqueeze(1).to_broadcast([P, NT, 64]), ALU.mult)
            for d, o in SWAP:
                last = nc.vector.tensor_tensor(sg[:, :, d:d + 16], sin[:, :, d:d + 16],
                                               g[:, o:o + 16].unsqueeze(1).to_broadcast([P, NT, 16]), ALU.mult)
            chain.link(last)

        def rope(chain, res, x, part, cg, sg, nt, heads):
            nc.vector.tensor_tensor(res, x, cg[:, 0:nt].unsqueeze(2).to_broadcast([P, nt, heads, 64]), ALU.mult)
            for d, o in SWAP:
                last = nc.vector.tensor_tensor(part[:, :, :, d:d + 16], x[:, :, :, o:o + 16],
                                               sg[:, 0:nt, d:d + 16].unsqueeze(2).to_broadcast([P, nt, heads, 16]), ALU.mult)
            chain.link(last)
            return nc.vector.tensor_tensor(res, res, part, ALU.add)

        def iterations(eng, n, body):
            with eng.Fori(0, n - 1) as i:
                body(i, True)
            body(n - 1, False)

        class Attention:

            def __init__(self, st, name, heads, dv, tiles, key_tiles):
                self.units = [(hh, t) for hh in range(heads) for t in tiles]
                self.U, self.dv, self.key_tiles, self.tiles = len(self.units), dv, key_tiles, tiles
                assert self.U % 2 == 0
                self.pexp = [sb(st, f"{name}_exp{s}", [P, T]) for s in range(2)]
                self.pT = [sb(st, f"{name}_expT{s}", [P, NT, P]) for s in range(2)]
                self.rowmax = sb(st, f"{name}_max", [P, 2, 4])
                self.rowsum = sb(st, f"{name}_sum", [P, 4, 3])
                self.osb = sb(st, f"{name}_o", [P, len(tiles), P])
                self.scored = sem(st, f"{name}_scored")
                self.maxed = sem(st, f"{name}_maxed")
                self.exped = sem(st, f"{name}_exped")
                self.turned = sem(st, f"{name}_turned")
                self.kept_lo = sem(st, f"{name}_kept_lo")
                self.kept_hi = sem(st, f"{name}_kept_hi")
                self.valued = sem(st, f"{name}_valued")
                self.divided = sem(st, f"{name}_divided")
                self.o_turned = sem(st, f"{name}_o_turned")
                self.o_kept = sem(st, f"{name}_o_kept")
                self.staged = sem(st, f"{name}_staged")
                self.q_turned = sem(st, f"{name}_q_turned")
                self.qk_kept = sem(st, f"{name}_qk_kept")
                self.chain = sem(st, f"{name}_chain")

            def pe_units(self, pe, i, score, value, early=None):
                def transposes(u):
                    t = self.units[u][1]
                    n = i * self.U + u
                    pe.wait_ge(self.exped, n + 1)
                    pe.wait_ge(self.kept_lo, n)
                    pe.wait_ge(self.kept_hi, n)
                    kt = self.key_tiles(t)
                    for q in range(len(kt)):
                        h = (len(kt) + 1) // 2
                        mm = nc.tensor.transpose(ps[:, 4 + q // h, (q % h) * P:(q % h + 1) * P],
                                                 self.pexp[u % 2][:, q * P:(q + 1) * P], ident[:])
                    mm.then_inc(self.turned, 1)

                def values(u):
                    hh, t = self.units[u]
                    n = i * self.U + u
                    pe.wait_ge(self.kept_lo, n + 1)
                    pe.wait_ge(self.kept_hi, n + 1)
                    pe.wait_ge(self.divided, n - 1 if u >= 1 else n)
                    kt = self.key_tiles(t)
                    o = ps[:, 6 + u % 2, 0:self.dv]
                    for q, k in enumerate(kt):
                        mm = nc.tensor.matmul(o, self.pT[u % 2][:, q, :], value(hh, k), start=(q == 0), stop=(q == len(kt) - 1))
                    mm.then_inc(self.valued, 1)

                def scores(u):
                    hh, t = self.units[u]
                    n = i * self.U + u
                    pe.wait_ge(self.exped, n - 1 if u >= 1 else n)
                    score(hh, t, 2 * (u % 2)).then_inc(self.scored, 1)

                scores(0)
                scores(1)
                pe.wait_ge(self.o_kept, i)
                transposes(0)
                for u in range(self.U):
                    if u + 2 < self.U:
                        scores(u + 2)
                    if u + 1 < self.U:
                        transposes(u + 1)
                    if early and u >= self.U - 2:
                        early(u - self.U + 2)
                    values(u)
                pe.wait_ge(self.divided, (i + 1) * self.U)
                pe.wait_ge(self.kept_lo, (i + 1) * self.U)
                pe.wait_ge(self.kept_hi, (i + 1) * self.U)
                for q in range(len(self.tiles)):
                    mm = nc.tensor.transpose(ps[:, 4 if q < NL else 5, (q % NL) * P:(q % NL + 1) * P],
                                             self.osb[:, q, :], ident[:])
                mm.then_inc(self.o_turned, 1)

            def dve_units(self, dve, i, chain, maximum, more_sum=None, early=None):
                def keep_hi(u):
                    t = self.units[u][1]
                    n = i * self.U + u
                    kt = len(self.key_tiles(t))
                    dve.wait_ge(self.turned, n + 1)
                    dve.wait_ge(self.valued, n - 1 if u >= 1 else n)
                    h = (kt + 1) // 2
                    nc.vector.tensor_copy(self.pT[u % 2][:, h:kt, :].rearrange("p a b -> p (a b)"),
                                          ps[:, 5, 0:(kt - h) * P]).then_inc(self.kept_hi, 1)

                def divide(u):
                    t = self.units[u][1]
                    n = i * self.U + u
                    dve.wait_ge(self.valued, n + 1)
                    s = self.rowsum[:, u % 4]
                    if more_sum:
                        chain.link(nc.vector.tensor_tensor(s[:, 0:1], s[:, 0:1], s[:, 2:3], ALU.add))
                    chain.link(nc.vector.reciprocal(s[:, 1:2], s[:, 0:1]))
                    hh = self.units[u][0]
                    if u == 0:
                        dve.wait_ge(self.o_turned, i)
                    nc.vector.tensor_scalar(self.osb[:, self.tiles.index(t), hh * self.dv:(hh + 1) * self.dv],
                                            ps[:, 6 + u % 2, 0:self.dv], s[:, 1:2], None,
                                            ALU.mult).then_inc(self.divided, 1)

                def maxima(u):
                    hh, t = self.units[u]
                    n = i * self.U + u
                    dve.wait_ge(self.scored, n + 1)
                    dve.wait_ge(self.exped, n - 1 if u >= 1 else n)
                    maximum(hh, t, 2 * (u % 2), u % 2).then_inc(self.maxed, 1)

                maxima(0)
                maxima(1)
                keep_hi(0)
                for u in range(self.U):
                    if u + 2 < self.U:
                        maxima(u + 2)
                    if u + 1 < self.U:
                        keep_hi(u + 1)
                    if early and u == self.U - 3:
                        early()
                    divide(u)

            def act_units(self, act, i, source, oT, more_exp=None, early=None):
                def exponentials(u):
                    hh, t = self.units[u]
                    n = i * self.U + u
                    act.wait_ge(self.maxed, n + 1)
                    act.wait_ge(self.turned, n - 1 if u >= 1 else n)
                    act.wait_ge(self.divided, n - 3 if u >= 4 else i * self.U)
                    if more_exp:
                        more_exp(hh, u)
                    src = source(t, 2 * (u % 2), u % 2)
                    nc.scalar.activation(self.pexp[u % 2][:, 0:src.shape[1]], src, ACT.Exp, bias=self.rowmax[:, u % 2, 3:4],
                                         accum_out=self.rowsum[:, u % 4, 0:1]).then_inc(self.exped, 1)

                def keep_lo(u):
                    t = self.units[u][1]
                    n = i * self.U + u
                    kt = len(self.key_tiles(t))
                    act.wait_ge(self.turned, n + 1)
                    act.wait_ge(self.valued, n - 1 if u >= 1 else n)
                    h = (kt + 1) // 2
                    nc.scalar.copy(self.pT[u % 2][:, 0:h, :].rearrange("p a b -> p (a b)"),
                                   ps[:, 4, 0:h * P]).then_inc(self.kept_lo, 1)

                exponentials(0)
                exponentials(1)
                keep_lo(0)
                for u in range(self.U):
                    if u + 1 < self.U:
                        keep_lo(u + 1)
                    if u + 2 < self.U:
                        exponentials(u + 2)
                    if early and u >= self.U - 2:
                        early(u - self.U + 2)
                act.wait_ge(self.o_turned, i + 1)
                w = min(len(self.tiles), NL) * P
                last = nc.scalar.copy(oT[:, ds(i, 1), 0:w], ps[:, 4:5, 0:w])
                if len(self.tiles) > NL:
                    last = nc.scalar.copy(oT[:, ds(i, 1), w:T], ps[:, 5:6, 0:T - w])
                last.then_inc(self.o_kept, 1)

        def load_bias(sp, l, bias, colmask, bl):
            sp.dma_start(colmask[:], const["colmask"]).then_inc(bl[0], 16)
            for h in range(NA_HEADS):
                for par in range(2):
                    src = bass.AP(tensor=rpb_pad.tensor, offset=(l * GRID_W * NA_HEADS * 15 + h * 15 + 1 - par) * RPBW + GRID_W - 1,
                                  ap=[[RPBW * 15 * NA_HEADS - 1, GRID_W], [RPBW, 14], [1, GRID_W]])
                    sp.dma_start(bias[par * 64:(par + 1) * 64, h, :].rearrange("p (j k) -> p j k", k=GRID_W), src).then_inc(bl[h // 2], 16)

        def neighbourhood(l, proj, stat, oT, bias, colmask, bl, last_layer):
            nq = NL if last_layer else NT
            keys_of = lambda t: list(range(NT)) if t < NL else list(range(NL, NT))
            with Scope() as st:
                a = Attention(st, "na", 2, NA_DIM, list(range(nq)), keys_of)
                bst = sb(st, "bias", [P, 2, 14, GRID_W])
                qst, kst = sb(st, "na_q", [P, nq, 2, 64]), sb(st, "na_k", [P, NT, 2, 64])
                qT, kT = sb(st, "na_qT", [P, T]), sb(st, "na_kT", [P, T])
                score = [sb(st, f"na_scores{s}", [P, T]) for s in range(2)]
                gain = sb(st, "na_gain", [P, 2])
                gl, based, gained = (sem(st, q) for q in ("gain_loaded", "bias_ready", "gain_ready"))
                block = st.enter_context(nc.Block())
                U = a.U

                @block.sync
                def _(sp):
                    for n, g in enumerate((na_q_g, na_k_g)):
                        for h in range(2):
                            sp.dma_start(gain[h * 64:(h + 1) * 64, n:n + 1], g[l].rearrange("(d o) -> d o", o=1)).then_inc(gl, 16)
                    sp.wait_ge(gl, 64)

                @block.gpsimd
                def _(pool):
                    for i in range(NA_HEADS // 2):
                        pool.wait_ge(bl[i], 80 if i == 0 else 64)
                        if i > 0:
                            pool.wait_ge(a.maxed, i * U)
                        for h in range(2):
                            last = nc.gpsimd.tensor_tensor(bst[:, h], bias[:, 2 * i + h, :].rearrange("p (j k) -> p j k", k=GRID_W),
                                                           colmask[:].unsqueeze(1).to_broadcast([P, 14, GRID_W]), ALU.add)
                        last.then_inc(based, 1)

                @block.tensor
                def _(pe):
                    def turn(i, n):
                        x, bank = ((qst, 0), (kst, 2))[n]
                        pe.wait_ge(a.staged, 2 * i + n + 1)
                        for t in range(x.shape[1]):
                            o = ps[:, bank, t * P:(t + 1) * P] if t < NL else ps[:, bank + 1, (t - NL) * P:(t - NL + 1) * P]
                            mm = nc.tensor.transpose(o, x[:, t].rearrange("p h d -> p (h d)"), ident[:])
                        mm.then_inc(a.q_turned, 1)

                    def pair(i, more):
                        pe.wait_ge(a.qk_kept, 2 * i + 2)

                        def scores(hh, t, bank):
                            r = slice(hh * 64, (hh + 1) * 64)
                            if t < NL:
                                nc.tensor.matmul(ps[:, bank, 0:S], qT[r, t * P:(t + 1) * P], kT[r, 0:S], start=True, stop=True)
                            return nc.tensor.matmul(ps[:, bank + 1, 0:L], qT[r, t * P:(t + 1) * P], kT[r, S:T], start=True, stop=True)

                        a.pe_units(pe, i, scores, lambda hh, k: proj[:, k, ds(C_NAV + (2 * i + hh) * 64, 64)],
                                   (lambda n: turn(i + 1, n)) if more else None)

                    turn(0, 0)
                    turn(0, 1)
                    iterations(pe, NA_HEADS // 2, pair)

                @block.vector
                def _(dve):
                    dve.wait_ge(gl, 64)
                    nc.vector.tensor_scalar(gain[:, 0:1], gain[:, 0:1], NA_DIM ** -0.5, None, ALU.mult).then_inc(gained, 1)
                    STEPS = 2 * NL + a.U

                    def stage(i):
                        dve.wait_ge(a.q_turned, 2 * i)
                        for n, (x, nt) in enumerate(((qst, nq), (kst, NT))):
                            nc.vector.tensor_tensor(x[:].rearrange("p t h d -> p t h d"),
                                                    proj[:, 0:nt, ds(n * NA_W + i * P, P)].rearrange("p t (h d) -> p t h d", d=64),
                                                    stat[:, 0:nt, ds(R_NA + 6 * n + 2 * i, 2)].unsqueeze(3).to_broadcast([P, nt, 2, 64]),
                                                    ALU.mult).then_inc(a.staged, 1)

                    def pair(i, more):
                        chain = Chain(dve, a.chain, i * STEPS)
                        dve.wait_ge(based, i + 1)

                        def maximum(hh, t, bank, s):
                            m = a.rowmax[:, s]
                            if t >= NL:
                                return nc.vector.tensor_reduce(m[:, 3:4], ps[:, bank + 1, 0:L], AX.X, ALU.max, negate=True)
                            j0 = 6 - 2 * t
                            nc.vector.tensor_scalar(score[s][:, S:T], ps[:, bank + 1, 0:L], 0.0, 3 * MASKED,
                                                    ALU.add, ALU.max, accum_out=m[:, 0:1])
                            chain.link(nc.vector.tensor_tensor_reduce(
                                score[s][:, 0:S], ps[:, bank, 0:S], bst[:, hh, j0:j0 + 8, :].rearrange("p j k -> p (j k)"),
                                1.0, 3 * MASKED, ALU.add, ALU.max, m[:, 1:2]))
                            return nc.vector.tensor_reduce(m[:, 3:4], m[:, 0:2], AX.X, ALU.max, negate=True)

                        a.dve_units(dve, i, chain, maximum, early=(lambda: stage(i + 1)) if more else None)
                        assert chain.n == STEPS, chain.n

                    stage(0)
                    iterations(dve, NA_HEADS // 2, pair)

                @block.scalar
                def _(act):
                    act.wait_ge(gained, 1)
                    def keep(i, n):
                        xT_, bank, w = ((qT, 0, nq * P), (kT, 2, T))[n]
                        act.wait_ge(a.q_turned, 2 * i + n + 1)
                        last = nc.scalar.mul(xT_[:, 0:S], ps[:, bank, 0:S], gain[:, n:n + 1])
                        if w > S:
                            last = nc.scalar.mul(xT_[:, S:T], ps[:, bank + 1, 0:L], gain[:, n:n + 1])
                        last.then_inc(a.qk_kept, 1)

                    def pair(i, more):
                        a.act_units(act, i, lambda t, bank, s: score[s][:] if t < NL else ps[:, bank + 1, 0:L], oT,
                                    early=(lambda n: keep(i + 1, n)) if more else None)

                    keep(0, 0)
                    keep(0, 1)
                    iterations(act, NA_HEADS // 2, pair)

        def windowed(l, proj, stat, oT, ahead, last_layer):
            nq = NL if last_layer else NT
            G = SWA_HEADS // SWA_KV_HEADS
            near = lambda t: list(range(max(t - 1, 0), min(t + 2, NL)))
            keys_of = lambda t: (near(t) if t < NL else []) + list(range(NL, NT))
            with Scope() as st:
                a = Attention(st, "sw", 2, SWA_DIM, list(range(nq)), keys_of)
                band = sb(st, "band", [P, 3 * P])
                cg, sg = [sb(st, f"sw_cos{n}", [P, NT, 64]) for n in range(2)], [sb(st, f"sw_sin{n}", [P, NT, 64]) for n in range(2)]
                g = [sb(st, f"sw_gain{n}", [P, 64]) for n in range(2)]
                sink, sink2 = sb(st, "sink", [P, SWA_HEADS]), sb(st, "sink_pair", [P, 2])
                raw, part, turn = (sb(st, f"sw_{q}", [P, NT, 2, 64]) for q in ("raw", "part", "roped"))
                qT, kT = sb(st, "sw_qT", [P, T]), sb(st, "sw_kT", [P, T])
                score = [sb(st, f"sw_scores{s}", [P, T]) for s in range(2)]
                gl = sem(st, "sw_consts_loaded")
                block = st.enter_context(nc.Block())
                U = a.U

                @block.sync
                def _(sp):
                    sp.dma_start(band[:], const["band"]).then_inc(gl, 16)
                    for n, v in enumerate((swa_q_g, swa_k_g)):
                        sp.dma_start(g[n][:], v[l:l + 1, :].to_broadcast([P, 64])).then_inc(gl, 16)
                    sp.dma_start(sink[:], swa_sink[l:l + 1, :].to_broadcast([P, SWA_HEADS])).then_inc(gl, 16)
                    ahead(sp)
                    sp.wait_ge(gl, 64)

                def turned(pe, nt):
                    for t in range(nt):
                        o = ps[:, 0, t * P:(t + 1) * P] if t < NL else ps[:, 1, (t - NL) * P:(t - NL + 1) * P]
                        mm = nc.tensor.transpose(o, turn[:, t].rearrange("p h d -> p (h d)"), ident[:])
                    mm.then_inc(a.q_turned, 1)

                @block.tensor
                def _(pe):
                    pe.wait_ge(a.staged, 1)
                    turned(pe, NT)
                    pe.wait_ge(a.qk_kept, 1)

                    def queries(i):
                        pe.wait_ge(a.staged, i + 2)
                        turned(pe, nq)

                    def group(i, more):
                        pe.wait_ge(a.qk_kept, i + 2)

                        def scores(hh, t, bank):
                            r = slice(hh * 64, (hh + 1) * 64)
                            if t < NL:
                                k = near(t)
                                nc.tensor.matmul(ps[:, bank, 0:len(k) * P], qT[r, t * P:(t + 1) * P],
                                                 kT[r, k[0] * P:(k[-1] + 1) * P], start=True, stop=True)
                            return nc.tensor.matmul(ps[:, bank + 1, 0:L], qT[r, t * P:(t + 1) * P], kT[r, S:T], start=True, stop=True)

                        a.pe_units(pe, i, scores, lambda hh, k: proj[:, k, C_SV + hh * 64:C_SV + (hh + 1) * 64],
                                   (lambda n: n or queries(i + 1)) if more else None)

                    queries(0)
                    iterations(pe, G, group)

                @block.vector
                def _(dve):
                    pre = Chain(dve, gl, 64)
                    dve.wait_ge(gl, 64)
                    rope_tables(pre, cg[0], sg[0], g[0], SWA_DIM ** -0.5)
                    rope_tables(pre, cg[1], sg[1], g[1], 1.0)
                    pre.link(nc.vector.tensor_tensor(raw[:], proj[:, :, C_SK:C_SV].rearrange("p t (h d) -> p t h d", d=64),
                                                     stat[:, :, R_SW + 6:R_SW + 8].unsqueeze(3).to_broadcast([P, NT, 2, 64]), ALU.mult))
                    rope(pre, turn[:], raw[:], part[:], cg[1], sg[1], NT, 2).then_inc(a.staged, 1)
                    STEPS = 3 + 3 * a.U

                    def stage(chain, i):
                        q = proj[:, 0:nq, C_SQ:C_SK].rearrange("p t (g j) -> p t g j", g=2)
                        r = stat[:, 0:nq, R_SW:R_SW + 6].rearrange("p t (g j) -> p t g j", g=2)
                        chain.link(nc.vector.tensor_tensor(raw[:, 0:nq], q[:, :, :, ds(i * 64, 64)],
                                                           r[:, :, :, ds(i, 1)].to_broadcast([P, nq, 2, 64]), ALU.mult))
                        dve.wait_ge(a.q_turned, i + 1)
                        rope(chain, turn[:, 0:nq], raw[:, 0:nq], part[:, 0:nq], cg[0], sg[0], nq, 2).then_inc(a.staged, 1)

                    def group(i, more):
                        chain = Chain(dve, a.chain, i * STEPS)
                        dve.wait_ge(a.exped, i * U)
                        chain.link(nc.vector.tensor_copy(sink2[:], sink[:].rearrange("p (g j) -> p g j", g=2)[:, :, ds(i, 1)].rearrange("p g j -> p (g j)")))

                        def maximum(hh, t, bank, s):
                            m = a.rowmax[:, s]
                            k = near(t) if t < NL else []
                            n = len(k) * P
                            last = nc.vector.tensor_scalar(score[s][:, n:n + L], ps[:, bank + 1, 0:L], 0.0, sink2[:, hh:hh + 1],
                                                           ALU.add, ALU.max, accum_out=m[:, 0:1])
                            if k:
                                b0 = (k[0] - t + 1) * P
                                last = nc.vector.tensor_tensor_reduce(score[s][:, 0:n], ps[:, bank, 0:n], band[:, b0:b0 + n],
                                                                      1.0, 3 * MASKED, ALU.add, ALU.max, m[:, 1:2])
                            chain.link(last)
                            return nc.vector.tensor_reduce(m[:, 3:4], m[:, 0:2 if k else 1], AX.X, ALU.max, negate=True)

                        a.dve_units(dve, i, chain, maximum, True, (lambda: stage(chain, i + 1)) if more else None)
                        assert not more or chain.n == STEPS, (chain.n, STEPS)

                    stage(pre, 0)
                    iterations(dve, G, group)

                @block.scalar
                def _(act):
                    act.wait_ge(a.q_turned, 1)
                    nc.scalar.copy(kT[:, 0:S], ps[:, 0, 0:S])
                    nc.scalar.copy(kT[:, S:T], ps[:, 1, 0:L]).then_inc(a.qk_kept, 1)

                    def queries(i):
                        act.wait_ge(a.q_turned, i + 2)
                        last = nc.scalar.copy(qT[:, 0:S], ps[:, 0, 0:S])
                        if nq > NL:
                            last = nc.scalar.copy(qT[:, S:T], ps[:, 1, 0:L])
                        last.then_inc(a.qk_kept, 1)

                    def group(i, more):

                        def sink_exp(hh, u):
                            nc.scalar.activation(a.rowsum[:, u % 4, 2:3], sink2[:, hh:hh + 1], ACT.Exp, bias=a.rowmax[:, u % 2, 3:4])

                        a.act_units(act, i, lambda t, bank, s: score[s][:, 0:len(keys_of(t)) * P], oT, sink_exp,
                                    (lambda n: n or queries(i + 1)) if more else None)

                    queries(0)
                    iterations(act, G, group)

        def latent(l, proj, stat, oT, last_layer):
            nq = NL if last_layer else NT
            keys_of = lambda t: (list(range(NL)) if t < NL else []) + list(range(NL, NT))
            QC = MLA_Q_RANK // P
            with Scope() as st:
                a = Attention(st, "mla", 1, MLA_V, list(range(nq)), keys_of)
                wuq, wukv = sb(st, "w_uq", [P, QC, MLA_HEADS * MLA_QK]), sb(st, "w_ukv", [P, MLA_HEADS * 256])
                cg, sg = [sb(st, f"mla_cos{n}", [P, NT, 64]) for n in range(2)], [sb(st, f"mla_sin{n}", [P, NT, 64]) for n in range(2)]
                g = [sb(st, f"mla_gain{n}", [P, 64]) for n in range(2)]
                gain = sb(st, "mla_gains", [P, 2 + QC + 1])
                shared = sb(st, "mla_shared", [P, max(NT * (QC + 1) * P, (NT + nq) * MLA_QK)])
                rank = shared[:, 0:NT * (QC + 1) * P].rearrange("p (t w) -> p t w", t=NT)
                sq = shared[:, 0:NT * MLA_QK].rearrange("p (t w) -> p t w", t=NT)
                qst = shared[:, NT * MLA_QK:(NT + nq) * MLA_QK].rearrange("p (t w) -> p t w", t=nq)
                cT_ = sb(st, "rank_T", [P, QC + 1, T])
                krope = sb(st, "k_roped", [P, NT, 1, 64])
                kst, vst = sb(st, "mla_k", [P, NT, P]), sb(st, "mla_v", [P, NT, P])
                part, kr = sq[:, :, 0:64].unsqueeze(2), sq[:, :, P:MLA_QK]
                r2 = sb(st, "mla_rstd", [P, 2, NT])
                qr = sb(st, "mla_q_rope", [P, nq, 1, 64])
                qT, kT = sb(st, "mla_qT", [P, T]), sb(st, "mla_kT", [P, T])
                qrT, krT = sb(st, "mla_qrT", [64, T]), sb(st, "mla_krT", [64, T])
                gl, wl, rt, root, upped, unpacked = (sem(st, q) for q in ("mla_consts_loaded", "w_u_loaded", "ranks_turned", "mla_root", "upped", "unpacked"))
                rk = [sem(st, "ranks_kept_act"), sem(st, "ranks_kept_dve")]
                kept_k = sem(st, "k_kept")
                block = st.enter_context(nc.Block())
                U = a.U
                ctx_kept = lambda q: sum(1 for c in range(q + 1) if c == QC or nq > NL)

                @block.sync
                def _(sp):
                    col = lambda v: v.rearrange("(d o) -> d o", o=1)
                    sp.dma_start(gain[:, 0:1], col(mla_q_g[l, 0:P])).then_inc(gl, 16)
                    sp.dma_start(gain[:, 1:2], col(mla_k_g[l, 0:P])).then_inc(gl, 16)
                    for q in range(QC):
                        sp.dma_start(gain[:, 2 + q:3 + q], col(mla_q_norm[l, q * P:(q + 1) * P])).then_inc(gl, 16)
                    sp.dma_start(gain[:, 2 + QC:3 + QC], col(mla_kv_norm[l])).then_inc(gl, 16)
                    for n, v in enumerate((mla_q_g, mla_k_g)):
                        sp.dma_start(g[n][:], v[l:l + 1, P:MLA_QK].to_broadcast([P, 64])).then_inc(gl, 16)
                    sp.dma_start(wuq[:], mla_w_uq[l].rearrange("(k p) n -> p k n", p=P)).then_inc(wl, 16)
                    sp.dma_start(wukv[:], mla_w_ukv[l]).then_inc(wl, 16)
                    sp.wait_ge(gl, 16 * (5 + QC))

                @block.tensor
                def _(pe):
                    pe.wait_ge(a.staged, 1)
                    for q in range(QC + 1):
                        b = 2 * (q % 2)
                        if q >= 2:
                            pe.wait_ge(rk[0], q - 1)
                            if ctx_kept(q - 2):
                                pe.wait_ge(rk[1], ctx_kept(q - 2))
                        for t in range(nq if q < QC else NT):
                            mm = nc.tensor.transpose(ps[:, b + t // NL, (t % NL) * P:(t % NL + 1) * P],
                                                     rank[:, t, q * P:(q + 1) * P], ident[:])
                        mm.then_inc(rt, 1)
                    pe.wait_ge(wl, 32)
                    pe.wait_ge(rk[0], QC + 1)
                    pe.wait_ge(rk[1], ctx_kept(QC))
                    with pe.Fori(0, MLA_HEADS) as i:
                        pe.wait_ge(a.exped, i * U)
                        pe.wait_ge(a.kept_lo, i * U)
                        pe.wait_ge(a.kept_hi, i * U)
                        pe.wait_ge(a.o_kept, i)
                        for t in range(nq):
                            for q in range(QC):
                                mm = nc.tensor.matmul(ps[:, t // 2, (t % 2) * MLA_QK:(t % 2 + 1) * MLA_QK],
                                                      cT_[:, q, t * P:(t + 1) * P], wuq[:, q, ds(i * MLA_QK, MLA_QK)],
                                                      start=(q == 0), stop=(q == QC - 1))
                        mm.then_inc(upped, 1)
                        for t in range(NT):
                            mm = nc.tensor.matmul(ps[:, 3 + t // 2, (t % 2) * 256:(t % 2 + 1) * 256],
                                                  cT_[:, QC, t * P:(t + 1) * P], wukv[:, ds(i * 256, 256)], start=True, stop=True)
                        mm.then_inc(upped, 1)
                        pe.wait_ge(unpacked, 2 * i + 2)
                        for n, (x, bank) in enumerate(((qst[:, :, 0:P], 4), (kst[:], 6), (qr[:, :, 0, :], 0), (kr, 2))):
                            if n < 2:
                                pe.wait_ge(a.staged, 4 * i + (2, 5)[n])
                            w = x.shape[2]
                            for t in range(x.shape[1]):
                                mm = nc.tensor.transpose(ps[0:w, bank + t // NL, (t % NL) * P:(t % NL + 1) * P], x[:, t, :], ident[:])
                            mm.then_inc(a.q_turned, 1)
                        pe.wait_ge(a.qk_kept, 2 * i + 2)
                        pe.wait_ge(kept_k, 2 * i + 2)

                        def scores(hh, t, bank):
                            q0 = slice(t * P, (t + 1) * P)
                            for b, c0, n in ([(bank, 0, S)] if t < NL else []) + [(bank + 1, S, L)]:
                                nc.tensor.matmul(ps[:, b, 0:n], qT[:, q0], kT[:, c0:c0 + n], start=True, stop=False)
                                mm = nc.tensor.matmul(ps[:, b, 0:n], qrT[:, q0], krT[:, c0:c0 + n], start=False, stop=True)
                            return mm

                        a.pe_units(pe, i, scores, lambda hh, k: vst[:, k, :])

                @block.vector
                def _(dve):
                    pre = Chain(dve, gl, 16 * (5 + QC))
                    dve.wait_ge(gl, 16 * (5 + QC))
                    pre.link(nc.vector.tensor_scalar(gain[:, 0:1], gain[:, 0:1], MLA_QK ** -0.5, None, ALU.mult))
                    rope_tables(pre, cg[0], sg[0], g[0], MLA_QK ** -0.5)
                    rope_tables(pre, cg[1], sg[1], g[1], 1.0)
                    for t in range(NT):
                        if t < nq:
                            nc.vector.tensor_scalar(rank[:, t, 0:QC * P], proj[:, t, C_CQ:C_CKV], stat[:, t, R_CQ:R_CQ + 1], None, ALU.mult)
                        last = nc.vector.tensor_scalar(rank[:, t, QC * P:], proj[:, t, C_CKV:C_KR], stat[:, t, R_CKV:R_CKV + 1], None, ALU.mult)
                    last.then_inc(a.staged, 1)
                    rope(pre, krope[:], proj[:, :, C_KR:C_SQ].rearrange("p t (o d) -> p t o d", o=1), vst[:, :, 0:64].unsqueeze(2), cg[1], sg[1], NT, 1)\
                        .then_inc(gl, 1)
                    pre.n += 1
                    for q in range(QC + 1):
                        dve.wait_ge(rt, q + 1)
                        b = 2 * (q % 2)
                        if q == QC or nq > NL:
                            nc.vector.tensor_scalar(cT_[:, q, S:T], ps[:, b + 1, 0:L], gain[:, 2 + q:3 + q], None, ALU.mult).then_inc(rk[1], 1)
                    dve.wait_ge(gl, 16 * (5 + QC) + pre.n)
                    dve.wait_ge(rk[1], ctx_kept(QC))
                    STEPS = 7 + a.U
                    with dve.Fori(0, MLA_HEADS) as i:
                        chain = Chain(dve, a.chain, i * STEPS)
                        dve.wait_ge(upped, 2 * i + 2)
                        for b in range(3):
                            kv = ps[:, 3 + b, :].rearrange("p (t w) -> p t w", w=256)
                            nc.vector.tensor_copy(kst[:, 2 * b:2 * b + 2, :], kv[:, :, 0:P])
                            last = nc.vector.tensor_copy(vst[:, 2 * b:2 * b + 2, :], kv[:, :, P:256])
                        last.then_inc(unpacked, 1)
                        chain.link(nc.vector.tensor_copy(r2[:, 0], stat[:, :, 0]))
                        dve.wait_ge(unpacked, 2 * i + 2)
                        chain.link(nc.vector.tensor_tensor(sq[:, 0:nq, :], qst, qst, ALU.mult))
                        chain.link(nc.vector.tensor_reduce(r2[:, 0, 0:nq], sq[:, 0:nq, :], AX.X, ALU.add))
                        chain.link(nc.vector.tensor_tensor(sq[:, :, 0:P], kst[:], kst[:], ALU.mult))
                        chain.link(nc.vector.tensor_reduce(r2[:, 1], sq[:, :, 0:P], AX.X, ALU.add))
                        chain.link(nc.vector.tensor_tensor(r2[:, 1], r2[:, 1], stat[:, :, R_KR], ALU.add))
                        nc.vector.tensor_scalar(r2[:], r2[:], 1.0 / MLA_QK, EPS, ALU.mult, ALU.add).then_inc(root, 1)
                        dve.wait_ge(root, 3 * i + 2)
                        nc.vector.reciprocal(r2[:], r2[:]).then_inc(root, 1)
                        dve.wait_ge(root, 3 * i + 3)
                        nc.vector.tensor_tensor(kst[:], kst[:], r2[:, 1].unsqueeze(2).to_broadcast([P, NT, P]), ALU.mult)
                        nc.vector.tensor_tensor(kr, krope[:, :, 0, :], r2[:, 1].unsqueeze(2).to_broadcast([P, NT, 64]), ALU.mult)
                        nc.vector.tensor_tensor(qst, qst, r2[:, 0, 0:nq].unsqueeze(2).to_broadcast([P, nq, MLA_QK]), ALU.mult).then_inc(a.staged, 1)
                        dve.wait_ge(a.staged, 4 * i + 2)
                        rope(chain, qr[:], qst[:, :, P:MLA_QK].unsqueeze(2), part[:, 0:nq], cg[0], sg[0], nq, 1).then_inc(a.staged, 3)
                        for n, (w, x_, bank) in enumerate(((P, kT, 6), (64, krT, 2))):
                            dve.wait_ge(a.q_turned, 4 * i + 2 * n + 2)
                            for c0, m, b in ((0, S, bank), (S, L, bank + 1)):
                                if n == 0:
                                    last = nc.vector.tensor_scalar(x_[:, c0:c0 + m], ps[:, b, 0:m], gain[:, 1:2], None, ALU.mult)
                                else:
                                    last = nc.vector.tensor_copy(x_[:, c0:c0 + m], ps[0:w, b, 0:m])
                            last.then_inc(kept_k, 1)

                        def maximum(hh, t, bank, s):
                            src = ps[:, bank:bank + 2, :].rearrange("p a b -> p (a b)")[:, 0:T] if t < NL else ps[:, bank + 1, 0:L]
                            return nc.vector.tensor_reduce(a.rowmax[:, s, 3:4], src, AX.X, ALU.max, negate=True)

                        a.dve_units(dve, i, chain, maximum)
                        assert chain.n == STEPS, chain.n

                @block.scalar
                def _(act):
                    for q in range(QC + 1):
                        act.wait_ge(rt, q + 1)
                        if q == 0:
                            act.wait_ge(gl, 16 * (5 + QC))
                        nc.scalar.mul(cT_[:, q, 0:S], ps[:, 2 * (q % 2), 0:S], gain[:, 2 + q:3 + q]).then_inc(rk[0], 1)
                    with act.Fori(0, MLA_HEADS) as i:
                        act.wait_ge(upped, 2 * i + 1)
                        for b in range(nq // 2):
                            last = nc.scalar.copy(qst[:, 2 * b:2 * b + 2, :], ps[:, b, 0:2 * MLA_QK].rearrange("p (t w) -> p t w", w=MLA_QK))
                        last.then_inc(unpacked, 1)
                        act.wait_ge(root, 3 * i + 1)
                        nc.scalar.activation(r2[:], r2[:], ACT.Sqrt).then_inc(root, 1)
                        for n, (w, x_, bank) in enumerate(((P, qT, 4), (64, qrT, 0))):
                            act.wait_ge(a.q_turned, 4 * i + 2 * n + 1)
                            for c0, m, b in ((0, S, bank), (S, L, bank + 1))[:1 if nq == NL else 2]:
                                if n == 0:
                                    last = nc.scalar.mul(x_[:, c0:c0 + m], ps[:, b, 0:m], gain[:, 0:1])
                                else:
                                    last = nc.scalar.copy(x_[:, c0:c0 + m], ps[0:w, b, 0:m])
                            last.then_inc(a.qk_kept, 1)
                        a.act_units(act, i, lambda t, bank, s: ps[:, bank:bank + 2, :].rearrange("p a b -> p (a b)")[:, 0:T]
                                    if t < NL else ps[:, bank + 1, 0:L], oT)

        def merge(l, hT, oT, mT, ctx_too):
            W = T if ctx_too else S
            rows = ((w_na_o, 0, 3), (w_mla_o, 6, 4), (w_swa_o, 3, 3))
            RAW, SPLIT = 3, 2
            with Scope() as st:
                h_hi, h_lo = (sb(st, f"hm_{q}", [P, KD, W], F32R) for q in ("hi", "lo"))
                wg = [sb(st, f"w_gates{s}", [P, KD, P]) for s in range(RAW)]
                w_hi, w_lo = ([sb(st, f"w_gates_{q}{s}", [P, KD, P], F32R) for s in range(SPLIT)] for q in ("hi", "lo"))
                wy = [sb(st, f"w_branch{s}", [P, 10, P]) for s in range(2)]
                sig = [sb(st, f"gate{s}", [P, W]) for s in range(2)]
                prod = sb(st, "gated", [P, W])
                gl = [sem(st, f"w_gates_loaded{s}") for s in range(RAW)]
                yl = [sem(st, f"w_branch_loaded{s}") for s in range(2)]
                h_hi_made, h_lo_made, w_hi_made, w_lo_made = (sem(st, "merge_" + q) for q in ("h_hi", "h_lo", "w_hi", "w_lo"))
                logits, ys, sigs, gated, ch = (sem(st, q) for q in ("logits", "branch_out", "gates", "gated", "merge_chain"))
                block = st.enter_context(nc.Block())
                UN = 2 * 3
                NI = KD // 2
                units = [(dc, b) for dc in range(2) for b in range(3)]

                @block.sync
                def _(sp):
                    def load(i, u):
                        dc, b = units[u]
                        n = i * UN + u
                        c0 = i * 2 * P + dc * P
                        if b == 0:
                            if not isinstance(i, int):
                                sp.wait_ge(ys, n - 3)
                            for w, q0, nq in rows[:2]:
                                sp.dma_start(wy[dc][:, q0:q0 + nq], w[l].rearrange("(k p) n -> p k n", p=P)[:, :, ds(c0, P)]).then_inc(yl[dc], 16)
                            for g in range(2):
                                sp.dma_start(wy[dc][g * 64:(g + 1) * 64, 3:6],
                                             w_swa_o[l].rearrange("(g j d) n -> g d j n", g=2, d=64)[g][:, :, ds(c0, P)]).then_inc(yl[dc], 16)
                        if not isinstance(i, int) or u >= RAW:
                            sp.wait_ge(w_lo_made, n - RAW + 1)
                        sp.dma_start(wg[u % RAW][:], w_in[l].rearrange("(k p) n -> p k n", p=P)[:, :, ds(C_GL + b * D + c0, P)]).then_inc(gl[u % RAW], 16)
                    for u in range(UN):
                        load(0, u)
                    with sp.Fori(1, NI) as i:
                        for u in range(UN):
                            load(i, u)

                @block.tensor
                def _(pe):
                    with pe.Fori(0, NI) as i:
                        for u, (dc, b) in enumerate(units):
                            n = i * UN + u
                            pe.wait_ge(gated, n - 1 if u >= 1 else n)
                            pe.wait_ge(w_hi_made, n + 1)
                            pe.wait_ge(w_lo_made, n + 1)
                            b0 = 4 * (u % 2)
                            for k in range(KD):
                                if u == 0:
                                    pe.wait_ge(h_hi_made, k + 1)
                                    pe.wait_ge(h_lo_made, k + 1)
                                for w, h in ((w_hi, h_hi), (w_hi, h_lo), (w_lo, h_hi)):
                                    for z, t0, m in streams(ctx_too):
                                        mm = nc.tensor.matmul(ps[:, b0 + z, 0:m], w[u % SPLIT][:, k, :], h[:, k, t0:t0 + m],
                                                              start=(k == 0 and w is w_hi and h is h_hi), stop=(k == KD - 1 and w is w_lo))
                            mm.then_inc(logits, 1)
                            if b == 0:
                                pe.wait_ge(yl[dc], 64 * i + 64)
                            _, q0, nq = rows[b]
                            for z, t0, m in streams(ctx_too):
                                for q in range(nq):
                                    mm = nc.tensor.matmul(ps[:, b0 + 2 + z, 0:m], wy[dc][:, q0 + q, :], oT[:, q0 + q, t0:t0 + m],
                                                          start=(q == 0), stop=(q == nq - 1))
                            mm.then_inc(ys, 1)

                @block.scalar
                def _(act):
                    for k in range(KD):
                        nc.scalar.copy(h_hi[:, k, :], hT[:, k, 0:W]).then_inc(h_hi_made, 1)
                    with act.Fori(0, NI) as i:
                        for u in range(UN):
                            n = i * UN + u
                            act.wait_ge(gl[u % RAW], 16 * (UN // RAW * i + u // RAW + 1))
                            act.wait_ge(logits, n - 1 if u >= 1 else n)
                            nc.scalar.copy(w_hi[u % SPLIT][:], wg[u % RAW][:]).then_inc(w_hi_made, 1)
                            act.wait_ge(logits, n + 1)
                            act.wait_ge(gated, n - 1 if u >= 1 else n)
                            for z, t0, m in streams(ctx_too):
                                last = nc.scalar.activation(sig[u % 2][:, t0:t0 + m], ps[:, 4 * (u % 2) + z, 0:m], ACT.Sigmoid)
                            last.then_inc(sigs, 1)

                @block.vector
                def _(dve):
                    for k in range(KD):
                        dve.wait_ge(h_hi_made, k + 1)
                        nc.vector.tensor_tensor(h_lo[:, k, :], hT[:, k, 0:W], h_hi[:, k, :].bitcast(F32), ALU.subtract).then_inc(h_lo_made, 1)
                    STEPS = 4
                    with dve.Fori(0, NI) as i:
                        chain = Chain(dve, ch, i * STEPS)

                        def split(u):
                            dve.wait_ge(w_hi_made, i * UN + u + 1)
                            nc.vector.tensor_tensor(w_lo[u % SPLIT][:], wg[u % RAW][:], w_hi[u % SPLIT][:].bitcast(F32), ALU.subtract).then_inc(w_lo_made, 1)

                        def gate(u):
                            dc, b = units[u]
                            dve.wait_ge(sigs, i * UN + u + 1)
                            dve.wait_ge(ys, i * UN + u + 1)
                            m_ = mT[:, ds(2 * i + dc, 1), :].rearrange("p o t -> p (o t)")
                            if b > 0:
                                dve.wait_ge(gated, i * UN + u)
                            for z, t0, m in streams(ctx_too):
                                last = nc.vector.tensor_tensor(m_[:, t0:t0 + m] if b == 0 else prod[:, t0:t0 + m], sig[u % 2][:, t0:t0 + m],
                                                               ps[:, 4 * (u % 2) + 2 + z, 0:m], ALU.mult)
                            if b > 0:
                                chain.link(last)
                                last = nc.vector.tensor_tensor(m_[:, 0:W], m_[:, 0:W], prod[:], ALU.add)
                            last.then_inc(gated, 1)

                        for u in range(UN):
                            split(u)
                            if u >= 1:
                                gate(u - 1)
                        gate(UN - 1)
                        assert chain.n == STEPS

        def output_projection(l, mT, ctx_too):
            W = T if ctx_too else S
            RAW, SPLIT = 3, 2
            with Scope() as st:
                m_hi, m_lo = (sb(st, f"m_{q}", [P, KD, W], F32R) for q in ("hi", "lo"))
                w = [sb(st, f"w_o{s}", [P, KD, P]) for s in range(RAW)]
                w_hi, w_lo = ([sb(st, f"w_o_{q}{s}", [P, KD, P], F32R) for s in range(SPLIT)] for q in ("hi", "lo"))
                wl = [sem(st, f"w_o_loaded{s}") for s in range(RAW)]
                m_hi_made, m_lo_made, w_hi_made, w_lo_made = (sem(st, "w_o_" + q) for q in ("m_hi", "m_lo", "w_hi", "w_lo"))
                multiplied, added = sem(st, "w_o_multiplied"), sem(st, "w_o_added")
                block = st.enter_context(nc.Block())

                @block.sync
                def _(sp):
                    for d in range(KD):
                        if d >= RAW:
                            sp.wait_ge(w_lo_made, d - RAW + 1)
                        sp.dma_start(w[d % RAW][:], w_o[l].rearrange("(k p) n -> p k n", p=P)[:, :, d * P:(d + 1) * P]).then_inc(wl[d % RAW], 16)

                @block.tensor
                def _(pe):
                    for d in range(KD):
                        if d >= 2:
                            pe.wait_ge(added, d - 1)
                        pe.wait_ge(w_hi_made, d + 1)
                        pe.wait_ge(w_lo_made, d + 1)
                        for k in range(KD):
                            if d == 0:
                                pe.wait_ge(m_hi_made, k + 1)
                                pe.wait_ge(m_lo_made, k + 1)
                            for w_, x in ((w_hi, m_hi), (w_hi, m_lo), (w_lo, m_hi)):
                                for z, t0, m in streams(ctx_too):
                                    mm = nc.tensor.matmul(ps[:, 2 * (d % 2) + z, 0:m], w_[d % SPLIT][:, k, :], x[:, k, t0:t0 + m],
                                                          start=(k == 0 and w_ is w_hi and x is m_hi), stop=(k == KD - 1 and w_ is w_lo))
                        mm.then_inc(multiplied, 1)

                @block.scalar
                def _(act):
                    def round_(d):
                        act.wait_ge(wl[d % RAW], 16 * (d // RAW + 1))
                        if d >= SPLIT:
                            act.wait_ge(multiplied, d - SPLIT + 1)
                        nc.scalar.copy(w_hi[d % SPLIT][:], w[d % RAW][:]).then_inc(w_hi_made, 1)

                    for k in range(KD):
                        nc.scalar.copy(m_hi[:, k, :], mT[:, k, 0:W]).then_inc(m_hi_made, 1)
                        if k in (3, 4):
                            round_(k - 3)
                    for d in range(SPLIT, KD):
                        round_(d)

                @block.vector
                def _(dve):
                    def add(d):
                        dve.wait_ge(multiplied, d + 1)
                        for z, t0, m in streams(ctx_too):
                            last = nc.vector.scalar_tensor_tensor(xT[:, d, t0:t0 + m], ps[:, 2 * (d % 2) + z, 0:m],
                                                                  modT[:, 2 * KD + d, z:z + 1], xT[:, d, t0:t0 + m], ALU.mult, ALU.add)
                        last.then_inc(added, 1)

                    def split(d):
                        dve.wait_ge(w_hi_made, d + 1)
                        nc.vector.tensor_tensor(w_lo[d % SPLIT][:], w[d % RAW][:], w_hi[d % SPLIT][:].bitcast(F32), ALU.subtract).then_inc(w_lo_made, 1)

                    for k in range(KD):
                        dve.wait_ge(m_hi_made, k + 1)
                        nc.vector.tensor_tensor(m_lo[:, k, :], mT[:, k, 0:W], m_hi[:, k, :].bitcast(F32), ALU.subtract).then_inc(m_lo_made, 1)
                        if k in (3, 4):
                            split(k - 3)
                    for d in range(SPLIT, KD):
                        split(d)
                        add(d - SPLIT)
                    for d in range(KD - SPLIT, KD):
                        add(d)

        def route(l, h2T, h2, aff, posm, posT, ctx_too):
            nt = NT if ctx_too else NL
            E = N_EXPERTS
            with Scope() as st:
                wr = sb(st, "router", [P, KD, E])
                affT = sb(st, "affinity_by_expert", [E, T])
                count = sb(st, "slot_count", [E, T])
                small = sb(st, "route_small", [P, 2, nt])
                left = sb(st, "left", [E, T])
                top8 = sb(st, "top8", [E, 8])
                zero = sb(st, "zero", [E, S])
                wl, lg, ch, ex, at, hk, ht, kept, pt, zs = (sem(st, q) for q in (
                    "router_loaded", "logits", "route_chain", "aff_exp", "aff_turned", "tokens_kept", "tokens_turned", "aff_kept", "pos_turned", "zeroed"))
                block = st.enter_context(nc.Block())

                @block.sync
                def _(sp):
                    sp.dma_start(wr[:], router[l].rearrange("(k p) e -> p k e", p=P)).then_inc(wl, 16)
                    sp.wait_ge(wl, 16)

                @block.gpsimd
                def _(pool):
                    nc.gpsimd.memset(zero[:], 0.0).then_inc(zs, 1)
                    nc.gpsimd.memset(posm[:], 0.0).then_inc(zs, 1)

                @block.tensor
                def _(pe):
                    pe.wait_ge(wl, 16)
                    for t in range(nt):
                        for k in range(KD):
                            mm = nc.tensor.matmul(ps[:, 0, t * E:(t + 1) * E], h2T[:, k, t * P:(t + 1) * P], wr[:, k, :],
                                                  start=(k == 0), stop=(k == KD - 1))
                    mm.then_inc(lg, 1)

                    def tokens(g):
                        if g >= 4:
                            pe.wait_ge(hk, g - 3)
                        t, half = g // 2, g % 2
                        for q in range(4):
                            k = 4 * half + q
                            mm = nc.tensor.transpose(ps[:, 2 + g % 4, q * P:(q + 1) * P], h2T[:, k, t * P:(t + 1) * P], ident[:])
                        mm.then_inc(ht, 1)
                    for g in range(4):
                        tokens(g)
                    pe.wait_ge(ex, 2)
                    for t in range(nt):
                        mm = nc.tensor.transpose(ps[0:E, 6 + t // NL, (t % NL) * P:(t % NL + 1) * P], aff[:, t, :], ident[:])
                    mm.then_inc(at, 1)
                    for g in range(4, 2 * nt):
                        tokens(g)
                    pe.wait_ge(pt, 1 + ctx_too)
                    for t in range(nt):
                        mm = nc.tensor.transpose(ps[:, 0, t * E:(t + 1) * E], posT[:, t * P:(t + 1) * P].bitcast(F32), ident[0:E, 0:E])
                    mm.then_inc(at, 1)

                @block.scalar
                def _(act):
                    act.wait_ge(ch, 2)
                    nc.scalar.activation(aff[:], aff[:], ACT.Exp).then_inc(ex, 1)
                    for g in range(2 * nt):
                        act.wait_ge(ht, g + 1)
                        nc.scalar.copy(h2[:, g // 2, (g % 2) * 512:(g % 2 + 1) * 512], ps[:, 2 + g % 4, :]).then_inc(hk, 1)

                @block.vector
                def _(dve):
                    chain = Chain(dve, ch)
                    dve.wait_ge(lg, 1)
                    raw = ps[:, 0, 0:nt * E].rearrange("p (t e) -> p t e", e=E)
                    chain.link(nc.vector.tensor_reduce(small[:, 0], raw, AX.X, ALU.max))
                    nc.vector.tensor_tensor(aff[:], raw, small[:, 0].unsqueeze(2).to_broadcast([P, nt, E]), ALU.subtract).then_inc(ch, 1)
                    dve.wait_ge(ex, 1)
                    chain.n += 1
                    chain.link(nc.vector.tensor_reduce(small[:, 0], aff[:], AX.X, ALU.add))
                    chain.link(nc.vector.reciprocal(small[:, 1], small[:, 0]))
                    nc.vector.tensor_tensor(aff[:], aff[:], small[:, 1].unsqueeze(2).to_broadcast([P, nt, E]), ALU.mult).then_inc(ex, 1)
                    dve.wait_ge(at, 1)
                    for z, t0, m in streams(ctx_too):
                        last = nc.vector.tensor_copy(affT[:, t0:t0 + m], ps[0:E, 6 + z, 0:m])
                    chain.link(last)
                    dve.wait_ge(zs, 2)
                    for z, t0, m in streams(ctx_too):
                        cur, rest = affT[:, t0:t0 + m], left[:, t0:t0 + m]
                        chain.link(nc.vector.max(top8[:], cur))
                        chain.link(nc.vector.match_replace(rest, top8[:], cur, -1.0))
                        rounds = (KL, KC)[z] // 8 - 1
                        for _ in range(rounds):
                            chain.link(nc.vector.max(top8[:], rest))
                            chain.link(nc.vector.match_replace(rest, top8[:], rest, -1.0))
                        chain.link(nc.vector.tensor_tensor(rest, rest, cur, ALU.not_equal))
                        chain.link(nc.vector.tensor_tensor_scan(count[:, t0:t0 + m], rest, zero[:, 0:m], 0.0, ALU.add, ALU.add))
                        last = nc.vector.tensor_tensor(posT[:, t0:t0 + m], count[:, t0:t0 + m], rest, ALU.mult)
                        last.then_inc(pt, 1)
                    dve.wait_ge(at, 2)
                    nc.vector.tensor_copy(posm[:, 0:nt, 0:E], ps[:, 0, 0:nt * E].rearrange("p (t e) -> p t e", e=E))

        class Ring:
            UNITS, SLOTS = 24, 6
            ORDER = [(s, j, kh) for s in range(2) for j in range(4) for kh in range(2)] + \
                    [(s, j, kh) for s in range(2) for j in range(4, 6) for kh in range(2)]

            def __init__(self, st):
                self.slot = [sb(st, f"w_expert{j}", [P, KD // 2, 512]) for j in range(self.SLOTS)]
                self.loaded = [sem(st, f"w_expert_loaded{j}") for j in range(self.SLOTS)]

            def load(self, sp, l, chunk, q):
                s, j, kh = self.ORDER[q % self.UNITS]
                w = (w_gate, w_up, w_gate, w_up, w_down, w_down)[j]
                half = (0, 0, 1, 1, 0, 1)[j]
                src = w[l].rearrange("e (k p) n -> p (e k) n", p=P)
                sp.dma_start(self.slot[q % self.SLOTS][:], src[:, ds(chunk[2 * s + kh], KD // 2), half * 512:(half + 1) * 512])\
                    .then_inc(self.loaded[q % self.SLOTS], 16)

        def experts(l, ring, h2, aff, posm, posT, ctx_too):
            E = N_EXPERTS
            M = MS if ctx_too else KL
            W = T if ctx_too else S
            zs_ = streams(ctx_too)
            KZ = (KL, KC)
            Q, AHEAD = ring.UNITS, 3
            with Scope() as st:
                slots, slot_of = sb(st, "slots", [P, KL]), sb(st, "slot_of", [P, 2])
                sel = sb(st, "pick_pair", [E, 2 * MS], F32R)
                w_hi, w_lo = ([sb(st, f"w_{q}{s}", [P, KD // 2, 512], F32R) for s in range(AHEAD)] for q in ("hi", "lo"))
                oh = [sb(st, f"one_hot{z}", [P, (S, L)[z] // P, 2, KZ[z]]) for z, _, _ in zs_]
                xg_hi, xg_lo = (sb(st, f"gathered_{q}", [P, KD, 2, M], F32R) for q in ("hi", "lo"))
                act_ = [sb(st, f"hidden{s}", [M, FF]) for s in range(2)]
                aT_hi, aT_lo = ([sb(st, f"hidden_T_{q}{s}", [P, FF // P, M], F32R) for s in range(2)] for q in ("hi", "lo"))
                y_hi, y_lo = ([sb(st, f"expert_out_{q}{z}", [2 * KZ[z], D], F32R) for z, _, _ in zs_] for q in ("hi", "lo"))
                gate, gate_next = sb(st, "gate", [P, 2]), sb(st, "gate_next", [P, 2])
                G = sb(st, "scatter", [P, W], F32R)
                consts, picked, one_hot, gathered = (sem(st, "moe_" + q) for q in ("consts_loaded", "picked", "one_hot", "gathered"))
                xg_hi_made, xg_lo_made, w_hi_made = (sem(st, "moe_" + q) for q in ("xg_hi", "xg_lo", "w_hi"))
                w_lo_made = [sem(st, "moe_w_lo_" + q) for q in ("dve", "pool")]
                multiplied, silued, hidden, turned = (sem(st, "moe_" + q) for q in ("multiplied", "silued", "hidden", "turned"))
                aT_hi_made, aT_lo_made, y_hi_made, y_lo_made = (sem(st, "moe_" + q) for q in ("aT_hi", "aT_lo", "y_hi", "y_lo"))
                gates = sem(st, "moe_gates")
                spread, scatter, scattered, added = (sem(st, "moe_" + q) for q in ("spread", "scatter", "scattered", "added"))
                block = st.enter_context(nc.Block())
                NP = E // 2
                GATES = 4 * M
                order = [(z, t0, m, d) for d in range(KD) for z, t0, m in zs_]
                NS = len(order)

                BY_POOL = (0, 1, 2, 8, 14, 20)
                by = [[q for q in range(Q) if (q in BY_POOL) == p] for p in (False, True)]

                def lo_made(eng, i, q):
                    p = q % Q in BY_POOL
                    eng.wait_ge(w_lo_made[p], len(by[p]) * (i + q // Q) + by[p].index(q % Q) + 1)

                def split(eng, subtract, i, q):
                    if (eng is nc.gpsimd) != (q % Q in BY_POOL):
                        return
                    eng.wait_ge(w_hi_made, Q * i + q + 1)
                    subtract(w_lo[q % AHEAD][:], ring.slot[q % ring.SLOTS][:], w_hi[q % AHEAD][:].bitcast(F32),
                             ALU.subtract).then_inc(w_lo_made[q % Q in BY_POOL], 1)

                def pairs(eng, body):
                    with eng.Fori(0, NP - 1) as i:
                        body(i, Q + AHEAD)
                    body(NP - 1, Q)

                @block.sync
                def _(sp):
                    sp.dma_start(slots[:], const["slots"]).then_inc(consts, 16)
                    sp.dma_start(slot_of[:], const["slot_of"]).then_inc(consts, 16)

                    def load(i, q):
                        if q >= ring.SLOTS:
                            lo_made(sp, i, q - ring.SLOTS)
                        else:
                            lo_made(sp, i - 1, q - ring.SLOTS + Q)
                        ring.load(sp, l, [2 * KD * i + c * KD // 2 for c in range(4)], q)
                    for q in range(ring.SLOTS, Q):
                        load(0, q)
                    with sp.Fori(1, NP) as i:
                        for q in range(Q):
                            load(i, q)

                @block.gpsimd
                def _(pool):
                    def prepare(i, end):
                        pool.wait_ge(spread, i)
                        for z, _, _ in zs_:
                            k, c0 = KZ[z], 2 * KL * z
                            last = nc.gpsimd.tensor_copy(sel[:, c0:c0 + 2 * k].rearrange("e (a b) -> e a b", b=k),
                                                         ident[0:E, ds(2 * i, 2)].unsqueeze(2).to_broadcast([E, 2, k]))
                        last.then_inc(picked, 1)
                        for q in range(AHEAD, end):
                            split(nc.gpsimd, nc.gpsimd.tensor_tensor, i, q)
                    for q in range(AHEAD):
                        split(nc.gpsimd, nc.gpsimd.tensor_tensor, 0, q)
                    pairs(pool, prepare)

                @block.tensor
                def _(pe):
                    def gather(i, banks):
                        pe.wait_ge(one_hot, i + 1)
                        for b in banks:
                            if b >= 2:
                                pe.wait_ge(xg_hi_made, 4 * i + b - 1)
                                pe.wait_ge(xg_lo_made, 4 * i + b - 1)
                            for d in range(2):
                                chunk = ps[:, 4 + b % 2, d * 2 * M:(d + 1) * 2 * M].rearrange("p (e c) -> p e c", e=2)
                                for z, t0, m in zs_:
                                    for t in range(m // P):
                                        mm = nc.tensor.matmul(chunk[:, :, KL * z:KL * z + KZ[z]],
                                                              h2[:, t0 // P + t, (2 * b + d) * P:(2 * b + d + 1) * P], oh[z][:, t],
                                                              start=(t == 0), stop=(t == m // P - 1))
                            if b == 3:
                                for z, t0, m in zs_:
                                    for t in range(m // P):
                                        mm = nc.tensor.matmul(ps[0:2 * KZ[z], 5, GATES + 2 * z:GATES + 2 * z + 2], oh[z][:, t].rearrange("p e s -> p (e s)"),
                                                              aff[:, t0 // P + t, ds(2 * i, 2)], start=(t == 0), stop=(t == m // P - 1))
                            mm.then_inc(gathered, 1)

                    def turn(i, s):
                        pe.wait_ge(consts, 32)
                        pe.wait_ge(hidden, 4 * i + 2 * s + 2)
                        for k in range(KD):
                            mm = nc.tensor.transpose(ps[:, 4 + k // 4, (k % 4) * M:(k % 4 + 1) * M], act_[s][:, k * P:(k + 1) * P], ident[0:M, 0:M])
                        mm.then_inc(turned, 1)

                    def unit(i, q):
                        s, j, kh = ring.ORDER[q]
                        n = Q * i + q
                        if q == 0:
                            pe.wait_ge(xg_hi_made, 4 * i + 4)
                            pe.wait_ge(xg_lo_made, 4 * i + 4)
                            pe.wait_ge(added, i * NS)
                        if s == 1 and j in (0, 2) and kh == 0:
                            pe.wait_ge(hidden, 4 * i + 1 + j // 2)
                        if j == 4 and kh == 0:
                            pe.wait_ge(aT_hi_made, 4 * i + 2 * s + 2)
                            pe.wait_ge(aT_lo_made, 4 * i + 2 * s + 2)
                        if s == 1 and j >= 4 and kh == 0:
                            pe.wait_ge(y_lo_made, 4 * i + j - 3)
                        b = j if j < 4 else j + 2
                        src = (xg_hi, xg_lo) if j < 4 else (aT_hi[s], aT_lo[s])
                        x_hi, x_lo = [[x[:, k, s, :] if j < 4 else x[:, k, :] for k in range(4 * kh, 4 * kh + 4)] for x in src]
                        pe.wait_ge(w_hi_made, n + 1)
                        for k in range(4):
                            nc.tensor.matmul(ps[0:M, b, :], x_hi[k], w_hi[q % AHEAD][:, k, :], start=(kh == 0 and k == 0), stop=False)
                            nc.tensor.matmul(ps[0:M, b, :], x_lo[k], w_hi[q % AHEAD][:, k, :], start=False, stop=False)
                        lo_made(pe, i, q)
                        for k in range(4):
                            mm = nc.tensor.matmul(ps[0:M, b, :], x_hi[k], w_lo[q % AHEAD][:, k, :], start=False, stop=(kh == 1 and k == 3))
                        mm.then_inc(multiplied, 1)

                    def pair(i, end):
                        for q in range(Q):
                            unit(i, q)
                            if q == 13:
                                turn(i, 0)
                            if q == 17:
                                turn(i, 1)
                                pe.wait_ge(picked, i + 1)
                                for z, t0, m in zs_:
                                    w = 2 * KZ[z]
                                    c0 = 2 * KL * z
                                    mm = nc.tensor.matmul(ps[0:w, 2 * z, 0:m], sel[:, c0:c0 + w], posT[:, t0:t0 + m], start=True, stop=True)
                                mm.then_inc(spread, 1)
                            if q in (19, 21) and end > Q:
                                if q == 19:
                                    pe.wait_ge(aT_hi_made, 4 * i + 4)
                                    pe.wait_ge(aT_lo_made, 4 * i + 4)
                                gather(i + 1, (0, 1) if q == 19 else (2, 3))
                        pe.wait_ge(scatter, i + 1)
                        for n, (z, t0, m, d) in enumerate(order):
                            if n in (0, NS // 2):
                                half = 2 * n // NS
                                pe.wait_ge(y_lo_made, 4 * i + 3 + half)
                            if n >= 4:
                                pe.wait_ge(added, i * NS + n - 3)
                            g = G[0:2 * KZ[z], t0:t0 + m]
                            nc.tensor.matmul(ps[:, n % 4, 0:m], y_hi[z][:, d * P:(d + 1) * P], g, start=True, stop=False)
                            nc.tensor.matmul(ps[:, n % 4, 0:m], y_lo[z][:, d * P:(d + 1) * P], g, start=False, stop=True).then_inc(scattered, 1)

                    pe.wait_ge(consts, 32)
                    gather(0, range(4))
                    pairs(pe, pair)

                @block.vector
                def _(dve):
                    def one_hots(i):
                        for z, t0, m in zs_:
                            k = KZ[z]
                            for t in range(m // P):
                                last = nc.vector.tensor_tensor(oh[z][:, t], posm[:, t0 // P + t, ds(2 * i, 2)].unsqueeze(2).to_broadcast([P, 2, k]),
                                                               slots[:, 0:k].unsqueeze(1).to_broadcast([P, 2, k]), ALU.is_equal)
                        last.then_inc(one_hot, 1)

                    def rest(i, banks):
                        for b in banks:
                            dve.wait_ge(xg_hi_made, 4 * i + b + 1)
                            if b == 3:
                                for z, _, _ in zs_:
                                    for e in range(2):
                                        r_ = slice(e * KZ[z], (e + 1) * KZ[z])
                                        c = GATES + 2 * z + e
                                        nc.vector.tensor_copy(gate_next[r_, z:z + 1], ps[r_, 5, c:c + 1])
                            x = xg_hi[:, 2 * b:2 * b + 2].rearrange("p k e m -> p (k e m)")
                            nc.vector.tensor_tensor(xg_lo[:, 2 * b:2 * b + 2].rearrange("p k e m -> p (k e m)"),
                                                    ps[:, 4 + b % 2, 0:4 * M], x.bitcast(F32), ALU.subtract).then_inc(xg_lo_made, 1)

                    def down_lo(i, s, h):
                        dve.wait_ge(gates, i + 1)
                        dve.wait_ge(y_hi_made, 4 * i + 2 * s + h + 1)
                        for z, _, _ in zs_:
                            k, r0 = KZ[z], KL * z
                            r_, c = slice(s * k, (s + 1) * k), slice(h * 512, (h + 1) * 512)
                            last = nc.vector.scalar_tensor_tensor(y_lo[z][r_, c], ps[r0:r0 + k, 6 + h, :], gate[r_, z:z + 1],
                                                                  y_hi[z][r_, c].bitcast(F32), ALU.mult, ALU.subtract)
                        last.then_inc(y_lo_made, 1)

                    def pair(i, end):
                        dve.wait_ge(xg_lo_made, 4 * i + 4)
                        dve.wait_ge(y_lo_made, 4 * i)
                        for z, _, _ in zs_:
                            last = nc.vector.tensor_copy(gate[0:2 * KZ[z], z:z + 1], gate_next[0:2 * KZ[z], z:z + 1])
                        last.then_inc(gates, 1)
                        for e in range(Q):
                            q = e + AHEAD
                            if e in (3, 7, 11, 15):
                                s, h = e // 8, e // 4 % 2
                                dve.wait_ge(silued, 4 * i + 2 * s + h + 1)
                                dve.wait_ge(multiplied, Q * i + e + 1)
                                a_ = act_[s][:, h * 512:(h + 1) * 512]
                                nc.vector.tensor_tensor(a_, a_, ps[0:M, 2 * h + 1, :], ALU.mult).then_inc(hidden, 1)
                            if e in (18, 20, 22):
                                down_lo(i, (e - 18) // 4, (e - 18) // 2 % 2)
                            if e == 23:
                                down_lo(i, 1, 1)
                                for n in range(4):
                                    add(i, n)
                            if q < end:
                                split(nc.vector, nc.vector.tensor_tensor, i, q)
                            if e in (13, 17):
                                s = (e - 13) // 4
                                for b in range(2):
                                    dve.wait_ge(aT_hi_made, 4 * i + 2 * s + b + 1)
                                    c = slice(4 * b, 4 * b + 4)
                                    nc.vector.tensor_tensor(aT_lo[s][:, c].rearrange("p k m -> p (k m)"), ps[:, 4 + b, 0:4 * M],
                                                            aT_hi[s][:, c].rearrange("p k m -> p (k m)").bitcast(F32),
                                                            ALU.subtract).then_inc(aT_lo_made, 1)
                            if e == 9 and end > Q:
                                dve.wait_ge(gathered, 4 * i + 4)
                                one_hots(i + 1)
                            if e == 18:
                                dve.wait_ge(spread, i + 1)
                                for z, t0, m in zs_:
                                    w = 2 * KZ[z]
                                    last = nc.vector.tensor_scalar(G[0:w, t0:t0 + m], ps[0:w, 2 * z, 0:m], slot_of[0:w, z:z + 1], None, ALU.is_equal)
                                last.then_inc(scatter, 1)
                            if e in (19, 21) and end > Q:
                                rest(i + 1, (0, 1) if e == 19 else (2, 3))
                        for n in range(4, NS):
                            add(i, n)

                    def add(i, n):
                        z, t0, m, d = order[n]
                        dve.wait_ge(scattered, i * NS + n + 1)
                        nc.vector.scalar_tensor_tensor(xT[:, d, t0:t0 + m], ps[:, n % 4, 0:m], modT[:, 5 * KD + d, z:z + 1],
                                                       xT[:, d, t0:t0 + m], ALU.mult, ALU.add).then_inc(added, 1)

                    dve.wait_ge(consts, 32)
                    one_hots(0)
                    for q in range(AHEAD):
                        split(nc.vector, nc.vector.tensor_tensor, 0, q)
                    rest(0, range(4))
                    pairs(dve, pair)

                @block.scalar
                def _(act):
                    def round_(i, q):
                        act.wait_ge(ring.loaded[q % ring.SLOTS], 16 * (Q // ring.SLOTS * i + q // ring.SLOTS + 1))
                        if q >= AHEAD:
                            act.wait_ge(multiplied, Q * i + q - AHEAD + 1)
                        nc.scalar.copy(w_hi[q % AHEAD][:], ring.slot[q % ring.SLOTS][:]).then_inc(w_hi_made, 1)

                    def gathered_hi(i, banks):
                        for b in banks:
                            act.wait_ge(gathered, 4 * i + b + 1)
                            nc.scalar.copy(xg_hi[:, 2 * b:2 * b + 2].rearrange("p k e m -> p (k e m)"), ps[:, 4 + b % 2, 0:4 * M]).then_inc(xg_hi_made, 1)

                    def down_hi(i, s, h):
                        act.wait_ge(multiplied, Q * i + 16 + 4 * s + 2 * h + 2)
                        act.wait_ge(gates, i + 1)
                        for z, _, _ in zs_:
                            k, r0 = KZ[z], KL * z
                            r_ = slice(s * k, (s + 1) * k)
                            last = nc.scalar.mul(y_hi[z][r_, h * 512:(h + 1) * 512], ps[r0:r0 + k, 6 + h, :], gate[r_, z:z + 1])
                        last.then_inc(y_hi_made, 1)

                    def pair(i, end):
                        for e in range(Q):
                            q = e + AHEAD
                            if e in (1, 5, 9, 13):
                                s, h = e // 8, e // 4 % 2
                                act.wait_ge(multiplied, Q * i + e + 1)
                                nc.scalar.activation(act_[s][:, h * 512:(h + 1) * 512], ps[0:M, 2 * h, :], ACT.Silu).then_inc(silued, 1)
                            if e in (17, 19, 21, 23):
                                down_hi(i, (e - 17) // 4, (e - 17) // 2 % 2)
                            if q < end:
                                round_(i, q)
                            if e in (13, 17):
                                s = (e - 13) // 4
                                act.wait_ge(turned, 2 * i + s + 1)
                                for b in range(2):
                                    nc.scalar.copy(aT_hi[s][:, 4 * b:4 * b + 4].rearrange("p k m -> p (k m)"), ps[:, 4 + b, 0:4 * M]).then_inc(aT_hi_made, 1)
                            if e in (19, 21) and end > Q:
                                gathered_hi(i + 1, (0, 1) if e == 19 else (2, 3))

                    for q in range(AHEAD):
                        round_(0, q)
                    gathered_hi(0, range(4))
                    pairs(act, pair)

        def store():
            with Scope() as st:
                rows = sb(st, "out_rows", [P, NL, D])
                turned, stored = sem(st, "out_turned"), sem(st, "stored")
                kept = [sem(st, "out_kept_dve"), sem(st, "out_kept_act")]
                block = st.enter_context(nc.Block())

                @block.tensor
                def _(pe):
                    for j in range(2 * NL):
                        if j >= 4:
                            pe.wait_ge(kept[j % 2], (j - 4) // 2 + 1)
                        for q in range(4):
                            mm = nc.tensor.transpose(ps[:, j % 4, q * P:(q + 1) * P], xT[:, 4 * (j % 2) + q, (j // 2) * P:(j // 2 + 1) * P], ident[:])
                        mm.then_inc(turned, 1)

                def keep(eng, copy, parity):
                    for t in range(NL):
                        eng.wait_ge(turned, 2 * t + parity + 1)
                        copy(rows[:, t, parity * 512:(parity + 1) * 512], ps[:, (2 * t + parity) % 4, :]).then_inc(kept[parity], 1)

                @block.vector
                def _(dve):
                    keep(dve, nc.vector.tensor_copy, 0)

                @block.scalar
                def _(act):
                    keep(act, nc.scalar.copy, 1)

                @block.sync
                def _(sp):
                    for t in range(NL):
                        for parity in range(2):
                            sp.wait_ge(kept[parity], t + 1)
                        sp.dma_start(out[0, t * P:(t + 1) * P, :], rows[:, t, :]).then_inc(stored, 16)
                    sp.wait_ge(stored, 16 * NL)

        setup()
        for l in range(DEPTH):
            last = l == DEPTH - 1
            modulation(l)
            with Scope() as mixed:
                mT = None
                with Scope() as mixers:
                    hT = sb(mixers, "hT", [P, KD, T])
                    oT = sb(mixers, "oT", [P, 10, T])
                    norm(0, hT, True)
                    with Scope() as heads:
                        proj = sb(heads, "proj", [P, NT, C_GL])
                        stat = sb(heads, "stat", [P, NT, N_STATS])
                        projection(l, hT, proj, stat, last)
                        with Scope() as biased:
                            bias = sb(biased, "rpb_spread", [P, NA_HEADS, 14 * GRID_W])
                            colmask = sb(biased, "colmask", [P, GRID_W])
                            bl = [sem(biased, f"bias_loaded{i}") for i in range(NA_HEADS // 2)]
                            windowed(l, proj, stat, oT[:, 3:6], lambda sp: load_bias(sp, l, bias, colmask, bl), last)
                            neighbourhood(l, proj, stat, oT[:, 0:3], bias, colmask, bl, last)
                        latent(l, proj, stat, oT[:, 6:10], last)
                    mT = sb(mixers, "mT", [P, KD, T])
                    merge(l, hT, oT, mT, not last)
                    output_projection(l, mT, not last)
            with Scope() as moe:
                nt = NL if last else NT
                ring = Ring(moe)
                h2 = sb(moe, "h2", [P, nt, D])
                posm = sb(moe, "slot_by_token", [P, nt, N_EXPERTS])
                posT = sb(moe, "slot_by_expert", [N_EXPERTS, T], F32R)
                aff = sb(moe, "affinity", [P, nt, N_EXPERTS])
                with Scope() as normed:
                    h2T = sb(normed, "h2T", [P, KD, T])
                    norm(1, h2T, not last, lambda sp: [ring.load(sp, l, (0, KD // 2), q) for q in range(ring.SLOTS)])
                    route(l, h2T, h2, aff, posm, posT, not last)
                experts(l, ring, h2, aff, posm, posT, not last)
        store()


_INS = ["x", "c", "ctx", "c_ctx", "norm1_g", "norm2_g", "w_ada", "b_ada", "w_in", "na_q_g", "na_k_g", "na_rpb",
        "mla_q_norm", "mla_w_uq", "mla_kv_norm", "mla_w_ukv", "mla_q_g", "mla_k_g", "swa_q_g", "swa_k_g", "swa_sink",
        "w_na_o", "w_mla_o", "w_swa_o", "w_o", "router", "w_gate", "w_up", "w_down"]


def kernel(**inputs):
    import numpy as _np
    import concourse.bacc as _bacc
    from concourse import mybir as _mybir
    from concourse.bass_utils import run_bass_kernel_spmd as _run

    nc = _bacc.Bacc("TRN2", target_bir_lowering=False, num_devices=1)
    arrays, args = {}, {}
    for name in _INS:
        a = _np.ascontiguousarray(inputs[name])
        arrays[f"in_{name}"] = a
        args[name] = nc.dram_tensor(f"in_{name}", a.shape, _mybir.dt.from_np(a.dtype), kind="ExternalInput").ap()
    out = nc.dram_tensor("out_x", inputs["x"].shape, F32, kind="ExternalOutput").ap()
    build(nc, out=out, **args)
    return _run(nc, [arrays], core_ids=[0]).results[0]["out_x"]
```
